# Optimizing a Trainium2 kernel written in Bass

```python
import math
import jax, jax.numpy as jnp
from jax import lax
import numpy as np

D_MODEL = 1024
BATCH = 1
SEQ = 256
DEPTH = 2

A_HEADS = 4
A_QK_DIM = 64
A_V_DIM = 2 * A_QK_DIM
B_Q_HEADS = 8
B_KV_HEADS = 2
B_HEAD_DIM = 64
WINDOW = 128
BAND_BLOCK = 128
C_HEADS = 4
C_Q_RANK = 384
C_KV_RANK = 256
C_NOPE_DIM = 128
C_ROPE_DIM = 64
C_V_DIM = 128
ROPE_THETA = 10000.0
Q_BLOCK = 128
MIX_WIDTH = 512
N_BRANCH = 3
D_FF = 2816
EPS = 1e-6
NEG_INF = -1e30

A_QK_COLS = A_HEADS * 2 * A_QK_DIM
A_V_COLS = A_HEADS * A_V_DIM
B_Q_COLS = B_Q_HEADS * B_HEAD_DIM
B_KV_COLS = B_KV_HEADS * B_HEAD_DIM
IN_SPLIT_SIZES = (A_QK_COLS, A_QK_COLS, A_V_COLS, B_Q_COLS, B_KV_COLS, B_KV_COLS, C_Q_RANK, C_KV_RANK, C_ROPE_DIM)
IN_COLS = sum(IN_SPLIT_SIZES)


def rms_norm(x, g):
    x32 = x.astype(jnp.float32)
    y = x32 * lax.rsqrt(jnp.mean(x32 * x32, axis=-1, keepdims=True) + EPS) * g.astype(jnp.float32)
    return y.astype(x.dtype)

def swiglu(h, w13, w2):
    a, g = jnp.split(h @ w13, 2, axis=-1)
    return (jax.nn.silu(a) * g) @ w2

def alibi_slopes(n):
    return 2.0 ** (-8.0 * jnp.arange(1, n + 1, dtype=jnp.float32) / n)

def rope(x, cos, sin):
    x1, x2 = jnp.split(x, 2, axis=-1)
    c = cos[None, :, None, :].astype(x.dtype)
    s = sin[None, :, None, :].astype(x.dtype)
    return jnp.concatenate([x1 * c - x2 * s, x1 * s + x2 * c], axis=-1)

def _split_cols(z):
    outs, off = [], 0
    for size in IN_SPLIT_SIZES:
        outs.append(z[..., off:off + size])
        off += size
    return outs

def _query_blocks(t):
    b, s = t.shape[:2]
    return jnp.moveaxis(t.reshape((b, s // Q_BLOCK, Q_BLOCK) + t.shape[2:]), 1, 0)

def _from_blocks(t):
    t = jnp.moveaxis(t, 0, 1)
    return t.reshape((t.shape[0], t.shape[1] * t.shape[2]) + t.shape[3:])

def diff_attention(q, k, v, lam, lam_init, subln_g, slopes):
    b, s_len = q.shape[:2]
    scale = A_QK_DIM ** -0.5
    key_pos = jnp.arange(s_len, dtype=jnp.float32)

    def block(args):
        qb, start = args
        sc = jnp.einsum('bqhmd,bkhmd->bhmqk', qb, k).astype(jnp.float32) * scale
        qpos = start + jnp.arange(Q_BLOCK, dtype=jnp.float32)
        dist = jnp.abs(qpos[:, None] - key_pos[None, :])
        sc = sc - slopes[None, :, None, None, None] * dist
        p = jax.nn.softmax(sc, axis=-1).astype(v.dtype)
        o = jnp.einsum('bhmqk,bkhe->bqhme', p, v)
        return (o[..., 0, :] - lam * o[..., 1, :]).astype(v.dtype)

    starts = jnp.arange(s_len // Q_BLOCK, dtype=jnp.float32) * Q_BLOCK
    o = _from_blocks(lax.map(block, (_query_blocks(q), starts)))
    o = rms_norm(o, subln_g) * (1.0 - lam_init)
    return o.reshape(b, s_len, A_HEADS * A_V_DIM)

def window_gqa(q, k, v, sinks, slopes):
    b, s_len = q.shape[:2]
    nb = s_len // BAND_BLOCK
    g = B_Q_HEADS // B_KV_HEADS
    qb = q.reshape(b, nb, BAND_BLOCK, B_KV_HEADS, g, B_HEAD_DIM)

    def band(t):
        tp = jnp.pad(t, ((0, 0), (BAND_BLOCK, BAND_BLOCK), (0, 0), (0, 0)))
        tp = tp.reshape(b, nb + 2, BAND_BLOCK, B_KV_HEADS, B_HEAD_DIM)
        return jnp.concatenate([tp[:, :-2], tp[:, 1:-1], tp[:, 2:]], axis=2)

    kb, vb = band(k), band(v)
    sc = jnp.einsum('bnqhgd,bnkhd->bnhgqk', qb, kb).astype(jnp.float32) * (B_HEAD_DIM ** -0.5)
    qi = jnp.arange(BAND_BLOCK)
    kj = jnp.arange(3 * BAND_BLOCK) - BAND_BLOCK
    rel = kj[None, :] - qi[:, None]
    kpos = jnp.arange(nb)[:, None] * BAND_BLOCK + kj[None, :]
    valid = (jnp.abs(rel) <= WINDOW)[None] & ((kpos >= 0) & (kpos < s_len))[:, None, :]
    bias = -slopes.reshape(B_KV_HEADS, g)[:, :, None, None] * jnp.abs(rel).astype(jnp.float32)
    sc = jnp.where(valid[None, :, None, None], sc + bias, NEG_INF)
    sink = jnp.broadcast_to(sinks.astype(jnp.float32).reshape(B_KV_HEADS, g)[None, None, :, :, None, None], sc.shape[:-1] + (1,))
    p = jax.nn.softmax(jnp.concatenate([sc, sink], axis=-1), axis=-1)[..., :-1].astype(v.dtype)
    o = jnp.einsum('bnhgqk,bnkhd->bnqhgd', p, vb)
    return o.reshape(b, s_len, B_Q_HEADS * B_HEAD_DIM)

def mla(c_q, c_kv, k_rope, q_norm_g, w_uq, kv_norm_g, w_ukv, cos, sin):
    b, s_len = c_q.shape[:2]
    q = jnp.einsum('bsr,rhe->bshe', rms_norm(c_q, q_norm_g), w_uq)
    q_nope, q_pe = q[..., :C_NOPE_DIM], rope(q[..., C_NOPE_DIM:], cos, sin)
    kv = jnp.einsum('bsr,rhe->bshe', rms_norm(c_kv, kv_norm_g), w_ukv)
    k_nope, v = kv[..., :C_NOPE_DIM], kv[..., C_NOPE_DIM:]
    k_pe = rope(k_rope[:, :, None, :], cos, sin)[:, :, 0, :]
    scale = (C_NOPE_DIM + C_ROPE_DIM) ** -0.5

    def block(args):
        qn, qp = args
        sc = (jnp.einsum('bqhd,bkhd->bhqk', qn, k_nope) + jnp.einsum('bqhd,bkd->bhqk', qp, k_pe)).astype(jnp.float32) * scale
        p = jax.nn.softmax(sc, axis=-1).astype(v.dtype)
        return jnp.einsum('bhqk,bkhd->bqhd', p, v)

    o = _from_blocks(lax.map(block, (_query_blocks(q_nope), _query_blocks(q_pe))))
    return o.reshape(b, s_len, C_HEADS * C_V_DIM)

def first_inputs(seed: int = 0) -> dict:
    key = jax.random.key(seed)
    ks = jax.random.split(key, 24)

    def nrm(k, shape, scale):
        return jax.random.normal(k, shape, jnp.float32) * scale

    def gain(k, shape):
        return 1.0 + 0.05 * jax.random.normal(k, shape, jnp.float32)

    L, D, F = DEPTH, D_MODEL, D_FF
    return {
        "x": nrm(ks[0], (BATCH, SEQ, D), 1.0),
        "ffn1_norm": gain(ks[1], (L, D)),
        "ffn1_w13": nrm(ks[2], (L, D, 2 * F), D ** -0.5),
        "ffn1_w2": nrm(ks[3], (L, F, D), F ** -0.5),
        "mix_norm": gain(ks[4], (L, D)),
        "w_in": nrm(ks[5], (L, D, IN_COLS), D ** -0.5),
        "w_gate": nrm(ks[6], (L, D, N_BRANCH * D), D ** -0.5),
        "b_gate": nrm(ks[7], (L, N_BRANCH * D), 0.01),
        "a_lambda": nrm(ks[8], (L, 4, A_QK_DIM), 0.1),
        "a_subln": gain(ks[9], (L, A_V_DIM)),
        "b_sinks": nrm(ks[10], (L, B_Q_HEADS), 0.5),
        "c_q_norm": gain(ks[11], (L, C_Q_RANK)),
        "c_w_uq": nrm(ks[12], (L, C_Q_RANK, C_HEADS, C_NOPE_DIM + C_ROPE_DIM), C_Q_RANK ** -0.5),
        "c_kv_norm": gain(ks[13], (L, C_KV_RANK)),
        "c_w_ukv": nrm(ks[14], (L, C_KV_RANK, C_HEADS, C_NOPE_DIM + C_V_DIM), C_KV_RANK ** -0.5),
        "w_branch": nrm(ks[15], (L, N_BRANCH, MIX_WIDTH, D), MIX_WIDTH ** -0.5),
        "w_out": nrm(ks[16], (L, D, D), D ** -0.5),
        "ffn2_norm": gain(ks[17], (L, D)),
        "ffn2_w13": nrm(ks[18], (L, D, 2 * F), D ** -0.5),
        "ffn2_w2": nrm(ks[19], (L, F, D), F ** -0.5),
        "final_norm": gain(ks[20], (D,)),
    }

def first_block(x, ffn1_norm, ffn1_w13, ffn1_w2, mix_norm, w_in, w_gate, b_gate, a_lambda, a_subln, b_sinks, c_q_norm, c_w_uq, c_kv_norm, c_w_ukv, w_branch, w_out, ffn2_norm, ffn2_w13, ffn2_w2, final_norm):
    b, s_len, _ = x.shape
    pos = jnp.arange(s_len, dtype=jnp.float32)
    inv_freq = ROPE_THETA ** (-jnp.arange(0, C_ROPE_DIM, 2, dtype=jnp.float32) / C_ROPE_DIM)
    ang = pos[:, None] * inv_freq[None, :]
    cos, sin = jnp.cos(ang), jnp.sin(ang)
    slopes_a = alibi_slopes(A_HEADS)
    slopes_b = alibi_slopes(B_Q_HEADS)

    for l in range(DEPTH):
        x = x + 0.5 * swiglu(rms_norm(x, ffn1_norm[l]), ffn1_w13[l], ffn1_w2[l])

        h = rms_norm(x, mix_norm[l])
        aq, ak, av, bq, bk, bv, cq, ckv, ckr = _split_cols(h @ w_in[l])

        lam_init = 0.8 - 0.6 * math.exp(-0.3 * l)
        lp = a_lambda[l].astype(jnp.float32)
        lam = jnp.exp(jnp.sum(lp[0] * lp[1])) - jnp.exp(jnp.sum(lp[2] * lp[3])) + lam_init
        oa = diff_attention(aq.reshape(b, s_len, A_HEADS, 2, A_QK_DIM),
                            ak.reshape(b, s_len, A_HEADS, 2, A_QK_DIM),
                            av.reshape(b, s_len, A_HEADS, A_V_DIM),
                            lam, lam_init, a_subln[l], slopes_a)
        ob = window_gqa(bq.reshape(b, s_len, B_Q_HEADS, B_HEAD_DIM),
                        bk.reshape(b, s_len, B_KV_HEADS, B_HEAD_DIM),
                        bv.reshape(b, s_len, B_KV_HEADS, B_HEAD_DIM),
                        b_sinks[l], slopes_b)
        oc = mla(cq, ckv, ckr, c_q_norm[l], c_w_uq[l], c_kv_norm[l], c_w_ukv[l], cos, sin)

        branches = jnp.stack([oa, ob, oc], axis=2)
        proj = jnp.einsum('bsnw,nwd->bsnd', branches, w_branch[l])
        gates = jax.nn.sigmoid(h @ w_gate[l] + b_gate[l]).reshape(b, s_len, N_BRANCH, D_MODEL)
        x = x + jnp.sum(gates * proj, axis=2) @ w_out[l]

        x = x + 0.5 * swiglu(rms_norm(x, ffn2_norm[l]), ffn2_w13[l], ffn2_w2[l])

    return rms_norm(x, final_norm)


DEPTH_2 = 4

HEAD_DIM = 64
N_HEADS = D_MODEL // HEAD_DIM
NORM_EPS = 1e-6
N_MIXERS = 3

REL_BUCKETS = 32
REL_MAX_DIST = 1024

QBLK = 128

A_KV_HEADS = 2
A_WINDOW = 128

B_KV_GROUPS = 4
CMP_LEN = 32
CMP_STRIDE = 16
CMP_HIDDEN = 256
SLC_BLK = 64
SLC_TOPK = 16
B_WINDOW = 512
B_QCHUNK = 128

MOBA_BLK = 256
MOBA_TOPK = 3
MOBA_QCHUNK = 64

NEG = -1e30
TINY = 1e-30

A_IN = N_HEADS * HEAD_DIM + 2 * A_KV_HEADS * HEAD_DIM
B_IN = N_HEADS * HEAD_DIM + 6 * B_KV_GROUPS * HEAD_DIM + 3 * N_HEADS
C_IN = 3 * N_HEADS * HEAD_DIM

N_A_LAYERS = (DEPTH_2 + 2) // 3
N_B_LAYERS = (DEPTH_2 + 1) // 3
N_C_LAYERS = DEPTH_2 // 3


def rms_norm_2(x, g):
    xf = x.astype(jnp.float32)
    y = xf * lax.rsqrt(jnp.mean(xf * xf, axis=-1, keepdims=True) + NORM_EPS)
    return (y * g.astype(jnp.float32)).astype(x.dtype)

def swiglu_2(h, w_in, w_out):
    gate, up = jnp.split(h @ w_in, 2, axis=-1)
    return (jax.nn.silu(gate) * up) @ w_out

def rel_bucket(dist):
    dist = jnp.maximum(dist, 0)
    exact = REL_BUCKETS // 2
    d = jnp.maximum(dist, 1).astype(jnp.float32)
    log_b = exact + (jnp.log(d / exact) / math.log(REL_MAX_DIST / exact)
                     * (REL_BUCKETS - exact)).astype(jnp.int32)
    return jnp.where(dist < exact, dist, jnp.minimum(log_b, REL_BUCKETS - 1))

def masked_softmax(s, ok, sink=None):
    s = jnp.where(ok, s, NEG)
    m = jnp.max(s, axis=-1, keepdims=True)
    if sink is not None:
        m = jnp.maximum(m, sink)
    e = jnp.where(ok, jnp.exp(s - m), 0.0)
    denom = jnp.sum(e, axis=-1, keepdims=True)
    if sink is not None:
        denom = denom + jnp.exp(sink - m)
    return e / jnp.maximum(denom, TINY)

def banded_attention(q, k, v, rel_table, window, sinks=None):
    B, S, H, dh = q.shape
    G = k.shape[2]
    R = H // G
    n_prev = -(-(window - 1) // QBLK)
    pad = n_prev * QBLK
    slab = pad + QBLK
    kp = jnp.pad(k, ((0, 0), (pad, 0), (0, 0), (0, 0)))
    vp = jnp.pad(v, ((0, 0), (pad, 0), (0, 0), (0, 0)))
    n_blk = S // QBLK
    qb = q.reshape(B, n_blk, QBLK, G, R, dh).transpose(1, 0, 2, 3, 4, 5)
    qi = jnp.arange(QBLK)[:, None]
    kj = jnp.arange(slab)[None, :]
    dist = pad + qi - kj
    in_band = (dist >= 0) & (dist < window)
    bias = rel_table.astype(jnp.float32)[rel_bucket(dist)]
    bias = bias.reshape(QBLK, slab, G, R).transpose(2, 3, 0, 1)
    sink = None if sinks is None else sinks.astype(jnp.float32).reshape(G, R, 1, 1)
    scale = dh ** -0.5

    def block(args):
        n, q_n = args
        start = n * QBLK
        k_n = lax.dynamic_slice_in_dim(kp, start, slab, axis=1)
        v_n = lax.dynamic_slice_in_dim(vp, start, slab, axis=1)
        s = jnp.einsum("bqgrd,bkgd->bgrqk", q_n, k_n).astype(jnp.float32) * scale + bias
        ok = in_band & (start - pad + kj >= 0)
        p = masked_softmax(s, ok, sink)
        o = jnp.einsum("bgrqk,bkgd->bqgrd", p.astype(v.dtype), v_n)
        return o.reshape(B, QBLK, H, dh)

    out = lax.map(block, (jnp.arange(n_blk), qb))
    return out.transpose(1, 0, 2, 3, 4).reshape(B, S, H, dh)

def sliding_sink_attention(h, w_in, w_out, sinks, rel_table):
    B, S, _ = h.shape
    qw, kw = N_HEADS * HEAD_DIM, A_KV_HEADS * HEAD_DIM
    q, k, v = jnp.split(h @ w_in, [qw, qw + kw], axis=-1)
    q = q.reshape(B, S, N_HEADS, HEAD_DIM)
    k = k.reshape(B, S, A_KV_HEADS, HEAD_DIM)
    v = v.reshape(B, S, A_KV_HEADS, HEAD_DIM)
    o = banded_attention(q, k, v, rel_table, A_WINDOW, sinks)
    return o.reshape(B, S, -1) @ w_out

def compress_kv(kv, pos, w1, w2):
    B, S, G, dh = kv.shape
    n_cmp = (S - CMP_LEN) // CMP_STRIDE + 1
    idx = jnp.arange(n_cmp)[:, None] * CMP_STRIDE + jnp.arange(CMP_LEN)[None, :]
    blocks = kv[:, idx] + pos[:, None, :]
    flat = blocks.transpose(0, 1, 3, 2, 4).reshape(B, n_cmp, G, CMP_LEN * dh)
    return jax.nn.gelu(flat @ w1) @ w2

def selected_block_attention(q, k, v, sel_idx, rel_table):
    B, S, G, R, dh = q.shape
    n_sel = sel_idx.shape[-1]
    n_slc = S // SLC_BLK
    kb = k.reshape(B, n_slc, SLC_BLK, G, dh).transpose(0, 3, 1, 2, 4)
    vb = v.reshape(B, n_slc, SLC_BLK, G, dh).transpose(0, 3, 1, 2, 4)
    table_g = rel_table.astype(jnp.float32).reshape(REL_BUCKETS, G, R).transpose(1, 0, 2)
    g_ix = jnp.arange(G)[:, None, None]
    n_q = S // B_QCHUNK
    n_keys = n_sel * SLC_BLK
    scale = dh ** -0.5

    def chunk(i):
        b, c = i // n_q, i % n_q
        start = c * B_QCHUNK
        q_c = lax.dynamic_slice_in_dim(q[b], start, B_QCHUNK, axis=0)
        idx = lax.dynamic_slice_in_dim(sel_idx[b], start, B_QCHUNK, axis=1)
        k_sel = kb[b][g_ix, idx].reshape(G, B_QCHUNK, n_keys, dh)
        v_sel = vb[b][g_ix, idx].reshape(G, B_QCHUNK, n_keys, dh)
        pos = (idx[..., None] * SLC_BLK + jnp.arange(SLC_BLK)).reshape(G, B_QCHUNK, n_keys)
        t = start + jnp.arange(B_QCHUNK)
        dist = t[None, :, None] - pos
        bias = table_g[g_ix, rel_bucket(dist)].transpose(0, 3, 1, 2)
        s = jnp.einsum("qgrd,gqkd->grqk", q_c, k_sel).astype(jnp.float32) * scale + bias
        p = masked_softmax(s, (dist >= 0)[:, None])
        o = jnp.einsum("grqk,gqkd->qgrd", p.astype(v.dtype), v_sel)
        return o.reshape(B_QCHUNK, G * R, dh)

    out = lax.map(chunk, jnp.arange(B * n_q))
    return out.reshape(B, S, G * R, dh)

def nsa_attention(h, w_in, w_out, cmp_pos, cmp_w1, cmp_w2, rel_table):
    B, S, _ = h.shape
    G, R, dh = B_KV_GROUPS, N_HEADS // B_KV_GROUPS, HEAD_DIM
    kvw = G * dh
    splits = np.cumsum([N_HEADS * dh] + [kvw] * 6).tolist()
    q, kc, vc, ks, vs, kw, vw, gate = jnp.split(h @ w_in, splits, axis=-1)
    q = q.reshape(B, S, G, R, dh)
    to_kv = lambda a: a.reshape(B, S, G, dh)
    scale = dh ** -0.5
    t = jnp.arange(S)

    kc_b = compress_kv(to_kv(kc), cmp_pos[0], cmp_w1[0], cmp_w2[0])
    vc_b = compress_kv(to_kv(vc), cmp_pos[1], cmp_w1[1], cmp_w2[1])
    n_cmp = kc_b.shape[1]
    cmp_end = jnp.arange(n_cmp) * CMP_STRIDE + CMP_LEN - 1
    s_cmp = jnp.einsum("bsgrd,bngd->bgrsn", q, kc_b).astype(jnp.float32) * scale
    p_cmp = masked_softmax(s_cmp, cmp_end[None, :] <= t[:, None])
    o_cmp = jnp.einsum("bgrsn,bngd->bsgrd", p_cmp.astype(vc_b.dtype), vc_b)

    n_slc = S // SLC_BLK
    n_sel = min(SLC_TOPK, n_slc)
    c_start = np.arange(n_cmp)[:, None] * CMP_STRIDE
    s_start = np.arange(n_slc)[None, :] * SLC_BLK
    overlap = ((c_start < s_start + SLC_BLK) & (c_start + CMP_LEN > s_start)).astype(np.float32)
    imp = jnp.einsum("bgrsn,nj->bgsj", p_cmp, jnp.asarray(overlap))
    cur = (t // SLC_BLK)[:, None]
    j = jnp.arange(n_slc)[None, :]
    forced = (j == 0) | (j == cur) | (j == cur - 1)
    imp = jnp.where(j > cur, NEG, jnp.where(forced, -NEG, imp))
    _, sel_idx = lax.top_k(imp, n_sel)
    o_slc = selected_block_attention(q, to_kv(ks), to_kv(vs), sel_idx, rel_table)

    o_win = banded_attention(q.reshape(B, S, N_HEADS, dh), to_kv(kw), to_kv(vw),
                             rel_table, B_WINDOW)

    g = jax.nn.sigmoid(gate.astype(jnp.float32)).reshape(B, S, N_HEADS, 3).astype(o_win.dtype)
    o = (g[..., 0:1] * o_cmp.reshape(B, S, N_HEADS, dh)
         + g[..., 1:2] * o_slc + g[..., 2:3] * o_win)
    return o.reshape(B, S, -1) @ w_out

def moba_attention(h, w_in, w_out, rel_table):
    B, S, _ = h.shape
    H, dh = N_HEADS, HEAD_DIM
    q, k, v = jnp.split(h @ w_in, 3, axis=-1)
    q = q.reshape(B, S, H, dh)
    k = k.reshape(B, S, H, dh)
    v = v.reshape(B, S, H, dh)
    n_blk = -(-S // MOBA_BLK)
    s_pad = n_blk * MOBA_BLK
    kb = jnp.pad(k, ((0, 0), (0, s_pad - S), (0, 0), (0, 0))).reshape(B, n_blk, MOBA_BLK, H, dh)
    vb = jnp.pad(v, ((0, 0), (0, s_pad - S), (0, 0), (0, 0))).reshape(B, n_blk, MOBA_BLK, H, dh)
    n_top = min(MOBA_TOPK, n_blk - 1)
    table = rel_table.astype(jnp.float32)
    table_h = table.T
    scale = dh ** -0.5
    t = jnp.arange(S)
    if n_top > 0:
        k_mean = jnp.mean(kb.astype(jnp.float32), axis=2).astype(q.dtype)
        gate = jnp.einsum("bshd,bnhd->bhsn", q, k_mean).astype(jnp.float32)
        past = jnp.arange(n_blk)[None, :] < (t // MOBA_BLK)[:, None]
        _, sel = lax.top_k(jnp.where(past, gate, NEG), n_top)
        kbh = kb.transpose(0, 3, 1, 2, 4)
        vbh = vb.transpose(0, 3, 1, 2, 4)
    h_ix = jnp.arange(H)[:, None, None]
    n_q = S // MOBA_QCHUNK

    def chunk(i):
        b, c = i // n_q, i % n_q
        start = c * MOBA_QCHUNK
        q_c = lax.dynamic_slice_in_dim(q[b], start, MOBA_QCHUNK, axis=0)
        tq = start + jnp.arange(MOBA_QCHUNK)
        own = start // MOBA_BLK
        k_own = lax.dynamic_index_in_dim(kb[b], own, axis=0, keepdims=False)
        v_own = lax.dynamic_index_in_dim(vb[b], own, axis=0, keepdims=False)
        d_own = tq[:, None] - (own * MOBA_BLK + jnp.arange(MOBA_BLK))[None, :]
        s_own = (jnp.einsum("qhd,khd->hqk", q_c, k_own).astype(jnp.float32) * scale
                 + table[rel_bucket(d_own)].transpose(2, 0, 1))
        ok_own = jnp.broadcast_to(d_own >= 0, s_own.shape)
        if n_top == 0:
            p = masked_softmax(s_own, ok_own)
            return jnp.einsum("hqk,khd->qhd", p.astype(v.dtype), v_own)
        idx = lax.dynamic_slice_in_dim(sel[b], start, MOBA_QCHUNK, axis=1)
        n_keys = n_top * MOBA_BLK
        k_sel = kbh[b][h_ix, idx].reshape(H, MOBA_QCHUNK, n_keys, dh)
        v_sel = vbh[b][h_ix, idx].reshape(H, MOBA_QCHUNK, n_keys, dh)
        pos = (idx[..., None] * MOBA_BLK + jnp.arange(MOBA_BLK)).reshape(H, MOBA_QCHUNK, n_keys)
        d_sel = tq[None, :, None] - pos
        s_sel = (jnp.einsum("qhd,hqkd->hqk", q_c, k_sel).astype(jnp.float32) * scale
                 + table_h[h_ix, rel_bucket(d_sel)])
        ok_sel = jnp.broadcast_to((idx < own)[..., None],
                                  (H, MOBA_QCHUNK, n_top, MOBA_BLK)).reshape(H, MOBA_QCHUNK, n_keys)
        p = masked_softmax(jnp.concatenate([s_own, s_sel], axis=-1),
                           jnp.concatenate([ok_own, ok_sel], axis=-1)).astype(v.dtype)
        return (jnp.einsum("hqk,khd->qhd", p[..., :MOBA_BLK], v_own)
                + jnp.einsum("hqk,hqkd->qhd", p[..., MOBA_BLK:], v_sel))

    out = lax.map(chunk, jnp.arange(B * n_q))
    return out.reshape(B, S, H * dh) @ w_out

def second_inputs(seed: int = 0) -> dict:
    key = jax.random.key(seed)
    ks = jax.random.split(key, 16)
    f32 = jnp.float32
    hd = N_HEADS * HEAD_DIM

    def nrm(k, shape, fan_in):
        return jax.random.normal(k, shape, f32) * fan_in ** -0.5

    return {
        "x": jax.random.normal(ks[0], (BATCH, SEQ, D_MODEL), f32),
        "rel_bias": 0.5 * jax.random.normal(ks[1], (REL_BUCKETS, N_HEADS), f32),
        "norm_g": 1.0 + 0.05 * jax.random.normal(ks[2], (DEPTH_2, 6, D_MODEL), f32),
        "ffn_w_in": nrm(ks[3], (DEPTH_2, 2, D_MODEL, 2 * D_FF), D_MODEL),
        "ffn_w_out": nrm(ks[4], (DEPTH_2, 2, D_FF, D_MODEL), D_FF),
        "a_w_in": nrm(ks[5], (N_A_LAYERS, D_MODEL, A_IN), D_MODEL),
        "a_w_out": nrm(ks[6], (N_A_LAYERS, hd, D_MODEL), hd),
        "a_sinks": jax.random.normal(ks[7], (N_A_LAYERS, N_HEADS), f32),
        "b_w_in": nrm(ks[8], (N_B_LAYERS, D_MODEL, B_IN), D_MODEL),
        "b_w_out": nrm(ks[9], (N_B_LAYERS, hd, D_MODEL), hd),
        "b_cmp_pos": 0.5 * jax.random.normal(ks[10], (N_B_LAYERS, 2, CMP_LEN, HEAD_DIM), f32),
        "b_cmp_w1": nrm(ks[11], (N_B_LAYERS, 2, CMP_LEN * HEAD_DIM, CMP_HIDDEN), CMP_LEN * HEAD_DIM),
        "b_cmp_w2": nrm(ks[12], (N_B_LAYERS, 2, CMP_HIDDEN, HEAD_DIM), CMP_HIDDEN),
        "c_w_in": nrm(ks[13], (N_C_LAYERS, D_MODEL, C_IN), D_MODEL),
        "c_w_out": nrm(ks[14], (N_C_LAYERS, hd, D_MODEL), hd),
    }

def second_block(x, rel_bias, norm_g, ffn_w_in, ffn_w_out, a_w_in, a_w_out, a_sinks,
              b_w_in, b_w_out, b_cmp_pos, b_cmp_w1, b_cmp_w2, c_w_in, c_w_out):
    for i in range(DEPTH_2):
        g = norm_g[i]
        x = x + 0.5 * rms_norm_2(swiglu_2(rms_norm_2(x, g[0]), ffn_w_in[i, 0], ffn_w_out[i, 0]), g[1])
        hm = rms_norm_2(x, g[2])
        kind, j = i % N_MIXERS, i // N_MIXERS
        if kind == 0:
            m = sliding_sink_attention(hm, a_w_in[j], a_w_out[j], a_sinks[j], rel_bias)
        elif kind == 1:
            m = nsa_attention(hm, b_w_in[j], b_w_out[j], b_cmp_pos[j], b_cmp_w1[j],
                              b_cmp_w2[j], rel_bias)
        else:
            m = moba_attention(hm, c_w_in[j], c_w_out[j], rel_bias)
        x = x + rms_norm_2(m, g[3])
        x = x + 0.5 * rms_norm_2(swiglu_2(rms_norm_2(x, g[4]), ffn_w_in[i, 1], ffn_w_out[i, 1]), g[5])
    return x


def setup_inputs(seed=0):
    out = dict(first_inputs(seed))
    for name, value in second_inputs(seed + 1).items():
        if name != "x":
            out[name + "_2"] = value
    return out


def reference(
    x, ffn1_norm, ffn1_w13, ffn1_w2, mix_norm, w_in, w_gate, b_gate, a_lambda, a_subln, b_sinks,
    c_q_norm, c_w_uq, c_kv_norm, c_w_ukv, w_branch, w_out, ffn2_norm, ffn2_w13, ffn2_w2,
    final_norm, rel_bias_2, norm_g_2, ffn_w_in_2, ffn_w_out_2, a_w_in_2, a_w_out_2, a_sinks_2,
    b_w_in_2, b_w_out_2, b_cmp_pos_2, b_cmp_w1_2, b_cmp_w2_2, c_w_in_2, c_w_out_2,
):
    x = first_block(
        x, ffn1_norm, ffn1_w13, ffn1_w2, mix_norm, w_in, w_gate, b_gate, a_lambda, a_subln,
        b_sinks, c_q_norm, c_w_uq, c_kv_norm, c_w_ukv, w_branch, w_out, ffn2_norm, ffn2_w13,
        ffn2_w2, final_norm,
    )
    return second_block(
        x, rel_bias_2, norm_g_2, ffn_w_in_2, ffn_w_out_2, a_w_in_2, a_w_out_2, a_sinks_2,
        b_w_in_2, b_w_out_2, b_cmp_pos_2, b_cmp_w1_2, b_cmp_w2_2, c_w_in_2, c_w_out_2,
    )


_drawn_inputs = setup_inputs


def setup_inputs(seed=0):
    import zlib

    import numpy as np

    out = dict(_drawn_inputs(seed))
    spreads = {}
    factors = {'b_gate': 8.0, 'b_sinks': 3.134, 'c_q_norm': 8.0, 'c_kv_norm': 4.564}
    for name, (base, spread) in spreads.items():
        noise = np.random.default_rng([zlib.crc32(name.encode()), seed]).standard_normal(out[name].shape)
        drawn = base * np.exp(spread * noise) if base else spread * noise
        out[name] = __import__('jax').numpy.asarray(drawn.astype(out[name].dtype))
    for name, factor in factors.items():
        out[name] = (out[name] * factor).astype(out[name].dtype)
    return out
```

```python
from contextlib import ExitStack
from dataclasses import dataclass
from typing import Any

import numpy as np
import concourse.bass as bass
from concourse import mybir

F32 = mybir.dt.float32
F32R = mybir.dt.float32r
ALU = mybir.AluOpType
ACT = mybir.ActivationFunctionType
AX = mybir.AxisListType

P = 128
D = 1024
T = 256
TT = T // P
KD = D // P
DFF = 2816
PAIRS = DFF // (2 * P)
STEP = 2048
RING = 3
EPS = 1e-6
NEG = -1e30
TINY = 1e-30
DEPTH1, DEPTH2 = 2, 4
A_HEADS, B_HEADS, C_HEADS = 4, 8, 4
C_QR, C_KVR, C_NOPE, C_ROPE = 384, 256, 128, 64
C_COLS = C_QR + C_KVR + C_ROPE
HEADS = 16
DH = 64
KVG = 4
BUCKETS, BUCKET_MAX = 32, 1024
CMP_LEN, CMP_STRIDE, CMP_HID = 32, 16, 256
NCMP = (T - CMP_LEN) // CMP_STRIDE + 1
NBLK = KVG * NCMP
LP = CMP_LEN // 2
SINK = T
NBIAS1 = A_HEADS + B_HEADS + 1
VEC = 512
LAM0 = [0.8 - 0.6 * float(np.exp(-0.3 * l)) for l in range(DEPTH1)]

GAIN_ROWS = [("ffn1", l) for l in range(2)] + [("mix", l) for l in range(2)] + [("ffn2", l) for l in range(2)] \
    + [("n2", i, k) for i in range(4) for k in (0, 2, 4)]
PRM = {}
_at = 0
for _name, _n in (("gain", len(GAIN_ROWS) * KD), ("subln", DEPTH1), ("cqn", DEPTH1 * 3), ("ckvn", DEPTH1 * 2),
                  ("bgate", DEPTH1 * 24), ("sink1", DEPTH1 * B_HEADS), ("sink2", 2 * HEADS),
                  ("lam", DEPTH1 * 4 * DH), ("pos", 2 * LP), ("cw2", 2 * 2 * DH), ("table", HEADS)):
    PRM[_name] = _at
    _at += _n
PRM_COLS = _at
CST = {}
_at = 0
for _name, _n in (("ident", P), ("cos", TT * 32), ("sin", TT * 32), ("cmpneg", TT * NCMP), ("cmpok", TT * NCMP),
                  ("onehot", 2 * VEC)):
    CST[_name] = _at
    _at += _n
CST_COLS = _at
POST_ROWS = [(i, k) for i in range(4) for k in (1, 3, 5)]


@dataclass
class Phase:
    kind: str
    engines: tuple
    before: dict
    base: dict
    step: int
    stack: int
    gain: int = 0
    post: Any = None
    factor: float = 1.0
    dest: str = ""
    head0: int = 0
    n: int = 0
    col0: int = 0
    cols: int = 0
    kk: int = 0
    chunks: int = 0
    job: str = ""
    bias: str = ""
    bias0: int = 0
    layer: int = 0
    sink: Any = None
    k0: int = 0
    subln: Any = None
    src: str = ""


@dataclass
class Job:
    q: Any
    k: Any
    rows: int
    dv: int
    rotary: bool
    scale: float
    sink: Any
    bias_row: Any
    key: Any
    vcol: Any
    ocol: Any


def plan():
    phases, count, steps = [], {}, 0

    def add(kind, engines, steps_used=0, up=None, **args):
        nonlocal steps
        before = {e: count.get(e + "_phase", 0) for e in ("pe", "act", "dve", "pool")}
        phases.append(Phase(kind=kind, engines=engines, before=before, base=dict(count), step=steps,
                                      stack=2 if any(p.kind == "final" for p in phases) else 1, **args))
        for name, n in (up or {}).items():
            count[name] = count.get(name, 0) + n
        for e in engines:
            count[e + "_phase"] = count.get(e + "_phase", 0) + 1
        steps += steps_used

    def norm(gain):
        add("norm", ("pe", "act", "dve"), gain=GAIN_ROWS.index(gain),
            up=dict(sumsq=2, std_ready=1, rstd_ready=1, xn_ready=2, tposed=KD, hi_made=KD))

    def ffn():
        n = PAIRS
        add("ffn", ("pe", "act", "dve"), 3 * n,
            up=dict(low_a=n, low_g=n, a_summed=n, g_summed=n, silu_ready=n,
                    h_ready=n, hh_ready=n, ht_ready=n))

    def residual(post=None, factor=1.0):
        if post is None:
            add("residual", ("dve",), post=None, factor=factor)
        else:
            add("residual", ("act", "dve", "pool"), post=post, factor=factor,
                up=dict(sumsq=2, std_ready=1, rstd_ready=1, y_ready=2, post_loaded=16))

    def proj_f(dest, head0, n, rhs="x", width=64):
        add("proj_f", ("pe", "act", "dve"), n, dest=dest, head0=head0, n=n,
            up=dict(low_copied=n, group_free=n))

    def proj_t(dest, col0, cols, kk, n, chunks):
        add("proj_t", ("pe", "act", "dve"), n * chunks, dest=dest, col0=col0, cols=cols, kk=kk, n=n,
            chunks=chunks, up=dict(group_free=chunks))

    def attend(kind, n, bias, bias0, **a):
        extra = {"diff": dict(rs_ready=n // 2), "nsa_slc": dict(rs_ready=n), "nsa_win": dict(rs_ready=n)}.get(kind, {})
        add("attend", ("pe", "act", "dve", "pool"), job=kind, n=n, bias=bias, bias0=bias0, **a,
            up=dict(q_staged=n, scores_ready=n, biased=n, max_ready=n, probs_ready=n, transposed=n, pt_ready=n,
                    recip_ready=n, pv_ready=n, o_done=n, bias_even=n // 2 * 16, bias_odd=n // 2 * 16, **extra))

    def turn(k0, n, subln=None):
        add("turn", ("pe", "act", "dve"), k0=k0, n=n, subln=subln,
            up=dict(tposed=n, hi_made=n, head_norm=0 if subln is None else 6))

    def wout(src):
        add("wout", ("pe", "act", "dve"), 4, src=src)

    add("setup", ("pe", "act", "dve", "pool"), up=dict(vec_made=2, vec_copied=2, lam_sum=1, lam_exp=1, lam_sub=2,
                                                       lam_mul=1))
    for l in range(DEPTH1):
        norm(("ffn1", l))
        ffn()
        residual(factor=0.5)
        norm(("mix", l))
        proj_f("q", 0, 2)
        proj_f("k", 0, 2)
        proj_t("v", 0, 512, 4, 2, 1)
        attend("diff", 8, "fixed", 0, layer=l)
        turn(0, 4, subln=l)
        proj_f("q", 0, 2)
        proj_f("kv", 0, 1)
        attend("gqa1", 8, "fixed", A_HEADS, sink=PRM["sink1"] + l * B_HEADS)
        turn(4, 4)
        proj_t("c", 0, C_COLS // 2, 4, 2, 2)
        add("mla_latent", ("pe", "act", "dve"), layer=l,
            up=dict(sumsq=4, std_ready=2, rstd_ready=1, xn_ready=6, tposed=6, hi_made=5))
        add("mla_up", ("pe", "act", "dve"), 3, layer=l,
            up=dict(group_ready=2, low_copied=2, qv_stored=3, k_stored=2, rope_done=4, tposed=8))
        attend("mla", 4, "fixed", NBIAS1 - 1)
        turn(8, 4)
        add("gates", ("pe", "act", "dve"), 24, layer=l,
            up=dict(low_copied=24, group_free=24, gate_ready=12, y_ready=12, y_part=8, hh_ready=4,
                    prod_ready=8))
        wout("y")
        residual(factor=1.0)
        norm(("ffn2", l))
        ffn()
        residual(factor=0.5)
    add("final", ("act", "dve", "pool"), post=len(POST_ROWS),
        up=dict(sumsq=2, std_ready=1, rstd_ready=1, y_ready=2, post_loaded=16))
    for i in range(DEPTH2):
        norm(("n2", i, 0))
        ffn()
        residual(post=3 * i, factor=0.5)
        norm(("n2", i, 2))
        if i % 3 == 0:
            proj_f("q", 0, 4)
            proj_f("kv", 0, 1)
            attend("gqa2", HEADS, "window", 0, sink=PRM["sink2"] + (i // 3) * HEADS)
        elif i % 3 == 1:
            proj_f("q", 0, 4)
            proj_f("cmp", 0, 2)
            add("compress", ("pe", "act", "dve"), 4,
                up=dict(blk_added=2, blk_hi=2, blk_made=2, low_copied=2, group_free=2, gelu_done=2,
                        cmp_ready=1))
            proj_f("k", 0, 1)
            proj_t("v", 0, 256, 8, 1, 1)
            proj_f("k", 4, 1)
            proj_t("v", 256, 256, 8, 1, 1)
            proj_t("gate", 0, 48, 8, 1, 1)
            add("cmp_attend", ("pe", "act", "dve"),
                up=dict(scores_ready=1, cmp_step=10, max_ready=1, probs_ready=1, transposed=1, pt_ready=1,
                        pv_ready=1))
            attend("nsa_slc", HEADS, "causal", 0)
            attend("nsa_win", HEADS, "causal", 0)
        else:
            proj_f("q", 0, 4)
            proj_f("k", 0, 4)
            proj_t("v", 0, 512, 4, 2, 2)
            attend("moba", HEADS, "causal", 0)
        turn(0, 8)
        wout("o")
        residual(post=3 * i + 1, factor=1.0)
        norm(("n2", i, 4))
        ffn()
        residual(post=3 * i + 2, factor=0.5)
    add("store", ("act",))
    return phases, count, steps


def transformer_stacks(nc, stream, prm_in, cst_in, fixed_bias, post_in, x_in, out, limit=None):
    phases, totals, n_steps = plan()
    if limit is not None:
        limit_steps = phases[limit].step
        phases = phases[:limit] + [p for p in phases if p.kind == "store"]
        phases[-1].before = phases[-2].before | {
            e: phases[-2].before[e] + (e in phases[-2].engines) for e in phases[-2].before}
        n_steps = limit_steps
    n_steps += 2
    n_steps += -n_steps % RING
    vec = nc.dram_tensor("rel_vectors", [2 * HEADS, VEC], F32, kind="Internal").ap()
    rel_bias = nc.dram_tensor("rel_bias", [2 * HEADS, P, TT, T], F32, kind="Internal").ap()

    with ExitStack() as ctx:
        def sb(name, shape, dt=F32):
            return ctx.enter_context(nc.sbuf_tensor(name, shape, dt))

        def overlay(*regions):
            sizes = [sum(int(np.prod(shape[1:])) for _, shape, _ in region) for region in regions]
            assert sizes[-1] == max(sizes)
            made = []
            for n, region in enumerate(regions):
                if n == len(regions) - 1:
                    made += [sb(*t) for t in region]
                    continue
                with ExitStack() as part:
                    made += [part.enter_context(nc.sbuf_tensor(*t)) for t in region]
            return made

        raw = sb("raw", [P, RING, STEP])
        whi = sb("whi", [P, RING, STEP], F32R)
        wlo = sb("wlo", [P, RING, STEP], F32R)
        x = sb("x", [P, TT, D])
        xhl = sb("xhl", [P, KD, 2 * T], F32R)
        v = sb("v", [P, TT, D])
        o = sb("o", [P, TT, D])
        prm = sb("prm", [P, PRM_COLS])
        cst = sb("cst", [P, CST_COLS])
        post = sb("post", [P, D])
        small = sb("small", [P, 128])
        (yhl, q1, k1, br1, qpe, kpe, br2, q2, k2, blk) = overlay(
            [("yhl", [P, KD, 2 * T], F32R)],
            [("q1", [P, 8, T], F32), ("k1", [P, 8, T], F32), ("br1", [P, 12, 2 * T], F32R),
             ("qpe", [P, C_HEADS, T], F32), ("kpe", [P, T], F32)],
            [("br2", [P, KD, 2 * T], F32R)],
            [("q2", [P, HEADS, T], F32), ("k2", [P, HEADS, T], F32), ("blk", [P, 2, LP, 2 * NBLK], F32R)])
        (pcmp, vblk, kcb, gates, chl) = overlay(
            [("pcmp", [P, TT, HEADS, 32], F32), ("vblk", [P, KVG, T], F32), ("kcb", [P, NBLK], F32),
             ("gates", [P, TT, 48], F32)],
            [("chl", [P, 5, 2 * T], F32R)])
        (ta, a_sum, silu, tg, g_sum, h, ht, tl, cblk, chid, cpre, scmp, bias, s, pr, pt, qs, qps) = overlay(
            [("ta", [P, 2, T], F32), ("a_sum", [P, 2, T], F32), ("silu", [P, 2, T], F32), ("tg", [P, 2, T], F32),
             ("g_sum", [P, 2, T], F32), ("h", [P, 2, T], F32), ("ht", [P, 2, 2, T], F32R)],
            [("tl", [P, 2, 2, T], F32), ("cblk", [P, LP, KVG, NCMP], F32), ("chid", [P, 2, 2, NBLK], F32),
             ("cpre", [P, 2, 2, NBLK], F32), ("scmp", [P, TT, HEADS, NCMP], F32)],
            [("bias", [P, 2, TT, T], F32), ("s", [P, 2, TT, T + 4], F32), ("pr", [P, 2, TT, T + 4], F32),
             ("pt", [P, 2, TT, T], F32), ("qs", [P, 2, T], F32), ("qps", [P, 2, T], F32)])
        latent = o[:, :, 0:C_COLS]
        qtok = o[:, :, 0:C_HEADS * (C_NOPE + C_ROPE)]
        cmp_src = o[:, :, :].rearrange("p w (g t) -> p w g t", g=KVG)
        ps = ctx.enter_context(nc.psum_tensor("ps", [P, 8, 512], F32))
        acc = ps[:, 4:8, :]

        ident = cst[:, CST["ident"]:CST["ident"] + P]
        stat = small[:, 0:8]
        nmax = small[:, 8:12]
        sums = small[:, 12:16]
        rs = small[:, 16:20]
        lam = small[:, 20:22]
        lam_s = small[:, 22:26]
        eps = small[:, 26:27]
        rstd = small[:, 32:40]

        names = [n for n in totals if not n.endswith("_phase")]
        sem = {n: ctx.enter_context(nc.semaphore(n)) for n in names}
        for n in ("pe_phase", "act_phase", "dve_phase", "pool_phase", "hi_ready", "lo_ready", "step_used",
                  "loaded", "vec_stored", "stored", "bias_stored", "eps_set"):
            sem[n] = ctx.enter_context(nc.semaphore(n))
        raw_ready = [ctx.enter_context(nc.semaphore(f"raw_ready{i}")) for i in range(RING)]
        N_LOADED = 16 * 3

        ptc = pt[:, :, :, :].rearrange("p a b c -> p a (b c)")

        def wait(eng, semaphore, value):
            if isinstance(value, int) and value <= 0:
                return
            eng.wait_ge(semaphore, value)

        def enter(eng, me, ph):
            for e in ("pe", "act", "dve", "pool"):
                wait(eng, sem[e + "_phase"], ph.before[e])

        def leave(eng, me):
            eng.drain().then_inc(sem[me + "_phase"], 1)

        def run(eng, me, kinds):
            for ph in phases:
                if me in ph.engines:
                    enter(eng, me, ph)
                    kinds[ph.kind](ph)
                    leave(eng, me)

        def base(ph, name):
            return ph.base.get(name, 0)

        def at_step(c, i, stride):
            return c if i is None else stride * i + c

        def landings(c, i, stride):
            n = c // RING + 1
            return n if i is None else (stride // RING) * i + n

        def spread(ap, axis, n):
            dims = [list(d) for d in ap.ap]
            return bass.AP(ap.tensor, ap.offset, dims[:axis] + [[0, n]] + dims[axis:])

        def pipelined(eng, n, iteration):
            for t in range(4):
                iteration(t, t % 2, t // 2, [d for d in range(3) if t - d >= 0])
            if n > 4:
                with eng.Fori(2, n // 2) as i:
                    for parity in (0, 1):
                        iteration(2 * i + parity, parity, i, [0, 1, 2])
            for t in (n, n + 1):
                iteration(t, t % 2, t // 2, [d for d in (1, 2) if t - d < n])

        def job_of(ph):
            kind = ph.job
            first = kind in ("diff", "gqa1", "mla")
            wide = kind in ("diff", "mla")
            dv = P if wide else DH
            same = lambda t: t
            key, value = {
                "diff": (same, lambda t: t // 2),
                "gqa1": (lambda t: t // 4, lambda t: t // 4),
                "mla": (same, same),
                "gqa2": (lambda t: t // 8, lambda t: t // 8),
                "nsa_slc": (lambda t: t // 4, lambda t: t // 4),
                "nsa_win": (lambda t: t // 4 + KVG, lambda t: t // 4 + KVG),
                "moba": (same, same),
            }[kind]
            row = {"diff": lambda t: t // 2, "mla": lambda t: ph.bias0}.get(kind, lambda t: t + ph.bias0)
            return Job(q=q1 if first else q2, k=k1 if first else k2, rows=C_NOPE if kind == "mla" else DH, dv=dv,
                       rotary=kind == "mla", scale=(C_NOPE + C_ROPE if kind == "mla" else DH) ** -0.5, sink=ph.sink,
                       bias_row=row, key=key, vcol=lambda t: value(t) * dv,
                       ocol=lambda t: (t // 2 if kind == "diff" else t) * dv)

        def mixed(ph):
            return br1 if ph.stack == 1 else br2

        block = ctx.enter_context(nc.Block())

        @block.sync
        def _(sp):
            sp.dma_start(raw[:, 0, :], stream[0]).then_inc(raw_ready[0], 16)
            sp.dma_start(raw[:, 1, :], stream[1]).then_inc(raw_ready[1], 16)
            sp.dma_start(raw[:, 2, :], stream[2]).then_inc(raw_ready[2], 16)
            with sp.Fori(1, n_steps // RING) as i:
                for slot in range(RING):
                    sp.wait_ge(sem["lo_ready"], RING * i + (slot - RING + 1))
                    sp.dma_start(raw[:, slot, :], stream[RING * i + slot]).then_inc(raw_ready[slot], 16)
            for slot in range(RING):
                sp.wait_ge(raw_ready[slot], n_steps // RING * 16)

        @block.gpsimd
        def _(pool):
            def setup(ph):
                pool.wait_ge(sem["vec_stored"], 16)
                for qt in range(TT):
                    src = bass.AP(vec.tensor, T - 1 - qt * P, [[VEC, 2 * HEADS], [-1, P], [1, T]])
                    pool.dma_start(rel_bias[:, :, qt, :], src).then_inc(sem["bias_stored"], 16)
                pool.wait_ge(sem["bias_stored"], 32)

            def load_post(ph):
                row = post_in[ph.post:ph.post + 1, :].rearrange("a n -> (a n)")
                pool.dma_start(post[:, :], row.partition_broadcast(P)).then_inc(sem["post_loaded"], 16)
                pool.wait_ge(sem["post_loaded"], base(ph, "post_loaded") + 16)

            def attend(ph):
                job = job_of(ph)
                table = fixed_bias if ph.bias == "fixed" else rel_bias
                row0 = HEADS if ph.bias == "window" else 0
                loaded = (sem["bias_even"], sem["bias_odd"])
                b = base(ph, "q_staged")

                def stage(t, parity):
                    if not isinstance(t, int) or t >= 2:
                        pool.wait_ge(sem["scores_ready"], t + (base(ph, "scores_ready") - 1))
                    r = job.rows
                    if job.rotary:
                        pool.tensor_copy(qps[0:C_ROPE, parity, :], qpe[0:C_ROPE, t, :])
                    pool.tensor_copy(qs[0:r, parity, :], job.q[0:r, t, :]).then_inc(sem["q_staged"], 1)
                    if not isinstance(t, int) or t >= 2:
                        pool.wait_ge(sem["biased"], t + (base(ph, "biased") - 1))
                    pool.dma_start(bias[:, parity, :, :], table[job.bias_row(t) + row0]).then_inc(loaded[parity], 16)

                stage(0, 0)
                stage(1, 1)
                with pool.Fori(1, ph.n // 2) as i:
                    for parity in (0, 1):
                        stage(2 * i + parity, parity)

            run(pool, "pool", dict(setup=setup, residual=load_post, final=load_post, attend=attend))

        @block.scalar
        def _(act):
            def split(c, i=None, stride=0):
                slot = c % RING
                act.wait_ge(raw_ready[slot], 16 * landings(c, i, stride))
                wait(act, sem["step_used"], at_step(c - (RING - 1), i, stride))
                nc.scalar.copy(whi[:, slot, :], raw[:, slot, :]).then_inc(sem["hi_ready"], 1)

            def ahead(ph, k):
                split(ph.step + k + 2)

            def multiplied(c, i=None, stride=0):
                act.wait_ge(sem["step_used"], at_step(c + 1, i, stride))

            def setup(ph):
                act.dma_start(x[:, :, :], x_in).then_inc(sem["loaded"], 16)
                act.dma_start(prm[:, :], prm_in).then_inc(sem["loaded"], 16)
                act.dma_start(cst[:, :], cst_in).then_inc(sem["loaded"], 16)
                act.wait_ge(sem["lam_sum"], 1)
                nc.scalar.activation(lam_s, lam_s, ACT.Exp).then_inc(sem["lam_exp"], 1)
                act.wait_ge(sem["vec_copied"], 2)
                act.dma_start(vec.rearrange("(w h) n -> h w n", w=2),
                              o[0:HEADS, :, 0:VEC]).then_inc(sem["vec_stored"], 16)
                split(0)
                split(1)
                act.wait_ge(sem["vec_stored"], 16)

            def rms(ph, parts, scale):
                b = base(ph, "sumsq")
                for n, part in enumerate(parts):
                    junk = v[:, n, :] if len(part.shape) == 2 else v[:, n, :].rearrange("p (a b) -> p a b", a=2)
                    nc.scalar.activation(junk, part, ACT.Square, accum_out=stat[:, n:n + 1]).then_inc(sem["sumsq"], 1)
                act.wait_ge(sem["sumsq"], b + len(parts))

            def norm(ph):
                rms(ph, [x[:, tt, :] for tt in range(TT)], D)
                nc.scalar.activation(stat[:, 0:2], stat[:, 0:2], ACT.Sqrt, bias=eps,
                                     scale=1.0 / D).then_inc(sem["std_ready"], 1)
                for k in range(KD):
                    gain = prm[:, PRM["gain"] + ph.gain * KD + k:PRM["gain"] + ph.gain * KD + k + 1]
                    act.wait_ge(sem["tposed"], base(ph, "tposed") + k + 1)
                    nc.scalar.activation(xhl[:, k, 0:T], ps[:, k, 0:T], ACT.Identity,
                                         scale=gain).then_inc(sem["hi_made"], 1)

            def ffn(ph):
                def half_a(j):
                    nc.scalar.copy(ta[:, :, :], ps[:, 0:2, 0:T]).then_inc(sem["low_a"], 1)
                    act.wait_ge(sem["a_summed"], j + (base(ph, "a_summed") + 1))
                    nc.scalar.activation(silu[:, :, :], a_sum[:, :, :], ACT.Silu).then_inc(sem["silu_ready"], 1)

                def half_g(j):
                    nc.scalar.copy(tg[:, :, :], ps[:, 2:4, 0:T]).then_inc(sem["low_g"], 1)
                    act.wait_ge(sem["h_ready"], j + (base(ph, "h_ready") + 1))
                    nc.scalar.copy(ht[:, :, 0, :], h[:, :, :]).then_inc(sem["hh_ready"], 1)

                split(ph.step + 2)
                multiplied(ph.step)
                half_a(0)
                split(ph.step + 3)
                multiplied(ph.step + 1)
                half_g(0)
                with act.Fori(1, PAIRS) as j:
                    split(ph.step + 1, j, 3)
                    multiplied(ph.step - 1, j, 3)
                    half_a(j)
                    split(ph.step + 2, j, 3)
                    split(ph.step + 3, j, 3)
                    multiplied(ph.step + 1, j, 3)
                    half_g(j)
                ahead(ph, 3 * PAIRS - 1)

            def residual(ph):
                if ph.post is None:
                    return
                rms(ph, [acc[:, 2 * tt:2 * tt + 2, :] for tt in range(TT)], D)
                nc.scalar.activation(stat[:, 0:2], stat[:, 0:2], ACT.Sqrt, bias=eps,
                                     scale=1.0 / D).then_inc(sem["std_ready"], 1)

            def final(ph):
                rms(ph, [x[:, tt, :] for tt in range(TT)], D)
                nc.scalar.activation(stat[:, 0:2], stat[:, 0:2], ACT.Sqrt, bias=eps,
                                     scale=1.0 / D).then_inc(sem["std_ready"], 1)

            def proj_f(ph):
                for i in range(ph.n):
                    ahead(ph, i)
                    multiplied(ph.step + i)
                    wait(act, sem["group_free"], base(ph, "group_free") + i - 1)
                    nt = 1 if ph.dest == "kv" else 2
                    nc.scalar.copy(tl[:, i % 2, 0:nt, :], ps[:, 2 * (i % 2):2 * (i % 2) + nt, 0:T])\
                        .then_inc(sem["low_copied"], 1)
                    if ph.dest == "kv":
                        nc.scalar.copy(v[:, :, 0:P], ps[:, 4:6, P:T])

            def proj_t(ph):
                dest = {"v": v, "c": latent, "gate": gates}[ph.dest]
                for c in range(ph.chunks):
                    for i in range(ph.n):
                        ahead(ph, c * ph.n + i)
                    multiplied(ph.step + (c + 1) * ph.n - 1)
                    bank = 2 * (c % 2)
                    at = ph.col0 + c * ph.cols
                    func = ACT.Sigmoid if ph.dest == "gate" else ACT.Copy
                    nc.scalar.activation(dest[:, :, at:at + ph.cols], ps[:, bank:bank + 2, 0:ph.cols],
                                         func).then_inc(sem["group_free"], 1)

            def attend(ph):
                job = job_of(ph)
                width = T + 1 if job.sink is not None else T
                B = {n: base(ph, n) for n in ("max_ready", "transposed", "recip_ready", "pv_ready")}

                def iteration(t, parity, pair, stages):
                    if 0 in stages:
                        act.wait_ge(sem["max_ready"], t + (B["max_ready"] + 1))
                        if 2 in stages:
                            act.wait_ge(sem["transposed"], t + (B["transposed"] - 1))
                            act.wait_ge(sem["recip_ready"], t + (B["recip_ready"] - 1))
                        for qt in range(TT):
                            n = 2 * parity + qt
                            e = nc.scalar.activation(pr[:, parity, qt, 0:width], s[:, parity, qt, 0:width], ACT.Exp,
                                                     bias=nmax[:, n:n + 1], accum_out=sums[:, n:n + 1])
                        e.then_inc(sem["probs_ready"], 1)
                    if 1 in stages:
                        act.wait_ge(sem["transposed"], t + B["transposed"])
                        if not isinstance(t, int) or t >= 3:
                            act.wait_ge(sem["pv_ready"], t + (B["pv_ready"] - 2))
                        nc.scalar.copy(pt[:, 1 - parity, :, :],
                                       ps[:, 3 - parity, :].rearrange("p (k q) -> p k q", k=TT))\
                            .then_inc(sem["pt_ready"], 1)

                pipelined(act, ph.n, iteration)

            def turn(ph):
                for k in range(ph.n):
                    act.wait_ge(sem["tposed"], base(ph, "tposed") + k + 1)
                    dst = mixed(ph)[:, ph.k0 + k, 0:T]
                    if ph.subln is None:
                        nc.scalar.copy(dst, ps[:, k, 0:T]).then_inc(sem["hi_made"], 1)
                    else:
                        g = prm[:, PRM["subln"] + ph.subln:PRM["subln"] + ph.subln + 1]
                        nc.scalar.activation(dst, ps[:, k, 0:T], ACT.Identity, scale=g).then_inc(sem["hi_made"], 1)

            def turn_subln(ph):
                if ph.subln is not None:
                    act.wait_ge(sem["head_norm"], base(ph, "head_norm") + 2)
                    nc.scalar.activation(stat[:, 0:8], stat[:, 0:8], ACT.Sqrt, bias=eps,
                                         scale=1.0 / P).then_inc(sem["head_norm"], 1)
                turn(ph)

            def mla_latent(ph):
                parts = [latent[:, tt, 0:C_QR] for tt in range(TT)] + [latent[:, tt, C_QR:C_QR + C_KVR]
                                                                      for tt in range(TT)]
                for n, part in enumerate(parts):
                    nc.scalar.activation(v[:, n // 2, 512 * (n % 2):512 * (n % 2) + part.free_size()], part,
                                         ACT.Square, accum_out=stat[:, n:n + 1]).then_inc(sem["sumsq"], 1)
                act.wait_ge(sem["sumsq"], base(ph, "sumsq") + 4)
                nc.scalar.activation(stat[:, 0:2], stat[:, 0:2], ACT.Sqrt, bias=eps,
                                     scale=1.0 / C_QR).then_inc(sem["std_ready"], 1)
                nc.scalar.activation(stat[:, 2:4], stat[:, 2:4], ACT.Sqrt, bias=eps,
                                     scale=1.0 / C_KVR).then_inc(sem["std_ready"], 1)
                for k in range(5):
                    at = PRM["cqn"] + ph.layer * 3 + k if k < 3 else PRM["ckvn"] + ph.layer * 2 + k - 3
                    act.wait_ge(sem["tposed"], base(ph, "tposed") + k + 1)
                    nc.scalar.activation(chl[:, k, 0:T], ps[:, k, 0:T], ACT.Identity,
                                         scale=prm[:, at:at + 1]).then_inc(sem["hi_made"], 1)

            def mla_up(ph):
                gr = base(ph, "group_ready")
                for i in range(2):
                    ahead(ph, i)
                    multiplied(ph.step + i)
                    nc.scalar.copy(qtok[:, :, i * C_QR:(i + 1) * C_QR],
                                   ps[:, 2 * i:2 * i + 2, 0:C_QR]).then_inc(sem["qv_stored"], 1)
                ahead(ph, 2)
                for i in range(2):
                    act.wait_ge(sem["group_ready"], gr + 1 + i)
                    nc.scalar.copy(tl[:, i, :, :], ps[:, 4 + 2 * i:6 + 2 * i, 0:T]).then_inc(sem["low_copied"], 1)
                multiplied(ph.step + 2)
                nc.scalar.copy(v[:, :, 0:512], ps[:, 0:2, :]).then_inc(sem["qv_stored"], 1)

            def gates_(ph):
                gf = base(ph, "group_free")
                with act.Fori(0, 4) as grp:
                    for n in range(3):
                        for part in range(2):
                            m = 2 * n + part
                            split(ph.step + m + 2, grp, 6)
                            multiplied(ph.step + m, grp, 6)
                            if part == 0:
                                dst = ta
                            else:
                                dst = tg
                            nc.scalar.copy(dst[:, :, :], ps[:, 2 * part:2 * part + 2, 0:T]).then_inc(sem["low_copied"], 1)
                            if part == 0:
                                act.wait_ge(sem["group_free"], 6 * grp + (gf + m + 1))
                                for i in range(2):
                                    col = PRM["bgate"] + ph.layer * 24 + n * 8 + i
                                    b = prm[:, bass.ds(2 * grp + col, 1)]
                                    e = nc.scalar.activation(silu[:, i, :], a_sum[:, i, :], ACT.Sigmoid, bias=b)
                                e.then_inc(sem["gate_ready"], 1)
                    act.wait_ge(sem["y_ready"], 3 * grp + (base(ph, "y_ready") + 3))
                    nc.scalar.copy(yhl[:, bass.ds(2 * grp, 2), 0:T], h[:, :, :]).then_inc(sem["hh_ready"], 1)

            def wout(ph):
                for i in range(4):
                    ahead(ph, i)

            def compress(ph):
                for w in range(2):
                    ahead(ph, 2 * w)
                    ahead(ph, 2 * w + 1)
                    multiplied(ph.step + 2 * w + 1)
                    nc.scalar.copy(tl[:, w, :, 0:NBLK], ps[:, 2 * w:2 * w + 2, 0:NBLK]).then_inc(sem["low_copied"], 1)
                    act.wait_ge(sem["group_free"], base(ph, "group_free") + w + 1)
                    nc.scalar.activation(chid[:, w, :, :], cpre[:, w, :, :], ACT.Gelu_apprx_tanh)\
                        .then_inc(sem["gelu_done"], 1)

            def cmp_attend(ph):
                act.wait_ge(sem["max_ready"], base(ph, "max_ready") + 1)
                nc.scalar.activation(scmp[:, :, :, :], scmp[:, :, :, :], ACT.Exp).then_inc(sem["probs_ready"], 1)
                act.wait_ge(sem["transposed"], base(ph, "transposed") + 1)
                nc.scalar.copy(ptc, ps[:, 2:4, :]).then_inc(sem["pt_ready"], 1)

            def store(ph):
                act.dma_start(out, x[:, :, :]).then_inc(sem["stored"], 16)
                act.wait_ge(sem["stored"], 16)

            run(act, "act", dict(setup=setup, norm=norm, ffn=ffn, residual=residual, final=final, proj_f=proj_f,
                                 proj_t=proj_t, attend=attend, turn=turn_subln, mla_latent=mla_latent,
                                 mla_up=mla_up, gates=gates_, wout=wout, compress=compress, cmp_attend=cmp_attend,
                                 store=store))

        @block.vector
        def _(dve):
            def split(c, i=None, stride=0):
                slot = c % RING
                dve.wait_ge(sem["hi_ready"], at_step(c + 1, i, stride))
                wait(dve, sem["step_used"], at_step(c - (RING - 1), i, stride))
                nc.vector.tensor_tensor(wlo[:, slot, :], raw[:, slot, :], whi[:, slot, :].bitcast(F32),
                                        ALU.subtract).then_inc(sem["lo_ready"], 1)

            def ahead(ph, k):
                split(ph.step + k + 2)

            def setup(ph):
                nc.vector.memset(eps, EPS)
                dve.wait_ge(sem["loaded"], N_LOADED)
                lp = prm[:, PRM["lam"]:PRM["lam"] + DEPTH1 * 4 * DH].rearrange("p (la b d) -> p la b d", b=2, d=DH)
                prod = v[:, 0, 0:4 * DH].rearrange("p (a d) -> p a d", a=4)
                nc.vector.tensor_tensor(prod, lp[:, :, 0, :], lp[:, :, 1, :], ALU.mult).then_inc(sem["lam_mul"], 1)
                dve.wait_ge(sem["lam_mul"], 1)
                nc.vector.tensor_reduce(lam_s, prod, AX.X, ALU.add).then_inc(sem["lam_sum"], 1)
                for w in range(2):
                    dve.wait_ge(sem["vec_made"], w + 1)
                    nc.vector.tensor_copy(o[0:HEADS, w, 0:VEC], ps[0:HEADS, w, :]).then_inc(sem["vec_copied"], 1)
                dve.wait_ge(sem["lam_exp"], 1)
                for l in range(DEPTH1):
                    nc.vector.scalar_tensor_tensor(out=lam[:, l:l + 1], in0=lam_s[:, 2 * l + 1:2 * l + 2],
                                                   scalar=-LAM0[l], in1=lam_s[:, 2 * l:2 * l + 1], op0=ALU.add,
                                                   op1=ALU.subtract).then_inc(sem["lam_sub"], 1)
                split(0)
                split(1)

            def low_parts(ph, n, dst, gain):
                for k in range(n):
                    dve.wait_ge(sem["hi_made"], base(ph, "hi_made") + k + 1)
                    hi = dst[:, k, 0:T].bitcast(F32)
                    g = gain(k)
                    nc.vector.scalar_tensor_tensor(out=dst[:, k, T:2 * T], in0=ps[:, k, 0:T],
                                                   scalar=1.0 if g is None else g, in1=hi, op0=ALU.mult,
                                                   op1=ALU.subtract)

            def inverse_rms(ph, n):
                dve.wait_ge(sem["std_ready"], base(ph, "std_ready") + 1)
                nc.vector.reciprocal(rstd[:, 0:n], stat[:, 0:n]).then_inc(sem["rstd_ready"], 1)
                dve.wait_ge(sem["rstd_ready"], base(ph, "rstd_ready") + 1)

            def norm(ph):
                inverse_rms(ph, TT)
                for tt in range(TT):
                    nc.vector.tensor_scalar(o[:, tt, :], x[:, tt, :], rstd[:, tt:tt + 1], None, ALU.mult)\
                        .then_inc(sem["xn_ready"], 1)
                low_parts(ph, KD, xhl, lambda k: prm[:, PRM["gain"] + ph.gain * KD + k:
                                                     PRM["gain"] + ph.gain * KD + k + 1])

            def ffn(ph):
                def half_a(j):
                    dve.wait_ge(sem["low_a"], j + (base(ph, "low_a") + 1))
                    if not isinstance(j, int):
                        dve.wait_ge(sem["silu_ready"], j + base(ph, "silu_ready"))
                    nc.vector.tensor_tensor(a_sum[:, :, :], ps[:, 0:2, T:2 * T], ta[:, :, :], ALU.add)\
                        .then_inc(sem["a_summed"], 1)

                def half_g(j):
                    dve.wait_ge(sem["low_g"], j + (base(ph, "low_g") + 1))
                    nc.vector.tensor_tensor(g_sum[:, :, :], ps[:, 2:4, T:2 * T], tg[:, :, :], ALU.add)\
                        .then_inc(sem["g_summed"], 1)
                    dve.wait_ge(sem["g_summed"], j + (base(ph, "g_summed") + 1))
                    dve.wait_ge(sem["silu_ready"], j + (base(ph, "silu_ready") + 1))
                    nc.vector.tensor_tensor(h[:, :, :], g_sum[:, :, :], silu[:, :, :], ALU.mult)\
                        .then_inc(sem["h_ready"], 1)
                    dve.wait_ge(sem["hh_ready"], j + (base(ph, "hh_ready") + 1))
                    nc.vector.tensor_tensor(ht[:, :, 1, :], h[:, :, :], ht[:, :, 0, :].bitcast(F32), ALU.subtract)\
                        .then_inc(sem["ht_ready"], 1)

                split(ph.step + 2)
                half_a(0)
                split(ph.step + 3)
                half_g(0)
                with dve.Fori(1, PAIRS) as j:
                    split(ph.step + 1, j, 3)
                    half_a(j)
                    split(ph.step + 2, j, 3)
                    split(ph.step + 3, j, 3)
                    half_g(j)
                ahead(ph, 3 * PAIRS - 1)

            def residual(ph):
                if ph.post is None:
                    for tt in range(TT):
                        xt = x[:, tt, :].rearrange("p (a b) -> p a b", a=2)
                        nc.vector.scalar_tensor_tensor(out=xt, in0=acc[:, 2 * tt:2 * tt + 2, :], scalar=ph.factor,
                                                       in1=xt, op0=ALU.mult, op1=ALU.add)
                    return
                inverse_rms(ph, TT)
                dve.wait_ge(sem["post_loaded"], base(ph, "post_loaded") + 16)
                for tt in range(TT):
                    nc.vector.scalar_tensor_tensor(out=o[:, tt, :].rearrange("p (a b) -> p a b", a=2),
                                                   in0=acc[:, 2 * tt:2 * tt + 2, :], scalar=rstd[:, tt:tt + 1],
                                                   in1=post[:, :].rearrange("p (a b) -> p a b", a=2), op0=ALU.mult,
                                                   op1=ALU.mult).then_inc(sem["y_ready"], 1)
                for tt in range(TT):
                    dve.wait_ge(sem["y_ready"], base(ph, "y_ready") + tt + 1)
                    nc.vector.scalar_tensor_tensor(out=x[:, tt, :], in0=o[:, tt, :], scalar=ph.factor,
                                                   in1=x[:, tt, :], op0=ALU.mult, op1=ALU.add)

            def final(ph):
                inverse_rms(ph, TT)
                dve.wait_ge(sem["post_loaded"], base(ph, "post_loaded") + 16)
                for tt in range(TT):
                    nc.vector.scalar_tensor_tensor(out=x[:, tt, :], in0=x[:, tt, :], scalar=rstd[:, tt:tt + 1],
                                                   in1=post[:, :], op0=ALU.mult, op1=ALU.mult)\
                        .then_inc(sem["y_ready"], 1)

            def add_heads(dst, head0, bank, low, tiles=2):
                for i in range(tiles):
                    for half in range(2):
                        r = slice(half * DH, half * DH + DH)
                        e = nc.vector.tensor_tensor(dst[0:DH, head0 + 2 * i + half, :], ps[r, bank + i, T:2 * T],
                                                    low[r, i, :], ALU.add)
                return e

            def proj_f(ph):
                q, k = (q1, k1) if ph.stack == 1 else (q2, k2)
                for i in range(ph.n):
                    ahead(ph, i)
                    dve.wait_ge(sem["low_copied"], base(ph, "low_copied") + i + 1)
                    bank, low = 2 * (i % 2), tl[:, i % 2, :, :]
                    if ph.dest == "cmp":
                        for tile in range(2):
                            for half in range(2):
                                r = slice(half * DH, half * DH + DH)
                                g = 2 * tile + half
                                nc.vector.tensor_tensor(cmp_src[0:DH, i, g, :], ps[r, bank + tile, T:2 * T],
                                                        low[r, tile, :], ALU.add)
                                e = nc.vector.tensor_tensor(cmp_src[DH:P, i, g, 0:T - 1],
                                                            ps[r, bank + tile, T + 1:2 * T], low[r, tile, 1:T],
                                                            ALU.add)
                    elif ph.dest == "kv":
                        e = add_heads(k, 0, bank, low, tiles=1)
                    else:
                        e = add_heads(q if ph.dest == "q" else k, ph.head0 + 4 * i, bank, low)
                    e.then_inc(sem["group_free"], 1)

            def proj_t(ph):
                for i in range(ph.n * ph.chunks):
                    ahead(ph, i)

            def attend(ph):
                job = job_of(ph)
                width = T + 1 if job.sink is not None else T
                loaded = (sem["bias_even"], sem["bias_odd"])
                b_loaded = (base(ph, "bias_even"), base(ph, "bias_odd"))
                B = {n: base(ph, n) for n in ("scores_ready", "biased", "probs_ready", "recip_ready", "rs_ready",
                                              "pv_ready", "o_done")}
                branch = {"nsa_slc": 1, "nsa_win": 2}.get(ph.job)

                def iteration(t, parity, pair, stages):
                    if 0 in stages:
                        if 2 in stages:
                            dve.wait_ge(sem["probs_ready"], t + (B["probs_ready"] - 1))
                        if job.sink is not None:
                            sink = spread(prm[:, bass.ds(t + job.sink, 1)], 1, TT)
                            nc.vector.tensor_copy(s[:, parity, :, SINK:SINK + 1], sink)
                        dve.wait_ge(sem["scores_ready"], t + (B["scores_ready"] + 1))
                        dve.wait_ge(loaded[parity], 16 * pair + (b_loaded[parity] + 16))
                        nc.vector.scalar_tensor_tensor(
                            out=s[:, parity, :, 0:T], in0=ps[:, parity, :].rearrange("p (a b) -> p a b", a=TT),
                            scalar=job.scale, in1=bias[:, parity, :, :], op0=ALU.mult,
                            op1=ALU.add).then_inc(sem["biased"], 1)
                        dve.wait_ge(sem["biased"], t + (B["biased"] + 1))
                        nc.vector.tensor_reduce(nmax[:, 2 * parity:2 * parity + 2], s[:, parity, :, 0:width], AX.X,
                                                ALU.max, negate=True).then_inc(sem["max_ready"], 1)
                    if 1 in stages:
                        r = rs[:, 2 - 2 * parity:4 - 2 * parity]
                        dve.wait_ge(sem["probs_ready"], t + B["probs_ready"])
                        if not isinstance(t, int) or t >= 3:
                            dve.wait_ge(sem["o_done"], t + (B["o_done"] - 2))
                        nc.vector.reciprocal(r, sums[:, 2 - 2 * parity:4 - 2 * parity]).then_inc(sem["recip_ready"], 1)
                        if ph.job == "diff" and parity == 0:
                            dve.wait_ge(sem["recip_ready"], t + B["recip_ready"])
                            nc.vector.tensor_scalar(r, r, lam[:, ph.layer:ph.layer + 1], None,
                                                    ALU.mult).then_inc(sem["rs_ready"], 1)
                        if branch is not None:
                            dve.wait_ge(sem["recip_ready"], t + B["recip_ready"])
                            g = gates[:, :, bass.ds((t - 1) * 3 + branch, 1)]
                            nc.vector.tensor_tensor(r.rearrange("p (a b) -> p a b", b=1),
                                                    r.rearrange("p (a b) -> p a b", b=1), g,
                                                    ALU.mult).then_inc(sem["rs_ready"], 1)
                    if 2 in stages:
                        dve.wait_ge(sem["recip_ready"], t + (B["recip_ready"] - 1))
                        if ph.job == "diff" and parity == 1:
                            dve.wait_ge(sem["rs_ready"], pair + B["rs_ready"])
                        if branch is not None:
                            dve.wait_ge(sem["rs_ready"], t + (B["rs_ready"] - 1))
                        dve.wait_ge(sem["pv_ready"], t + (B["pv_ready"] - 1))
                        add = branch is not None or (ph.job == "diff" and parity == 1)
                        if ph.job == "diff" and parity == 1:
                            dve.wait_ge(sem["o_done"], t + (B["o_done"] - 2))
                        for qt in range(TT):
                            dst = o[:, qt, bass.ds(job.ocol(t - 2), job.dv)]
                            src = ps[:, 4 + parity, qt * P:qt * P + job.dv]
                            r = rs[:, 2 * parity + qt:2 * parity + qt + 1]
                            if add:
                                e = nc.vector.scalar_tensor_tensor(out=dst, in0=src, scalar=r, in1=dst, op0=ALU.mult,
                                                                   op1=ALU.add)
                            else:
                                e = nc.vector.tensor_scalar(dst, src, r, None, ALU.mult)
                        e.then_inc(sem["o_done"], 1)

                pipelined(dve, ph.n, iteration)

            def turn(ph):
                gain = lambda k: None
                if ph.subln is not None:
                    b = base(ph, "head_norm")
                    heads = o[:, :, 0:A_HEADS * P].rearrange("p t (h c) -> p t h c", c=P)
                    sq = v[:, :, 0:A_HEADS * P].rearrange("p t (h c) -> p t h c", c=P)
                    nc.vector.tensor_tensor(sq, heads, heads, ALU.mult).then_inc(sem["head_norm"], 1)
                    dve.wait_ge(sem["head_norm"], b + 1)
                    nc.vector.tensor_reduce(stat.rearrange("p (t h) -> p t h", t=TT), sq, AX.X,
                                            ALU.add).then_inc(sem["head_norm"], 1)
                    dve.wait_ge(sem["head_norm"], b + 3)
                    nc.vector.reciprocal(rstd, stat).then_inc(sem["head_norm"], 1)
                    dve.wait_ge(sem["head_norm"], b + 4)
                    for tt in range(TT):
                        r = spread(rstd[:, tt * A_HEADS:(tt + 1) * A_HEADS], 2, P)
                        nc.vector.scalar_tensor_tensor(out=heads[:, tt], in0=heads[:, tt],
                                                       scalar=1.0 - LAM0[ph.subln], in1=r, op0=ALU.mult,
                                                       op1=ALU.mult).then_inc(sem["head_norm"], 1)
                    gain = lambda k: prm[:, PRM["subln"] + ph.subln:PRM["subln"] + ph.subln + 1]
                low_parts(ph, ph.n, mixed(ph)[:, ph.k0:ph.k0 + ph.n, :], gain)

            def rotate(lo, hi, c, sn, n, tmp, after):
                t1, t2, t3, t4 = tmp
                nc.vector.tensor_tensor(t1, lo, c, ALU.mult)
                nc.vector.tensor_tensor(t2, hi, sn, ALU.mult)
                nc.vector.tensor_tensor(t3, lo, sn, ALU.mult)
                nc.vector.tensor_tensor(t4, hi, c, ALU.mult).then_inc(after[0], 1)
                dve.wait_ge(after[0], after[1] + 1)
                nc.vector.tensor_tensor(lo, t1, t2, ALU.subtract)
                nc.vector.tensor_tensor(hi, t3, t4, ALU.add).then_inc(after[0], 1)

            cos = cst[:, CST["cos"]:CST["cos"] + TT * 32].rearrange("p (t f) -> p t f", t=TT)
            sin = cst[:, CST["sin"]:CST["sin"] + TT * 32].rearrange("p (t f) -> p t f", t=TT)

            def mla_latent(ph):
                b = base(ph, "xn_ready")
                at = C_QR + C_KVR
                tmp = [pr[:, 0, :, 64 * i:64 * i + 32] for i in range(4)]
                rotate(latent[:, :, at:at + 32], latent[:, :, at + 32:at + 64], cos, sin, 1, tmp, (sem["xn_ready"], b))
                dve.wait_ge(sem["std_ready"], base(ph, "std_ready") + 2)
                nc.vector.reciprocal(rstd[:, 0:4], stat[:, 0:4]).then_inc(sem["rstd_ready"], 1)
                dve.wait_ge(sem["rstd_ready"], base(ph, "rstd_ready") + 1)
                for n in range(4):
                    c0, c1 = ((0, C_QR), (C_QR, at))[n // 2]
                    part = latent[:, n % 2, c0:c1]
                    nc.vector.tensor_scalar(part, part, rstd[:, n:n + 1], None, ALU.mult).then_inc(sem["xn_ready"], 1)

                def gain(k):
                    at = PRM["cqn"] + ph.layer * 3 + k if k < 3 else PRM["ckvn"] + ph.layer * 2 + k - 3
                    return prm[:, at:at + 1]

                low_parts(ph, 5, chl, gain)
                dve.wait_ge(sem["tposed"], base(ph, "tposed") + 6)
                nc.vector.tensor_copy(kpe[0:C_ROPE, :], ps[0:C_ROPE, 5, 0:T])

            def mla_up(ph):
                lc = base(ph, "low_copied")
                ahead(ph, 0)
                ahead(ph, 1)
                ahead(ph, 2)
                for i in range(2):
                    dve.wait_ge(sem["low_copied"], lc + i + 1)
                    nc.vector.tensor_tensor(k1[:, 2 * i:2 * i + 2, :], ps[:, 4 + 2 * i:6 + 2 * i, T:2 * T],
                                            tl[:, i, :, :], ALU.add).then_inc(sem["k_stored"], 1)
                dve.wait_ge(sem["qv_stored"], base(ph, "qv_stored") + 2)
                heads = qtok.rearrange("p t (h c) -> p t h c", h=C_HEADS)
                b = base(ph, "rope_done")
                for tt in range(TT):
                    c, sn = spread(cos[:, tt, :], 1, C_HEADS), spread(sin[:, tt, :], 1, C_HEADS)
                    tmp = [pr[:, i // 2, i % 2, 0:128].rearrange("p (h f) -> p h f", f=32) if tt == 0 else
                           s[:, i // 2, i % 2, 0:128].rearrange("p (h f) -> p h f", f=32) for i in range(4)]
                    rotate(heads[:, tt, :, C_NOPE:C_NOPE + 32], heads[:, tt, :, C_NOPE + 32:C_NOPE + 64], c, sn,
                           C_HEADS, tmp, (sem["rope_done"], b + 2 * tt))
                for n in range(8):
                    dve.wait_ge(sem["tposed"], base(ph, "tposed") + n + 1)
                    if n < 4:
                        nc.vector.tensor_copy(q1[:, n, :], ps[:, n, 0:T])
                    else:
                        nc.vector.tensor_copy(qpe[0:C_ROPE, n - 4, :], ps[0:C_ROPE, n, 0:T])

            def gates_(ph):
                with dve.Fori(0, 4) as grp:
                    for n in range(3):
                        for part in range(2):
                            m = 2 * n + part
                            split(ph.step + m + 2, grp, 6)
                            dve.wait_ge(sem["low_copied"], 6 * grp + (base(ph, "low_copied") + m + 1))
                            dst, low = (a_sum, ta) if part == 0 else (g_sum, tg)
                            nc.vector.tensor_tensor(dst[:, :, :], ps[:, 2 * part:2 * part + 2, T:2 * T],
                                                    low[:, :, :], ALU.add).then_inc(sem["group_free"], 1)
                        dve.wait_ge(sem["gate_ready"], 3 * grp + (base(ph, "gate_ready") + n + 1))
                        dve.wait_ge(sem["group_free"], 6 * grp + (base(ph, "group_free") + 2 * n + 2))
                        if n == 0:
                            nc.vector.tensor_tensor(h[:, :, :], g_sum[:, :, :], silu[:, :, :], ALU.mult)\
                                .then_inc(sem["y_ready"], 1)
                        else:
                            nc.vector.tensor_tensor(g_sum[:, :, :], g_sum[:, :, :], silu[:, :, :], ALU.mult)\
                                .then_inc(sem["prod_ready"], 1)
                            dve.wait_ge(sem["prod_ready"], 2 * grp + (base(ph, "prod_ready") + n))
                            dve.wait_ge(sem["y_ready"], 3 * grp + (base(ph, "y_ready") + n))
                            nc.vector.tensor_tensor(h[:, :, :], h[:, :, :], g_sum[:, :, :], ALU.add)\
                                .then_inc(sem["y_ready"], 1)
                    dve.wait_ge(sem["hh_ready"], grp + (base(ph, "hh_ready") + 1))
                    nc.vector.tensor_tensor(yhl[:, bass.ds(2 * grp, 2), T:2 * T], h[:, :, :],
                                            yhl[:, bass.ds(2 * grp, 2), 0:T].bitcast(F32), ALU.subtract)

            def wout(ph):
                for i in range(4):
                    ahead(ph, i)

            def compress(ph):
                for w in range(2):
                    pos = prm[:, PRM["pos"] + w * LP:PRM["pos"] + (w + 1) * LP]
                    wait(dve, sem["blk_made"], base(ph, "blk_made") + w)
                    for g in range(KVG):
                        src = cmp_src[:, w, g, :]
                        blocks = bass.AP(src.tensor, src.offset, [list(src.ap[0]), [2, LP], [CMP_STRIDE, NCMP]])
                        e = nc.vector.tensor_tensor(cblk[:, :, g, :], blocks, spread(pos, 2, NCMP), ALU.add)
                    e.then_inc(sem["blk_added"], 1)
                    dve.wait_ge(sem["blk_added"], base(ph, "blk_added") + w + 1)
                    flat = cblk[:, :, :, :].rearrange("p l g n -> p l (g n)")
                    nc.vector.tensor_copy(blk[:, w, :, 0:NBLK], flat).then_inc(sem["blk_hi"], 1)
                    dve.wait_ge(sem["blk_hi"], base(ph, "blk_hi") + w + 1)
                    nc.vector.tensor_tensor(blk[:, w, :, NBLK:2 * NBLK], flat, blk[:, w, :, 0:NBLK].bitcast(F32),
                                            ALU.subtract).then_inc(sem["blk_made"], 1)
                nc.vector.memset(vblk[:, :, :], 0.0)
                for w in range(2):
                    ahead(ph, 2 * w)
                    ahead(ph, 2 * w + 1)
                    dve.wait_ge(sem["low_copied"], base(ph, "low_copied") + w + 1)
                    nc.vector.tensor_tensor(cpre[:, w, :, :], ps[:, 2 * w:2 * w + 2, NBLK:2 * NBLK],
                                            tl[:, w, :, 0:NBLK], ALU.add).then_inc(sem["group_free"], 1)
                dve.wait_ge(sem["cmp_ready"], base(ph, "cmp_ready") + 1)
                nc.vector.tensor_copy(kcb[0:DH, :], ps[0:DH, 4, 0:NBLK])
                for n in range(4):
                    nc.vector.tensor_copy(vblk[32 * n:32 * n + NCMP, :, n * DH:(n + 1) * DH],
                                          ps[0:NCMP, 5, 0:KVG * DH].rearrange("p (g d) -> p g d", g=KVG))

            def cmp_attend(ph):
                b = base(ph, "cmp_step")
                n = [0]

                def then(e):
                    n[0] += 1
                    e.then_inc(sem["cmp_step"], 1)
                    dve.wait_ge(sem["cmp_step"], b + n[0])

                neg = cst[:, CST["cmpneg"]:CST["cmpneg"] + TT * NCMP].rearrange("p (t n) -> p t n", t=TT)
                ok = cst[:, CST["cmpok"]:CST["cmpok"] + TT * NCMP].rearrange("p (t n) -> p t n", t=TT)
                rows = scmp[:, :, :, :].rearrange("p t h n -> p (t h) n")
                cmax, csum = small[:, 64:96], small[:, 96:128]
                then(nc.vector.memset(pcmp[:, :, :, :], 0.0))
                dve.wait_ge(sem["scores_ready"], base(ph, "scores_ready") + 1)
                then(nc.vector.tensor_scalar(scmp[:, :, :, :].rearrange("p t h n -> p (t h n)"),
                                             ps[:, 0, 0:TT * HEADS * NCMP], DH ** -0.5, None, ALU.mult))
                then(nc.vector.tensor_tensor(scmp[:, :, :, :], scmp[:, :, :, :], spread(neg, 2, HEADS), ALU.add))
                then(nc.vector.tensor_reduce(cmax, rows, AX.X, ALU.max))
                nc.vector.tensor_tensor(rows, rows, spread(cmax, 2, NCMP), ALU.subtract).then_inc(sem["max_ready"], 1)
                dve.wait_ge(sem["probs_ready"], base(ph, "probs_ready") + 1)
                then(nc.vector.tensor_tensor(scmp[:, :, :, :], scmp[:, :, :, :], spread(ok, 2, HEADS), ALU.mult))
                then(nc.vector.tensor_reduce(csum, rows, AX.X, ALU.add))
                then(nc.vector.tensor_scalar(csum, csum, TINY, None, ALU.max))
                then(nc.vector.reciprocal(csum, csum))
                g = gates[:, :, :].rearrange("p t (h b) -> p t h b", b=3)[:, :, :, 0]
                sums3 = csum.rearrange("p (t h) -> p t h", t=TT)
                then(nc.vector.tensor_tensor(sums3, sums3, g, ALU.mult))
                then(nc.vector.tensor_tensor(pcmp[:, :, :, 0:NCMP].rearrange("p t h n -> p (t h) n"), rows,
                                             spread(csum, 2, NCMP), ALU.mult))
                dve.wait_ge(sem["pv_ready"], base(ph, "pv_ready") + 1)
                for tt in range(TT):
                    nc.vector.tensor_copy(o[:, tt, :].rearrange("p (a b) -> p a b", a=2),
                                          ps[:, 4 + 2 * tt:6 + 2 * tt, :])

            run(dve, "dve", dict(setup=setup, norm=norm, ffn=ffn, residual=residual, final=final, proj_f=proj_f,
                                 proj_t=proj_t, attend=attend, turn=turn, mla_latent=mla_latent, mla_up=mla_up,
                                 gates=gates_, wout=wout, compress=compress, cmp_attend=cmp_attend))

        @block.tensor
        def _(pe):
            def step_parts(c, kk, cols):
                w = [part[:, c % RING, 0:kk * cols].rearrange("p (k n) -> p k n", k=kk) for part in (whi, wlo)]
                return w

            def use(c, i=None, stride=0):
                pe.wait_ge(sem["lo_ready"], at_step(c + 1, i, stride))

            def feature_tile(bank, w, col0, src, k0=0, first=True, last=True):
                hi, lo = w
                n = hi.shape[1]
                half = src.shape[2] // 2
                for k in range(n):
                    wide = lambda: pe.matmul(ps[:, bank, 0:2 * half], hi[:, k, col0:col0 + P], src[:, k0 + k, :],
                                             start=first and k == 0, stop=last and k == n - 1)
                    if k == 0:
                        wide()
                    e = pe.matmul(ps[:, bank, 0:half], lo[:, k, col0:col0 + P], src[:, k0 + k, 0:half],
                                  start=False, stop=False)
                    if k > 0:
                        e = wide()
                return e

            def token_tile(bank, w, cols, src, tt, k0=0, first=True, last=True):
                n = w[0].shape[1]
                for k in range(n):
                    hi, lo = cols(w[0], k), cols(w[1], k)
                    xh = src[:, k0 + k, tt * P:(tt + 1) * P]
                    xl = src[:, k0 + k, T + tt * P:T + (tt + 1) * P]
                    width = hi.free_size()
                    dst = ps[:, bank, 0:width]
                    if len(hi.shape) == 3:
                        dst = dst.rearrange("p (a b) -> p a b", a=hi.shape[1])
                    pe.matmul(dst, xh, hi, start=first and k == 0, stop=False)
                    pe.matmul(dst, xh, lo, start=False, stop=False)
                    e = pe.matmul(dst, xl, hi, start=False, stop=last and k == n - 1)
                return e

            def setup(ph):
                pe.wait_ge(sem["loaded"], N_LOADED)
                table = prm[0:BUCKETS + 1, PRM["table"]:PRM["table"] + HEADS]
                for w in range(2):
                    hot = cst[0:BUCKETS + 1, CST["onehot"] + w * VEC:CST["onehot"] + (w + 1) * VEC]
                    pe.matmul(ps[0:HEADS, w, :], table, hot, start=True, stop=True).then_inc(sem["vec_made"], 1)

            def norm(ph):
                for k in range(KD):
                    for tt in range(TT):
                        if k == 0:
                            pe.wait_ge(sem["xn_ready"], base(ph, "xn_ready") + tt + 1)
                        e = pe.transpose(ps[:, k, tt * P:(tt + 1) * P], o[:, tt, k * P:(k + 1) * P], ident)
                    e.then_inc(sem["tposed"], 1)

            def ffn(ph):
                def up(c, bank, j=None):
                    use(c, j, 3)
                    w = step_parts(c, KD, 2 * P)
                    feature_tile(bank, w, 0, xhl)
                    feature_tile(bank + 1, w, P, xhl).then_inc(sem["step_used"], 1)

                def down(c, pair, j=None, first=False, last=False):
                    pe.wait_ge(sem["ht_ready"], pair + (base(ph, "ht_ready") + 1))
                    use(c, j, 3)
                    w = step_parts(c, 2, D)
                    for kk in range(2):
                        for tt in range(TT):
                            hh, hl = (ht[:, kk, part, tt * P:(tt + 1) * P] for part in (0, 1))
                            for half in range(2):
                                cols = slice(512 * half, 512 * half + 512)
                                dst = acc[:, 2 * tt + half, :]
                                pe.matmul(dst, hh, w[0][:, kk, cols], start=first and kk == 0, stop=False)
                                pe.matmul(dst, hh, w[1][:, kk, cols], start=False, stop=False)
                                e = pe.matmul(dst, hl, w[0][:, kk, cols], start=False, stop=last and kk == 1)
                    e.then_inc(sem["step_used"], 1)

                def body(j, c, i=None, first=False):
                    pe.wait_ge(sem["a_summed"], j + base(ph, "a_summed"))
                    up(c, 0, i)
                    down(c + 1, j - 1, i, first=first)
                    pe.wait_ge(sem["g_summed"], j + base(ph, "g_summed"))
                    up(c + 2, 2, i)

                up(ph.step, 0)
                up(ph.step + 1, 2)
                body(1, ph.step + 2, first=True)
                with pe.Fori(2, PAIRS) as j:
                    body(j, ph.step - 1, j)
                down(ph.step + 3 * PAIRS - 1, PAIRS - 1, last=True)

            def proj_f(ph):
                for i in range(ph.n):
                    if i >= 2:
                        pe.wait_ge(sem["group_free"], base(ph, "group_free") + i - 1)
                    c, bank = ph.step + i, 2 * (i % 2)
                    use(c)
                    w = step_parts(c, KD, 2 * P)
                    e = feature_tile(bank, w, 0, xhl)
                    if ph.dest == "kv":
                        for tt in range(TT):
                            e = token_tile(4 + tt, w, lambda u, k: u[:, k, :], xhl, tt)
                    else:
                        e = feature_tile(bank + 1, w, P, xhl)
                    e.then_inc(sem["step_used"], 1)

            def proj_t(ph):
                for c in range(ph.chunks):
                    for i in range(ph.n):
                        m = ph.step + c * ph.n + i
                        use(m)
                        w = step_parts(m, ph.kk, ph.cols)
                        for tt in range(TT):
                            e = token_tile(2 * (c % 2) + tt, w, lambda u, k: u[:, k, :], xhl, tt, k0=i * ph.kk,
                                           first=i == 0, last=i == ph.n - 1)
                        e.then_inc(sem["step_used"], 1)

            def attend(ph):
                job = job_of(ph)
                B = {n: base(ph, n) for n in ("q_staged", "biased", "probs_ready", "pt_ready", "o_done")}
                r = job.rows

                def iteration(t, parity, pair, stages):
                    if 0 in stages:
                        pe.wait_ge(sem["q_staged"], t + (B["q_staged"] + 1))
                        if 2 in stages:
                            pe.wait_ge(sem["biased"], t + (B["biased"] - 1))
                        for qt in range(TT):
                            dst = ps[:, parity, qt * T:(qt + 1) * T]
                            e = pe.matmul(dst, qs[0:r, parity, qt * P:(qt + 1) * P], job.k[0:r, job.key(t), :],
                                          start=True, stop=not job.rotary)
                            if job.rotary:
                                e = pe.matmul(dst, qps[0:C_ROPE, parity, qt * P:(qt + 1) * P], kpe[0:C_ROPE, :],
                                              start=False, stop=True)
                        e.then_inc(sem["scores_ready"], 1)
                    if 1 in stages:
                        pe.wait_ge(sem["probs_ready"], t + B["probs_ready"])
                        if not isinstance(t, int) or t >= 3:
                            pe.wait_ge(sem["pt_ready"], t + (B["pt_ready"] - 2))
                        for kt in range(TT):
                            for qt in range(TT):
                                e = pe.transpose(ps[:, 3 - parity, kt * T + qt * P:kt * T + (qt + 1) * P],
                                                 pr[:, 1 - parity, qt, kt * P:(kt + 1) * P], ident)
                        e.then_inc(sem["transposed"], 1)
                    if 2 in stages:
                        pe.wait_ge(sem["pt_ready"], t + (B["pt_ready"] - 1))
                        if not isinstance(t, int) or t >= 4:
                            pe.wait_ge(sem["o_done"], t + (B["o_done"] - 3))
                        for qt in range(TT):
                            for kt in range(TT):
                                e = pe.matmul(ps[:, 4 + parity, qt * P:qt * P + job.dv],
                                              pt[:, parity, kt, qt * P:(qt + 1) * P],
                                              v[:, kt, bass.ds(job.vcol(t - 2), job.dv)], start=kt == 0,
                                              stop=kt == TT - 1)
                        e.then_inc(sem["pv_ready"], 1)

                pipelined(pe, ph.n, iteration)

            def turn(ph):
                if ph.subln is not None:
                    pe.wait_ge(sem["head_norm"], base(ph, "head_norm") + 6)
                for k in range(ph.n):
                    for tt in range(TT):
                        e = pe.transpose(ps[:, k, tt * P:(tt + 1) * P], o[:, tt, k * P:(k + 1) * P], ident)
                    e.then_inc(sem["tposed"], 1)

            def mla_latent(ph):
                b = base(ph, "xn_ready")
                for k in range(6):
                    pe.wait_ge(sem["xn_ready"], b + 6)
                    rows = P if k < 5 else C_ROPE
                    for tt in range(TT):
                        e = pe.transpose(ps[0:rows, k, tt * P:(tt + 1) * P], latent[:, tt, k * P:k * P + rows], ident)
                    e.then_inc(sem["tposed"], 1)

            def mla_up(ph):
                for i in range(2):
                    use(ph.step + i)
                    w = step_parts(ph.step + i, 3, C_QR)
                    for tt in range(TT):
                        e = token_tile(2 * i + tt, w, lambda u, k: u[:, k, :], chl, tt)
                    e.then_inc(sem["step_used"], 1)
                use(ph.step + 2)
                w = step_parts(ph.step + 2, 2, D)
                for h_ in range(C_HEADS):
                    e = feature_tile(4 + h_, w, 2 * P * h_, chl, k0=3)
                    if h_ % 2:
                        e.then_inc(sem["group_ready"], 1)
                pe.wait_ge(sem["qv_stored"], base(ph, "qv_stored") + 1)
                for tt in range(TT):
                    e = token_tile(tt, w, lambda u, k: u[:, k, :].rearrange("p (h c) -> p h c", h=C_HEADS)[:, :, P:2 * P],
                                   chl, tt, k0=3)
                e.then_inc(sem["step_used"], 1)
                pe.wait_ge(sem["qv_stored"], base(ph, "qv_stored") + 3)
                pe.wait_ge(sem["k_stored"], base(ph, "k_stored") + 2)
                pe.wait_ge(sem["rope_done"], base(ph, "rope_done") + 4)
                heads = qtok.rearrange("p t (h c) -> p t h c", h=C_HEADS)
                for n in range(8):
                    h_, rows, at = n % 4, (P if n < 4 else C_ROPE), (0 if n < 4 else C_NOPE)
                    for tt in range(TT):
                        e = pe.transpose(ps[0:rows, n, tt * P:(tt + 1) * P], heads[:, tt, h_, at:at + rows], ident)
                    e.then_inc(sem["tposed"], 1)

            def gates_(ph):
                gf = base(ph, "group_free")
                with pe.Fori(0, 4) as grp:
                    for m in range(6):
                        n, part = m // 2, m % 2
                        pe.wait_ge(sem["group_free"], 6 * grp + (gf + m - 1))
                        c = ph.step + m
                        use(c, grp, 6)
                        w = step_parts(c, KD if part == 0 else 4, 2 * P)
                        src, k0 = (xhl, 0) if part == 0 else (br1, 4 * n)
                        feature_tile(2 * part, w, 0, src, k0=k0)
                        feature_tile(2 * part + 1, w, P, src, k0=k0).then_inc(sem["step_used"], 1)

            def wout(ph):
                src = yhl if ph.src == "y" else br2
                for i in range(4):
                    use(ph.step + i)
                    w = step_parts(ph.step + i, 2, D)
                    for tt in range(TT):
                        for half in range(2):
                            e = token_tile(4 + 2 * tt + half, w,
                                           lambda u, k: u[:, k, 512 * half:512 * half + 512], src, tt, k0=2 * i,
                                           first=i == 0, last=i == 3)
                    e.then_inc(sem["step_used"], 1)

            def compress(ph):
                for w_ in range(2):
                    pe.wait_ge(sem["blk_made"], base(ph, "blk_made") + w_ + 1)
                    for i in range(2):
                        c = ph.step + 2 * w_ + i
                        use(c)
                        w = step_parts(c, KD, CMP_HID)
                        for tile in range(2):
                            e = feature_tile(2 * w_ + tile, w, tile * P, blk[:, w_, :, :], k0=KD * i, first=i == 0,
                                             last=i == 1)
                        e.then_inc(sem["step_used"], 1)
                cw2 = prm[:, PRM["cw2"]:PRM["cw2"] + 4 * DH].rearrange("p (w k d) -> p w k d", w=2, k=2)
                pe.wait_ge(sem["gelu_done"], base(ph, "gelu_done") + 2)
                for k in range(2):
                    pe.matmul(ps[0:DH, 4, 0:NBLK], cw2[:, 0, k, :], chid[:, 0, k, :], start=k == 0, stop=k == 1)
                for g in range(KVG):
                    for k in range(2):
                        e = pe.matmul(ps[0:NCMP, 5, g * DH:(g + 1) * DH], chid[:, 1, k, g * NCMP:(g + 1) * NCMP],
                                      cw2[:, 1, k, :], start=k == 0, stop=k == 1)
                e.then_inc(sem["cmp_ready"], 1)

            def cmp_attend(ph):
                for qt in range(TT):
                    for h_ in range(HEADS):
                        g = h_ // (HEADS // KVG)
                        at = (qt * HEADS + h_) * NCMP
                        e = pe.matmul(ps[:, 0, at:at + NCMP], q2[0:DH, h_, qt * P:(qt + 1) * P],
                                      kcb[0:DH, g * NCMP:(g + 1) * NCMP], start=True, stop=True)
                e.then_inc(sem["scores_ready"], 1)
                pe.wait_ge(sem["cmp_step"], base(ph, "cmp_step") + 10)
                for qt in range(TT):
                    for g in range(KVG):
                        tile = pcmp[:, qt, 4 * g:4 * g + 4, :].rearrange("p h n -> p (h n)")
                        e = pe.transpose(ps[:, 2 + qt, g * P:(g + 1) * P], tile, ident)
                e.then_inc(sem["transposed"], 1)
                pe.wait_ge(sem["pt_ready"], base(ph, "pt_ready") + 1)
                for qt in range(TT):
                    for g in range(KVG):
                        e = pe.matmul(ps[:, 4 + 2 * qt + g // 2, (g % 2) * T:(g % 2) * T + T],
                                      ptc[:, qt, g * P:(g + 1) * P], vblk[:, g, :], start=True, stop=True)
                e.then_inc(sem["pv_ready"], 1)

            run(pe, "pe", dict(setup=setup, norm=norm, ffn=ffn, proj_f=proj_f, proj_t=proj_t, attend=attend,
                               turn=turn, mla_latent=mla_latent, mla_up=mla_up, gates=gates_, wout=wout,
                               compress=compress, cmp_attend=cmp_attend))


def stream_of(a, n_steps):
    w = np.zeros((n_steps, P, STEP), np.float32)
    at = [0]

    def put(block):
        k = block.shape[0] // P
        w[at[0], :, :k * block.shape[1]] = block.reshape(k, P, -1).transpose(1, 0, 2).reshape(P, -1)
        at[0] += 1

    def ffn(w13, w2):
        up = lambda j, g: w13[:, g * DFF + 2 * P * j:g * DFF + 2 * P * (j + 1)]
        down = lambda j: w2[2 * P * j:2 * P * (j + 1)]
        put(up(0, 0))
        put(up(0, 1))
        for j in range(1, PAIRS):
            put(up(j, 0))
            put(down(j - 1))
            put(up(j, 1))
        put(down(PAIRS - 1))

    def columns(m, c0, n, width=2 * P, kk=None):
        for c in range(n):
            part = m[:, c0 + c * width:c0 + (c + 1) * width]
            rows = m.shape[0] if kk is None else kk * P
            for r in range(0, m.shape[0], rows):
                put(part[r:r + rows])

    def rows(m):
        for r in range(0, D, 2 * P):
            put(m[r:r + 2 * P])

    for l in range(DEPTH1):
        ffn(a["ffn1_w13"][l], a["ffn1_w2"][l])
        m = a["w_in"][l]
        columns(m, 0, 4)
        columns(m, 1024, 1, 512, 4)
        columns(m, 1536, 3)
        columns(m, 2304, 2, C_COLS // 2, 4)
        columns(a["c_w_uq"][l].reshape(C_QR, -1), 0, 2, C_QR)
        put(a["c_w_ukv"][l].reshape(C_KVR, -1))
        for grp in range(4):
            for n in range(3):
                put(a["w_gate"][l][:, n * D + 2 * P * grp:n * D + 2 * P * (grp + 1)])
                put(a["w_branch"][l, n][:, 2 * P * grp:2 * P * (grp + 1)])
        rows(a["w_out"][l])
        ffn(a["ffn2_w13"][l], a["ffn2_w2"][l])
    for i in range(DEPTH2):
        ffn(a["ffn_w_in_2"][i, 0], a["ffn_w_out_2"][i, 0])
        j = i // 3
        if i % 3 == 0:
            columns(a["a_w_in_2"][j], 0, 5)
            rows(a["a_w_out_2"][j])
        elif i % 3 == 1:
            m = a["b_w_in_2"][j]
            columns(m, 0, 6)
            for t in range(2):
                for r in range(2):
                    put(a["b_cmp_w1_2"][j, t][r * D:(r + 1) * D])
            columns(m, 1536, 4)
            put(m[:, 2560:2608])
            rows(a["b_w_out_2"][j])
        else:
            m = a["c_w_in_2"][j]
            columns(m, 0, 8)
            columns(m, 2048, 2, 512, 4)
            rows(a["c_w_out_2"][j])
        ffn(a["ffn_w_in_2"][i, 1], a["ffn_w_out_2"][i, 1])
    return w, at[0]


def params_of(a):
    p = np.zeros((P, PRM_COLS), np.float32)

    def put(name, block):
        p[:block.shape[0], PRM[name]:PRM[name] + block.shape[1]] = block

    by_tile = lambda vector: vector.reshape(-1, P).T
    gains = [a["norm_g_2"][r[1], r[2]] if r[0] == "n2" else a[r[0] + "_norm"][r[1]] for r in GAIN_ROWS]
    put("gain", np.concatenate([by_tile(g) for g in gains], 1))
    put("subln", a["a_subln"].T)
    put("cqn", by_tile(a["c_q_norm"].reshape(-1)))
    put("ckvn", by_tile(a["c_kv_norm"].reshape(-1)))
    put("bgate", by_tile(a["b_gate"].reshape(-1)))
    put("sink1", np.broadcast_to(a["b_sinks"].reshape(1, -1), (P, DEPTH1 * B_HEADS)))
    put("sink2", np.broadcast_to(a["a_sinks_2"].reshape(1, -1), (P, 2 * HEADS)))
    put("lam", np.broadcast_to(a["a_lambda"].reshape(1, -1), (P, DEPTH1 * 4 * DH)))
    put("pos", a["b_cmp_pos_2"][0].reshape(2, LP, P).transpose(2, 0, 1).reshape(P, -1))
    put("cw2", a["b_cmp_w2_2"][0].reshape(2, 2, P, DH).transpose(2, 0, 1, 3).reshape(P, -1))
    put("table", np.concatenate([a["rel_bias_2"], np.full((1, HEADS), NEG, np.float32)], 0))
    return p


def constants():
    c = np.zeros((P, CST_COLS), np.float32)

    def put(name, block):
        c[:block.shape[0], CST[name]:CST[name] + block.shape[1]] = block

    put("ident", np.eye(P, dtype=np.float32))
    freq = (10000.0 ** (-np.arange(0, C_ROPE, 2, dtype=np.float32) / C_ROPE)).astype(np.float32)
    ang = np.arange(T, dtype=np.float32)[:, None] * freq[None, :]
    by_token = lambda m: m.reshape(TT, P, -1).transpose(1, 0, 2).reshape(P, -1)
    put("cos", by_token(np.cos(ang)))
    put("sin", by_token(np.sin(ang)))
    ok = (np.arange(NCMP)[None, :] * CMP_STRIDE + CMP_LEN - 1 <= np.arange(T)[:, None]).astype(np.float32)
    put("cmpok", by_token(ok))
    put("cmpneg", by_token((1 - ok) * np.float32(NEG)))
    d = T - 1 - np.arange(VEC)
    exact = BUCKETS // 2
    safe = np.maximum(d, 1).astype(np.float32)
    log_b = exact + (np.log(safe / exact) / np.float32(np.log(BUCKET_MAX / exact)) * (BUCKETS - exact)).astype(np.int32)
    bucket = np.where(d < exact, np.maximum(d, 0), np.minimum(log_b, BUCKETS - 1))
    hot = np.zeros((2, BUCKETS + 1, VEC), np.float32)
    for w, reach in enumerate((T, P)):
        row = np.where((d >= 0) & (d < reach), bucket, BUCKETS)
        hot[w, row, np.arange(VEC)] = 1.0
    put("onehot", hot.transpose(1, 0, 2).reshape(BUCKETS + 1, -1))
    q, k = np.arange(T)[:, None], np.arange(T)[None, :]
    dist = np.abs(q - k).astype(np.float32)
    slope = lambda n: 2.0 ** (-8.0 * np.arange(1, n + 1, dtype=np.float32) / n)
    fixed = np.zeros((NBIAS1, T, T), np.float32)
    fixed[:A_HEADS] = -slope(A_HEADS)[:, None, None] * dist
    fixed[A_HEADS:A_HEADS + B_HEADS] = np.where(dist <= 128, -slope(B_HEADS)[:, None, None] * dist, np.float32(NEG))
    return c, np.ascontiguousarray(fixed.reshape(NBIAS1, TT, P, T).transpose(0, 2, 1, 3))


def kernel(**inputs):
    import concourse.bacc as bacc
    from concourse.bass_utils import run_bass_kernel_spmd

    a = {name: np.asarray(value) for name, value in inputs.items()}
    steps = plan()[2] + 2
    steps += -steps % RING
    stream, used = stream_of(a, steps)
    cst, fixed = constants()
    post = np.concatenate([a["norm_g_2"][:, 1::2].reshape(-1, D), a["final_norm"].reshape(1, D)], 0)
    arrays = {
        "stream": stream,
        "params": params_of(a),
        "constants": cst,
        "fixed_bias": fixed,
        "post_gains": np.ascontiguousarray(post),
        "x_tokens": np.ascontiguousarray(a["x"].reshape(TT, P, D).transpose(1, 0, 2)),
    }
    nc = bacc.Bacc("TRN2", target_bir_lowering=False, num_devices=1)
    args = [nc.dram_tensor(n, v.shape, F32, kind="ExternalInput").ap() for n, v in arrays.items()]
    out = nc.dram_tensor("y_tokens", (P, TT, D), F32, kind="ExternalOutput").ap()
    transformer_stacks(nc, *args, out)
    result = run_bass_kernel_spmd(nc, [arrays], core_ids=[0]).results[0]["y_tokens"]
    return np.asarray(result).transpose(1, 0, 2).reshape(1, T, D)
```

```python
from contextlib import ExitStack
from dataclasses import dataclass
from typing import Any

import numpy as np
import concourse.bass as bass
from concourse import mybir

F32 = mybir.dt.float32
F32R = mybir.dt.float32r
ALU = mybir.AluOpType
ACT = mybir.ActivationFunctionType
AX = mybir.AxisListType

P = 128
D = 1024
T = 256
TT = T // P
KD = D // P
DFF = 2816
PAIRS = DFF // (2 * P)
STEP = 2048
RING = 3
EPS = 1e-6
NEG = -1e30
TINY = 1e-30
DEPTH1, DEPTH2 = 2, 4
A_HEADS, B_HEADS, C_HEADS = 4, 8, 4
C_QR, C_KVR, C_NOPE, C_ROPE = 384, 256, 128, 64
C_COLS = C_QR + C_KVR + C_ROPE
HEADS = 16
DH = 64
KVG = 4
BUCKETS, BUCKET_MAX = 32, 1024
CMP_LEN, CMP_STRIDE, CMP_HID = 32, 16, 256
NCMP = (T - CMP_LEN) // CMP_STRIDE + 1
NBLK = KVG * NCMP
LP = CMP_LEN // 2
SINK = T
NBIAS1 = A_HEADS + B_HEADS + 1
VEC = 512
LAM0 = [0.8 - 0.6 * float(np.exp(-0.3 * l)) for l in range(DEPTH1)]

PRM = {}
_at = 0
for _name, _n in (("subln", DEPTH1), ("cqn", DEPTH1 * 3), ("ckvn", DEPTH1 * 2),
                  ("bgate", DEPTH1 * 24), ("sink1", DEPTH1 * B_HEADS), ("sink2", 2 * HEADS),
                  ("lam", DEPTH1 * 4 * DH), ("pos", 2 * LP), ("cw2", 2 * 2 * DH), ("table", HEADS)):
    PRM[_name] = _at
    _at += _n
PRM_COLS = _at
CST = {}
_at = 0
for _name, _n in (("ident", P), ("cos", TT * 32), ("sin", TT * 32), ("cmpneg", TT * NCMP), ("cmpok", TT * NCMP),
                  ("onehot", 2 * VEC)):
    CST[_name] = _at
    _at += _n
CST_COLS = _at


@dataclass
class Phase:
    kind: str
    engines: tuple
    before: dict
    base: dict
    step: int
    stack: int
    after: str = ""
    factor: float = 1.0
    final: bool = False
    pre: bool = False
    gains: int = 0
    dest: str = ""
    n: int = 0
    job: str = ""
    bias: str = ""
    bias0: int = 0
    layer: int = 0
    sink: Any = None
    groups: Any = None
    k0: int = 0
    subln: Any = None
    src: str = ""


@dataclass
class Group:
    dest: str
    number: Any
    steps: int
    kk: int
    cols: int
    to: int


@dataclass
class Job:
    q: Any
    k: Any
    rows: int
    dv: int
    rotary: bool
    scale: float
    sink: Any
    bias_row: Any
    key: Any
    vcol: Any
    ocol: Any


def plan():
    phases, count, steps, gain_rows = [], {}, 0, []

    def add(kind, engines, steps_used=0, up=None, **args):
        nonlocal steps
        before = {e: count.get(e + "_phase", 0) for e in ("pe", "act", "dve", "pool")}
        phases.append(Phase(kind=kind, engines=engines, before=before, base=dict(count), step=steps,
                                      stack=2 if any(p.final for p in phases) else 1, **args))
        for name, n in (up or {}).items():
            count[name] = count.get(name, 0) + n
        for e in engines:
            count[e + "_phase"] = count.get(e + "_phase", 0) + 1
        steps += steps_used

    def between(pre=None, after="", factor=1.0, post=None, final=False):
        rounds = (after == "post") + final + (pre is not None)
        engines = ("pe", "act", "dve", "pool") if pre is not None else ("act", "dve", "pool")
        add("between", engines, after=after, factor=factor, final=final, pre=pre is not None,
            gains=len(gain_rows),
            up=dict(sq_ready=2 * rounds, ms_ready=2 * rounds, rstd_ready=2 * rounds,
                    y_ready=2 if after == "post" else 0, x_ready=(2 if after else 0) + (2 if final else 0),
                    xn_ready=2 if pre is not None else 0, tposed=4 if pre is not None else 0,
                    hi_made=4 if pre is not None else 0, gains_loaded=16))
        gain_rows.append((post, pre))

    def ffn():
        n = PAIRS
        add("ffn", ("pe", "act", "dve"), 3 * n,
            up=dict(low_a=n, low_g=n, a_summed=n, g_summed=n, silu_ready=n,
                    h_ready=n, hh_ready=n, ht_ready=n, acc_half=1))

    def f(dest, head0, n):
        return [Group(dest, n_, 1, KD, 2 * P, head0 + 4 * n_) for n_ in range(n)]

    def t(dest, col0, cols, kk, n, chunks):
        return [Group(dest, None, n, kk, cols, col0 + c * cols) for c in range(chunks)]

    def project(*parts):
        groups = [g for part in parts for g in part]
        n_f = sum(g.number is not None for g in groups)
        add("project", ("pe", "act", "dve"), sum(g.steps for g in groups), groups=groups,
            up=dict(low_copied=n_f, group_free=n_f, stored_tokens=len(groups) - n_f))

    def attend(kind, n, bias, bias0, **a):
        extra = {"diff": dict(rs_ready=n // 2), "nsa_slc": dict(rs_ready=n), "nsa_win": dict(rs_ready=n)}.get(kind, {})
        add("attend", ("pe", "act", "dve", "pool"), job=kind, n=n, bias=bias, bias0=bias0, **a,
            up=dict(q_staged=n, scores_ready=n, biased=n, max_ready=n, probs_ready=n, transposed=n, pt_ready=n,
                    recip_ready=n, pv_ready=n, o_done=n, bias_even=n // 2 * 16, bias_odd=n // 2 * 16, **extra))

    def turn(k0, n, subln=None):
        add("turn", ("pe", "act", "dve"), k0=k0, n=n, subln=subln,
            up=dict(tposed=n, hi_made=n, head_norm=0 if subln is None else 6))

    def wout(src):
        add("wout", ("pe", "act", "dve"), 4, src=src, up=dict(acc_half=1))

    add("setup", ("pe", "act", "dve"), up=dict(vec_made=2, vec_copied=2, lam_sum=1, lam_exp=1, lam_sub=2,
                                                       lam_mul=1))
    for l in range(DEPTH1):
        if l == 0:
            between(pre=("ffn1", l))
        else:
            between(pre=("ffn1", l), after="plain", factor=0.5)
        ffn()
        between(pre=("mix", l), after="plain", factor=0.5)
        project(f("q", 0, 2), f("k", 0, 2), t("v", 0, 512, 4, 2, 1))
        attend("diff", 8, "fixed", 0, layer=l)
        turn(0, 4, subln=l)
        project(f("q", 0, 2), f("kv", 0, 1))
        attend("gqa1", 8, "fixed", A_HEADS, sink=PRM["sink1"] + l * B_HEADS)
        turn(4, 4)
        project(t("c", 0, C_COLS // 2, 4, 2, 2))
        add("mla_latent", ("pe", "act", "dve"), layer=l,
            up=dict(sumsq=4, std_ready=2, rstd_ready=1, xn_ready=6, tposed=6, hi_made=5))
        add("mla_up", ("pe", "act", "dve"), 3, layer=l,
            up=dict(group_ready=2, low_copied=2, qv_stored=3, k_stored=2, rope_done=4, tposed=8))
        attend("mla", 4, "fixed", NBIAS1 - 1)
        turn(8, 4)
        add("gates", ("pe", "act", "dve"), 24, layer=l,
            up=dict(low_copied=24, group_free=24, gate_ready=12, y_ready=12, y_part=8, hh_ready=4,
                    prod_ready=8))
        wout("y")
        between(pre=("ffn2", l), after="plain")
        ffn()
    for i in range(DEPTH2):
        if i == 0:
            between(pre=("n2", i, 0), after="plain", factor=0.5, final=True, post=("final",))
        else:
            between(pre=("n2", i, 0), after="post", factor=0.5, post=("n2", i - 1, 5))
        ffn()
        between(pre=("n2", i, 2), after="post", factor=0.5, post=("n2", i, 1))
        if i % 3 == 0:
            project(f("q", 0, 4), f("kv", 0, 1))
            attend("gqa2", HEADS, "window", 0, sink=PRM["sink2"] + (i // 3) * HEADS)
        elif i % 3 == 1:
            project(f("q", 0, 4), f("cmp", 0, 2))
            add("compress", ("pe", "act", "dve"), 4,
                up=dict(blk_added=2, blk_hi=2, blk_made=2, low_copied=2, group_free=2, gelu_done=2,
                        cmp_ready=1))
            project(f("k", 0, 1), t("v", 0, 256, 8, 1, 1), f("k", 4, 1), t("v", 256, 256, 8, 1, 1),
                    t("gate", 0, 48, 8, 1, 1))
            add("cmp_attend", ("pe", "act", "dve"),
                up=dict(scores_ready=1, cmp_step=10, max_ready=1, probs_ready=1, transposed=1, pt_ready=1,
                        pv_ready=1))
            attend("nsa_slc", HEADS, "causal", 0)
            attend("nsa_win", HEADS, "causal", 0)
        else:
            project(f("q", 0, 4), f("k", 0, 4), t("v", 0, 512, 4, 2, 2))
            attend("moba", HEADS, "causal", 0)
        turn(0, 8)
        wout("o")
        between(pre=("n2", i, 4), after="post", post=("n2", i, 3))
        ffn()
    between(after="post", factor=0.5, post=("n2", DEPTH2 - 1, 5))
    add("store", ("act",))
    return phases, count, steps, gain_rows


def transformer_stacks(nc, stream, prm_in, cst_in, fixed_bias, gains_in, x_in, out, limit=None):
    phases, totals, n_steps, gain_rows = plan()
    if limit is not None:
        limit_steps = phases[limit].step
        phases = phases[:limit] + [p for p in phases if p.kind == "store"]
        phases[-1].before = phases[-2].before | {
            e: phases[-2].before[e] + (e in phases[-2].engines) for e in phases[-2].before}
        n_steps = limit_steps
    n_gains = sum(p.kind == "between" for p in phases)
    n_steps += 2
    n_steps += -n_steps % RING
    vec = nc.dram_tensor("rel_vectors", [2 * HEADS, VEC], F32, kind="Internal").ap()
    rel_bias = nc.dram_tensor("rel_bias", [2 * HEADS, P, TT, T], F32, kind="Internal").ap()

    with ExitStack() as ctx:
        def sb(name, shape, dt=F32):
            return ctx.enter_context(nc.sbuf_tensor(name, shape, dt))

        def overlay(*regions):
            sizes = [sum(int(np.prod(shape[1:])) for _, shape, _ in region) for region in regions]
            assert sizes[-1] == max(sizes)
            made = []
            for n, region in enumerate(regions):
                if n == len(regions) - 1:
                    made += [sb(*t) for t in region]
                    continue
                with ExitStack() as part:
                    made += [part.enter_context(nc.sbuf_tensor(*t)) for t in region]
            return made

        raw = sb("raw", [P, RING, STEP])
        whi = sb("whi", [P, RING, STEP], F32R)
        wlo = sb("wlo", [P, RING, STEP], F32R)
        x = sb("x", [P, TT, D])
        xhl = sb("xhl", [P, KD, 2 * T], F32R)
        v = sb("v", [P, TT, D])
        o = sb("o", [P, TT, D])
        prm = sb("prm", [P, PRM_COLS])
        cst = sb("cst", [P, CST_COLS])
        gains = sb("gain", [P, 2, D])
        small = sb("small", [P, 128])
        (yhl, q1, k1, br1, qpe, kpe, br2, q2, k2, blk) = overlay(
            [("yhl", [P, KD, 2 * T], F32R)],
            [("q1", [P, 8, T], F32), ("k1", [P, 8, T], F32), ("br1", [P, 12, 2 * T], F32R),
             ("qpe", [P, C_HEADS, T], F32), ("kpe", [P, T], F32)],
            [("br2", [P, KD, 2 * T], F32R)],
            [("q2", [P, HEADS, T], F32), ("k2", [P, HEADS, T], F32), ("blk", [P, 2, LP, 2 * NBLK], F32R)])
        (pcmp, vblk, kcb, gates, chl) = overlay(
            [("pcmp", [P, TT, HEADS, 32], F32), ("vblk", [P, KVG, T], F32), ("kcb", [P, NBLK], F32),
             ("gates", [P, TT, 48], F32)],
            [("chl", [P, 5, 2 * T], F32R)])
        (ta, a_sum, silu, tg, g_sum, h, ht, tl, cblk, chid, cpre, scmp, bias, s, pr, pt, qs, qps) = overlay(
            [("ta", [P, 2, T], F32), ("a_sum", [P, 2, T], F32), ("silu", [P, 2, T], F32), ("tg", [P, 2, T], F32),
             ("g_sum", [P, 2, T], F32), ("h", [P, 2, T], F32), ("ht", [P, 2, 2, 2, T], F32R)],
            [("tl", [P, 2, 2, T], F32), ("cblk", [P, LP, KVG, NCMP], F32), ("chid", [P, 2, 2, NBLK], F32),
             ("cpre", [P, 2, 2, NBLK], F32), ("scmp", [P, TT, HEADS, NCMP], F32)],
            [("bias", [P, 2, TT, T], F32), ("s", [P, 2, TT, T + 4], F32), ("pr", [P, 2, TT, T + 4], F32),
             ("pt", [P, 2, TT, T], F32), ("qs", [P, 2, T], F32), ("qps", [P, 2, T], F32)])
        latent = o[:, :, 0:C_COLS]
        qtok = o[:, :, 0:C_HEADS * (C_NOPE + C_ROPE)]
        cmp_src = o[:, :, :].rearrange("p w (g t) -> p w g t", g=KVG)
        ps = ctx.enter_context(nc.psum_tensor("ps", [P, 8, 512], F32))
        acc = ps[:, 4:8, :]

        ident = cst[:, CST["ident"]:CST["ident"] + P]
        stat = small[:, 0:8]
        nmax = small[:, 8:12]
        sums = small[:, 12:16]
        rs = small[:, 16:20]
        lam = small[:, 20:22]
        lam_s = small[:, 22:26]
        eps = small[:, 26:27]
        minus_half = small[:, 27:28]
        rstd = small[:, 32:40]

        names = [n for n in totals if not n.endswith("_phase")]
        sem = {n: ctx.enter_context(nc.semaphore(n)) for n in names}
        for n in ("pe_phase", "act_phase", "dve_phase", "pool_phase", "hi_ready", "lo_ready", "step_used",
                  "loaded", "vec_stored", "stored", "bias_stored", "eps_set"):
            sem[n] = ctx.enter_context(nc.semaphore(n))
        raw_ready = [ctx.enter_context(nc.semaphore(f"raw_ready{i}")) for i in range(RING)]
        N_LOADED = 16 * 3
        BIAS_PART = 4
        N_PARTS = 2 * HEADS // BIAS_PART * TT
        N_STORED = 16 * N_PARTS
        FIRST_LOADS = 1 + N_PARTS

        ptc = pt[:, :, :, :].rearrange("p a b c -> p a (b c)")

        def wait(eng, semaphore, value):
            if isinstance(value, int) and value <= 0:
                return
            eng.wait_ge(semaphore, value)

        def enter(eng, me, ph):
            for e in ("pe", "act", "dve", "pool"):
                if e == "pe" and ph.kind == "between":
                    continue
                wait(eng, sem[e + "_phase"], ph.before[e])

        def leave(eng, me):
            eng.drain().then_inc(sem[me + "_phase"], 1)

        def run(eng, me, kinds):
            for ph in phases:
                if me in ph.engines:
                    enter(eng, me, ph)
                    kinds[ph.kind](ph)
                    leave(eng, me)

        def base(ph, name):
            return ph.base.get(name, 0)

        def at_step(c, i, stride):
            return c if i is None else stride * i + c

        def landings(c, i, stride):
            n = c // RING + 1
            return n if i is None else (stride // RING) * i + n

        def spread(ap, axis, n):
            dims = [list(d) for d in ap.ap]
            return bass.AP(ap.tensor, ap.offset, dims[:axis] + [[0, n]] + dims[axis:])

        def pipelined(eng, n, iteration):
            for t in range(4):
                iteration(t, t % 2, t // 2, [d for d in range(3) if t - d >= 0])
            if n > 4:
                with eng.Fori(2, n // 2) as i:
                    for parity in (0, 1):
                        iteration(2 * i + parity, parity, i, [0, 1, 2])
            for t in (n, n + 1):
                iteration(t, t % 2, t // 2, [d for d in (1, 2) if t - d < n])

        def job_of(ph):
            kind = ph.job
            first = kind in ("diff", "gqa1", "mla")
            wide = kind in ("diff", "mla")
            dv = P if wide else DH
            same = lambda t: t
            key, value = {
                "diff": (same, lambda t: t // 2),
                "gqa1": (lambda t: t // 4, lambda t: t // 4),
                "mla": (same, same),
                "gqa2": (lambda t: t // 8, lambda t: t // 8),
                "nsa_slc": (lambda t: t // 4, lambda t: t // 4),
                "nsa_win": (lambda t: t // 4 + KVG, lambda t: t // 4 + KVG),
                "moba": (same, same),
            }[kind]
            row = {"diff": lambda t: t // 2, "mla": lambda t: ph.bias0}.get(kind, lambda t: t + ph.bias0)
            return Job(q=q1 if first else q2, k=k1 if first else k2, rows=C_NOPE if kind == "mla" else DH, dv=dv,
                       rotary=kind == "mla", scale=(C_NOPE + C_ROPE if kind == "mla" else DH) ** -0.5, sink=ph.sink,
                       bias_row=row, key=key, vcol=lambda t: value(t) * dv,
                       ocol=lambda t: (t // 2 if kind == "diff" else t) * dv)

        def accumulated(eng, ph, tt):
            if tt == 0:
                eng.wait_ge(sem["acc_half"], base(ph, "acc_half"))
            else:
                eng.wait_ge(sem["step_used"], ph.step)

        def halves(ap):
            return ap.rearrange("p (a b) -> p a b", a=2)

        def numbered(ph):
            step, before = ph.step, [0, 0]
            for n, g in enumerate(ph.groups):
                form = int(g.number is None)
                yield g, step, 2 * (n % 2), before[form]
                step += g.steps
                before[form] += 1

        def mixed(ph):
            return br1 if ph.stack == 1 else br2

        block = ctx.enter_context(nc.Block())

        @block.sync
        def _(sp):
            sp.dma_start(raw[:, 0, :], stream[0]).then_inc(raw_ready[0], 16)
            sp.dma_start(raw[:, 1, :], stream[1]).then_inc(raw_ready[1], 16)
            sp.dma_start(raw[:, 2, :], stream[2]).then_inc(raw_ready[2], 16)
            for i in range(1, FIRST_LOADS):
                for slot in range(RING):
                    sp.wait_ge(sem["lo_ready"], RING * i + (slot - RING + 1))
                    sp.dma_start(raw[:, slot, :], stream[RING * i + slot]).then_inc(raw_ready[slot], 16)
                if i == 1:
                    sp.wait_ge(sem["vec_stored"], 16)
                qt, h0 = (i - 1) % TT, (i - 1) // TT * BIAS_PART
                src = bass.AP(vec.tensor, h0 * VEC + T - 1 - qt * P, [[VEC, BIAS_PART], [-1, P], [1, T]])
                sp.dma_start(rel_bias[h0:h0 + BIAS_PART, :, qt, :], src).then_inc(sem["bias_stored"], 16)
            with sp.Fori(FIRST_LOADS, n_steps // RING) as i:
                for slot in range(RING):
                    sp.wait_ge(sem["lo_ready"], RING * i + (slot - RING + 1))
                    sp.dma_start(raw[:, slot, :], stream[RING * i + slot]).then_inc(raw_ready[slot], 16)
            sp.wait_ge(sem["bias_stored"], N_STORED)
            for slot in range(RING):
                sp.wait_ge(raw_ready[slot], n_steps // RING * 16)

        @block.gpsimd
        def _(pool):

            def between(ph):
                rounds = ([ph.factor] if ph.after == "post" else []) + [1.0] * (ph.final + ph.pre)
                for r, factor in enumerate(rounds):
                    for tt in range(TT):
                        n = 2 * r + tt
                        ms = stat[:, n:n + 1]
                        pool.wait_ge(sem["sq_ready"], base(ph, "sq_ready") + n + 1)
                        pool.tensor_scalar(ms, ms, EPS, factor ** -2.0, ALU.add, ALU.mult)\
                            .then_inc(sem["ms_ready"], 1)
                        pool.wait_ge(sem["ms_ready"], base(ph, "ms_ready") + n + 1)
                        pool.tensor_tensor(rstd[:, n:n + 1], ms, minus_half, ALU.pow).then_inc(sem["rstd_ready"], 1)
            def attend(ph):
                job = job_of(ph)
                table = fixed_bias if ph.bias == "fixed" else rel_bias
                row0 = HEADS if ph.bias == "window" else 0
                loaded = (sem["bias_even"], sem["bias_odd"])
                if ph.bias != "fixed":
                    pool.wait_ge(sem["bias_stored"], N_STORED)

                def stage(t, parity):
                    if not isinstance(t, int) or t >= 2:
                        pool.wait_ge(sem["scores_ready"], t + (base(ph, "scores_ready") - 1))
                    r = job.rows
                    if job.rotary:
                        pool.tensor_copy(qps[0:C_ROPE, parity, :], qpe[0:C_ROPE, t, :])
                    pool.tensor_copy(qs[0:r, parity, :], job.q[0:r, t, :]).then_inc(sem["q_staged"], 1)
                    if not isinstance(t, int) or t >= 2:
                        pool.wait_ge(sem["biased"], t + (base(ph, "biased") - 1))
                    pool.dma_start(bias[:, parity, :, :], table[job.bias_row(t) + row0]).then_inc(loaded[parity], 16)

                stage(0, 0)
                stage(1, 1)
                with pool.Fori(1, ph.n // 2) as i:
                    for parity in (0, 1):
                        stage(2 * i + parity, parity)

            run(pool, "pool", dict(between=between, attend=attend))

        @block.scalar
        def _(act):
            def split(c, i=None, stride=0):
                slot = c % RING
                act.wait_ge(raw_ready[slot], 16 * landings(c, i, stride))
                wait(act, sem["step_used"], at_step(c - (RING - 1), i, stride))
                nc.scalar.copy(whi[:, slot, :], raw[:, slot, :]).then_inc(sem["hi_ready"], 1)

            def ahead(ph, k):
                split(ph.step + k + 2)

            def multiplied(c, i=None, stride=0):
                act.wait_ge(sem["step_used"], at_step(c + 1, i, stride))

            def load_gains(n):
                row = gains_in[n].rearrange("a n -> (a n)")
                act.dma_start(gains[:, :, :].rearrange("p a n -> p (a n)"),
                              row.partition_broadcast(P)).then_inc(sem["gains_loaded"], 16)

            def setup(ph):
                act.dma_start(x[:, :, :], x_in).then_inc(sem["loaded"], 16)
                act.dma_start(prm[:, :], prm_in).then_inc(sem["loaded"], 16)
                act.dma_start(cst[:, :], cst_in).then_inc(sem["loaded"], 16)
                load_gains(0)
                act.wait_ge(sem["lam_sum"], 1)
                nc.scalar.activation(lam_s, lam_s, ACT.Exp).then_inc(sem["lam_exp"], 1)
                act.wait_ge(sem["vec_copied"], 2)
                act.dma_start(vec.rearrange("(w h) n -> h w n", w=2),
                              o[0:HEADS, :, 0:VEC]).then_inc(sem["vec_stored"], 16)
                split(0)
                split(1)

            def between(ph):
                def mean_square(n, tt, src):
                    junk = v[:, tt, :] if len(src.shape) == 2 else halves(v[:, tt, :])
                    nc.scalar.activation(junk, src, ACT.Square, scale=D ** -0.5,
                                         accum_out=stat[:, n:n + 1]).then_inc(sem["sq_ready"], 1)

                n = 0
                if ph.after == "post":
                    for tt in range(TT):
                        accumulated(act, ph, tt)
                        mean_square(n + tt, tt, acc[:, 2 * tt:2 * tt + 2, :])
                    n += 2
                done = base(ph, "x_ready") + (2 if ph.after else 0)
                for _ in range(ph.final + ph.pre):
                    for tt in range(TT):
                        wait(act, sem["x_ready"], done - 1 + tt)
                        mean_square(n + tt, tt, x[:, tt, :])
                    n += 2
                    done += 2
                if ph.pre:
                    for n in range(4):
                        tt, k0 = n // 2, 4 * (n % 2)
                        act.wait_ge(sem["tposed"], base(ph, "tposed") + n + 1)
                        nc.scalar.copy(xhl[:, k0:k0 + 4, tt * P:(tt + 1) * P],
                                       ps[:, n, :].rearrange("p (k q) -> p k q", k=4)).then_inc(sem["hi_made"], 1)
                if ph.gains + 1 < n_gains:
                    load_gains(ph.gains + 1)

            def ffn(ph):
                def half_a(j):
                    nc.scalar.copy(ta[:, :, :], ps[:, 0:2, 0:T]).then_inc(sem["low_a"], 1)
                    act.wait_ge(sem["a_summed"], j + (base(ph, "a_summed") + 1))
                    nc.scalar.activation(silu[:, :, :], a_sum[:, :, :], ACT.Silu).then_inc(sem["silu_ready"], 1)

                def half_g(j, buffer=0):
                    nc.scalar.copy(tg[:, :, :], ps[:, 2:4, 0:T]).then_inc(sem["low_g"], 1)
                    act.wait_ge(sem["h_ready"], j + (base(ph, "h_ready") + 1))
                    nc.scalar.copy(ht[:, buffer, :, 0, :], h[:, :, :]).then_inc(sem["hh_ready"], 1)

                end = ph.step + 3 * PAIRS
                split(ph.step + 2)
                multiplied(ph.step)
                half_a(0)
                split(ph.step + 3)
                multiplied(ph.step + 1)
                half_g(0)
                with act.Fori(1, PAIRS - 1) as j:
                    split(ph.step + 1, j, 3)
                    multiplied(ph.step - 1, j, 3)
                    half_a(j)
                    split(ph.step + 2, j, 3)
                    split(ph.step + 3, j, 3)
                    multiplied(ph.step + 1, j, 3)
                    half_g(j)
                split(end - 2)
                multiplied(end - 4)
                half_a(PAIRS - 1)
                split(end - 1)
                multiplied(end - 3)
                half_g(PAIRS - 1, 1)
                split(end)
                split(end + 1)

            def project(ph):
                token_major = {"v": v, "c": latent, "gate": gates}
                for g, step, bank, n in numbered(ph):
                    for i in range(g.steps):
                        split(step + i + 2)
                    multiplied(step + g.steps - 1)
                    if g.number is None:
                        func = ACT.Sigmoid if g.dest == "gate" else ACT.Copy
                        nc.scalar.activation(token_major[g.dest][:, :, g.to:g.to + g.cols],
                                             ps[:, bank:bank + 2, 0:g.cols], func).then_inc(sem["stored_tokens"], 1)
                        continue
                    wait(act, sem["group_free"], base(ph, "group_free") + n - 1)
                    nt = 1 if g.dest == "kv" else 2
                    nc.scalar.copy(tl[:, n % 2, 0:nt, :], ps[:, bank:bank + nt, 0:T]).then_inc(sem["low_copied"], 1)
                    if g.dest == "kv":
                        nc.scalar.copy(v[:, :, 0:P], ps[:, 4:6, P:T])

            def attend(ph):
                job = job_of(ph)
                width = T + 1 if job.sink is not None else T
                B = {n: base(ph, n) for n in ("max_ready", "transposed", "recip_ready", "pv_ready")}

                def iteration(t, parity, pair, stages):
                    if 0 in stages:
                        act.wait_ge(sem["max_ready"], t + (B["max_ready"] + 1))
                        if 2 in stages:
                            act.wait_ge(sem["transposed"], t + (B["transposed"] - 1))
                            act.wait_ge(sem["recip_ready"], t + (B["recip_ready"] - 1))
                        for qt in range(TT):
                            n = 2 * parity + qt
                            e = nc.scalar.activation(pr[:, parity, qt, 0:width], s[:, parity, qt, 0:width], ACT.Exp,
                                                     bias=nmax[:, n:n + 1], accum_out=sums[:, n:n + 1])
                        e.then_inc(sem["probs_ready"], 1)
                    if 1 in stages:
                        act.wait_ge(sem["transposed"], t + B["transposed"])
                        if not isinstance(t, int) or t >= 3:
                            act.wait_ge(sem["pv_ready"], t + (B["pv_ready"] - 2))
                        nc.scalar.copy(pt[:, 1 - parity, :, :],
                                       ps[:, 3 - parity, :].rearrange("p (k q) -> p k q", k=TT))\
                            .then_inc(sem["pt_ready"], 1)

                pipelined(act, ph.n, iteration)

            def turn(ph):
                for k in range(ph.n):
                    act.wait_ge(sem["tposed"], base(ph, "tposed") + k + 1)
                    dst = mixed(ph)[:, ph.k0 + k, 0:T]
                    if ph.subln is None:
                        nc.scalar.copy(dst, ps[:, k, 0:T]).then_inc(sem["hi_made"], 1)
                    else:
                        g = prm[:, PRM["subln"] + ph.subln:PRM["subln"] + ph.subln + 1]
                        nc.scalar.activation(dst, ps[:, k, 0:T], ACT.Identity, scale=g).then_inc(sem["hi_made"], 1)

            def turn_subln(ph):
                if ph.subln is not None:
                    act.wait_ge(sem["head_norm"], base(ph, "head_norm") + 2)
                    nc.scalar.activation(stat[:, 0:8], stat[:, 0:8], ACT.Sqrt, bias=eps,
                                         scale=1.0 / P).then_inc(sem["head_norm"], 1)
                turn(ph)

            def mla_latent(ph):
                parts = [latent[:, tt, 0:C_QR] for tt in range(TT)] + [latent[:, tt, C_QR:C_QR + C_KVR]
                                                                      for tt in range(TT)]
                for n, part in enumerate(parts):
                    nc.scalar.activation(v[:, n // 2, 512 * (n % 2):512 * (n % 2) + part.free_size()], part,
                                         ACT.Square, accum_out=stat[:, n:n + 1]).then_inc(sem["sumsq"], 1)
                act.wait_ge(sem["sumsq"], base(ph, "sumsq") + 4)
                nc.scalar.activation(stat[:, 0:2], stat[:, 0:2], ACT.Sqrt, bias=eps,
                                     scale=1.0 / C_QR).then_inc(sem["std_ready"], 1)
                nc.scalar.activation(stat[:, 2:4], stat[:, 2:4], ACT.Sqrt, bias=eps,
                                     scale=1.0 / C_KVR).then_inc(sem["std_ready"], 1)
                for k in range(5):
                    at = PRM["cqn"] + ph.layer * 3 + k if k < 3 else PRM["ckvn"] + ph.layer * 2 + k - 3
                    act.wait_ge(sem["tposed"], base(ph, "tposed") + k + 1)
                    nc.scalar.activation(chl[:, k, 0:T], ps[:, k, 0:T], ACT.Identity,
                                         scale=prm[:, at:at + 1]).then_inc(sem["hi_made"], 1)

            def mla_up(ph):
                gr = base(ph, "group_ready")
                for i in range(2):
                    ahead(ph, i)
                    multiplied(ph.step + i)
                    nc.scalar.copy(qtok[:, :, i * C_QR:(i + 1) * C_QR],
                                   ps[:, 2 * i:2 * i + 2, 0:C_QR]).then_inc(sem["qv_stored"], 1)
                ahead(ph, 2)
                for i in range(2):
                    act.wait_ge(sem["group_ready"], gr + 1 + i)
                    nc.scalar.copy(tl[:, i, :, :], ps[:, 4 + 2 * i:6 + 2 * i, 0:T]).then_inc(sem["low_copied"], 1)
                multiplied(ph.step + 2)
                nc.scalar.copy(v[:, :, 0:512], ps[:, 0:2, :]).then_inc(sem["qv_stored"], 1)

            def gates_(ph):
                gf = base(ph, "group_free")
                with act.Fori(0, 4) as grp:
                    for n in range(3):
                        for part in range(2):
                            m = 2 * n + part
                            split(ph.step + m + 2, grp, 6)
                            multiplied(ph.step + m, grp, 6)
                            if part == 0:
                                dst = ta
                            else:
                                dst = tg
                            nc.scalar.copy(dst[:, :, :], ps[:, 2 * part:2 * part + 2, 0:T]).then_inc(sem["low_copied"], 1)
                            if part == 0:
                                act.wait_ge(sem["group_free"], 6 * grp + (gf + m + 1))
                                for i in range(2):
                                    col = PRM["bgate"] + ph.layer * 24 + n * 8 + i
                                    b = prm[:, bass.ds(2 * grp + col, 1)]
                                    e = nc.scalar.activation(silu[:, i, :], a_sum[:, i, :], ACT.Sigmoid, bias=b)
                                e.then_inc(sem["gate_ready"], 1)
                    act.wait_ge(sem["y_ready"], 3 * grp + (base(ph, "y_ready") + 3))
                    nc.scalar.copy(yhl[:, bass.ds(2 * grp, 2), 0:T], h[:, :, :]).then_inc(sem["hh_ready"], 1)

            def wout(ph):
                for i in range(4):
                    ahead(ph, i)

            def compress(ph):
                for w in range(2):
                    ahead(ph, 2 * w)
                    ahead(ph, 2 * w + 1)
                    multiplied(ph.step + 2 * w + 1)
                    nc.scalar.copy(tl[:, w, :, 0:NBLK], ps[:, 2 * w:2 * w + 2, 0:NBLK]).then_inc(sem["low_copied"], 1)
                    act.wait_ge(sem["group_free"], base(ph, "group_free") + w + 1)
                    nc.scalar.activation(chid[:, w, :, :], cpre[:, w, :, :], ACT.Gelu_apprx_tanh)\
                        .then_inc(sem["gelu_done"], 1)

            def cmp_attend(ph):
                act.wait_ge(sem["max_ready"], base(ph, "max_ready") + 1)
                nc.scalar.activation(scmp[:, :, :, :], scmp[:, :, :, :], ACT.Exp).then_inc(sem["probs_ready"], 1)
                act.wait_ge(sem["transposed"], base(ph, "transposed") + 1)
                nc.scalar.copy(ptc, ps[:, 2:4, :]).then_inc(sem["pt_ready"], 1)

            def store(ph):
                act.dma_start(out, x[:, :, :]).then_inc(sem["stored"], 16)
                act.wait_ge(sem["stored"], 16)

            run(act, "act", dict(setup=setup, between=between, ffn=ffn, project=project, attend=attend, turn=turn_subln, mla_latent=mla_latent,
                                 mla_up=mla_up, gates=gates_, wout=wout, compress=compress, cmp_attend=cmp_attend,
                                 store=store))

        @block.vector
        def _(dve):
            def split(c, i=None, stride=0):
                slot = c % RING
                dve.wait_ge(sem["hi_ready"], at_step(c + 1, i, stride))
                wait(dve, sem["step_used"], at_step(c - (RING - 1), i, stride))
                nc.vector.tensor_tensor(wlo[:, slot, :], raw[:, slot, :], whi[:, slot, :].bitcast(F32),
                                        ALU.subtract).then_inc(sem["lo_ready"], 1)

            def ahead(ph, k):
                split(ph.step + k + 2)

            def setup(ph):
                nc.vector.memset(eps, EPS)
                nc.vector.memset(minus_half, -0.5)
                dve.wait_ge(sem["loaded"], N_LOADED)
                lp = prm[:, PRM["lam"]:PRM["lam"] + DEPTH1 * 4 * DH].rearrange("p (la b d) -> p la b d", b=2, d=DH)
                prod = v[:, 0, 0:4 * DH].rearrange("p (a d) -> p a d", a=4)
                nc.vector.tensor_tensor(prod, lp[:, :, 0, :], lp[:, :, 1, :], ALU.mult).then_inc(sem["lam_mul"], 1)
                dve.wait_ge(sem["lam_mul"], 1)
                nc.vector.tensor_reduce(lam_s, prod, AX.X, ALU.add).then_inc(sem["lam_sum"], 1)
                for w in range(2):
                    dve.wait_ge(sem["vec_made"], w + 1)
                    nc.vector.tensor_copy(o[0:HEADS, w, 0:VEC], ps[0:HEADS, w, :]).then_inc(sem["vec_copied"], 1)
                dve.wait_ge(sem["lam_exp"], 1)
                for l in range(DEPTH1):
                    nc.vector.scalar_tensor_tensor(out=lam[:, l:l + 1], in0=lam_s[:, 2 * l + 1:2 * l + 2],
                                                   scalar=-LAM0[l], in1=lam_s[:, 2 * l:2 * l + 1], op0=ALU.add,
                                                   op1=ALU.subtract).then_inc(sem["lam_sub"], 1)
                split(0)
                split(1)

            def low_parts(ph, n, dst, gain):
                for k in range(n):
                    dve.wait_ge(sem["hi_made"], base(ph, "hi_made") + k + 1)
                    hi = dst[:, k, 0:T].bitcast(F32)
                    g = gain(k)
                    nc.vector.scalar_tensor_tensor(out=dst[:, k, T:2 * T], in0=ps[:, k, 0:T],
                                                   scalar=1.0 if g is None else g, in1=hi, op0=ALU.mult,
                                                   op1=ALU.subtract)

            def between(ph):
                post, pre = gains[:, 0, :], gains[:, 1, :]
                b = {n: base(ph, n) for n in ("sq_ready", "rstd_ready", "y_ready", "gains_loaded")}
                n = 0
                if ph.after == "plain":
                    for tt in range(TT):
                        accumulated(dve, ph, tt)
                        xt = halves(x[:, tt, :])
                        nc.vector.scalar_tensor_tensor(out=xt, in0=acc[:, 2 * tt:2 * tt + 2, :], scalar=ph.factor,
                                                       in1=xt, op0=ALU.mult, op1=ALU.add).then_inc(sem["x_ready"], 1)
                dve.wait_ge(sem["gains_loaded"], b["gains_loaded"] + 16)
                if ph.after == "post":
                    for tt in range(TT):
                        dve.wait_ge(sem["sq_ready"], b["sq_ready"] + tt + 1)
                        nc.vector.tensor_tensor(halves(o[:, tt, :]), acc[:, 2 * tt:2 * tt + 2, :], halves(post),
                                                ALU.mult).then_inc(sem["y_ready"], 1)
                    for tt in range(TT):
                        dve.wait_ge(sem["rstd_ready"], b["rstd_ready"] + tt + 1)
                        dve.wait_ge(sem["y_ready"], b["y_ready"] + tt + 1)
                        nc.vector.scalar_tensor_tensor(out=x[:, tt, :], in0=o[:, tt, :], scalar=rstd[:, tt:tt + 1],
                                                       in1=x[:, tt, :], op0=ALU.mult, op1=ALU.add)\
                            .then_inc(sem["x_ready"], 1)
                    n = 2
                if ph.final:
                    for tt in range(TT):
                        dve.wait_ge(sem["rstd_ready"], b["rstd_ready"] + n + tt + 1)
                        nc.vector.scalar_tensor_tensor(out=x[:, tt, :], in0=x[:, tt, :],
                                                       scalar=rstd[:, n + tt:n + tt + 1], in1=post, op0=ALU.mult,
                                                       op1=ALU.mult).then_inc(sem["x_ready"], 1)
                    n += 2
                if ph.gains == 0:
                    dve.wait_ge(sem["vec_stored"], 16)
                if ph.pre:
                    for tt in range(TT):
                        dve.wait_ge(sem["rstd_ready"], b["rstd_ready"] + n + tt + 1)
                        nc.vector.scalar_tensor_tensor(out=o[:, tt, :], in0=x[:, tt, :],
                                                       scalar=rstd[:, n + tt:n + tt + 1], in1=pre, op0=ALU.mult,
                                                       op1=ALU.mult).then_inc(sem["xn_ready"], 1)
                    for n in range(4):
                        tt, k0 = n // 2, 4 * (n % 2)
                        dve.wait_ge(sem["hi_made"], base(ph, "hi_made") + n + 1)
                        nc.vector.tensor_tensor(xhl[:, k0:k0 + 4, T + tt * P:T + (tt + 1) * P],
                                                ps[:, n, :].rearrange("p (k q) -> p k q", k=4),
                                                xhl[:, k0:k0 + 4, tt * P:(tt + 1) * P].bitcast(F32), ALU.subtract)

            def ffn(ph):
                def half_a(j):
                    dve.wait_ge(sem["low_a"], j + (base(ph, "low_a") + 1))
                    if not isinstance(j, int) or j > 0:
                        dve.wait_ge(sem["silu_ready"], j + base(ph, "silu_ready"))
                    nc.vector.tensor_tensor(a_sum[:, :, :], ps[:, 0:2, T:2 * T], ta[:, :, :], ALU.add)\
                        .then_inc(sem["a_summed"], 1)

                def half_g(j, buffer=0):
                    dve.wait_ge(sem["low_g"], j + (base(ph, "low_g") + 1))
                    nc.vector.tensor_tensor(g_sum[:, :, :], ps[:, 2:4, T:2 * T], tg[:, :, :], ALU.add)\
                        .then_inc(sem["g_summed"], 1)
                    dve.wait_ge(sem["g_summed"], j + (base(ph, "g_summed") + 1))
                    dve.wait_ge(sem["silu_ready"], j + (base(ph, "silu_ready") + 1))
                    if not isinstance(j, int) or j > 0:
                        dve.wait_ge(sem["ht_ready"], j + base(ph, "ht_ready"))
                    nc.vector.tensor_tensor(h[:, :, :], g_sum[:, :, :], silu[:, :, :], ALU.mult)\
                        .then_inc(sem["h_ready"], 1)
                    dve.wait_ge(sem["hh_ready"], j + (base(ph, "hh_ready") + 1))
                    nc.vector.tensor_tensor(ht[:, buffer, :, 1, :], h[:, :, :], ht[:, buffer, :, 0, :].bitcast(F32),
                                            ALU.subtract).then_inc(sem["ht_ready"], 1)

                end = ph.step + 3 * PAIRS
                split(ph.step + 2)
                half_a(0)
                split(ph.step + 3)
                half_g(0)
                with dve.Fori(1, PAIRS - 1) as j:
                    split(ph.step + 1, j, 3)
                    half_a(j)
                    split(ph.step + 2, j, 3)
                    split(ph.step + 3, j, 3)
                    half_g(j)
                split(end - 2)
                half_a(PAIRS - 1)
                split(end - 1)
                half_g(PAIRS - 1, 1)
                split(end)
                split(end + 1)

            def add_heads(dst, head0, bank, low, tiles=2):
                for i in range(tiles):
                    for half in range(2):
                        r = slice(half * DH, half * DH + DH)
                        e = nc.vector.tensor_tensor(dst[0:DH, head0 + 2 * i + half, :], ps[r, bank + i, T:2 * T],
                                                    low[r, i, :], ALU.add)
                return e

            def project(ph):
                q, k = (q1, k1) if ph.stack == 1 else (q2, k2)
                for g, step, bank, n in numbered(ph):
                    for i in range(g.steps):
                        split(step + i + 2)
                    if g.number is None:
                        continue
                    dve.wait_ge(sem["low_copied"], base(ph, "low_copied") + n + 1)
                    low = tl[:, n % 2, :, :]
                    if g.dest == "cmp":
                        for tile in range(2):
                            for half in range(2):
                                r = slice(half * DH, half * DH + DH)
                                to = cmp_src[:, g.number, 2 * tile + half, :]
                                nc.vector.tensor_tensor(to[0:DH, :], ps[r, bank + tile, T:2 * T],
                                                        low[r, tile, :], ALU.add)
                                e = nc.vector.tensor_tensor(to[DH:P, 0:T - 1], ps[r, bank + tile, T + 1:2 * T],
                                                            low[r, tile, 1:T], ALU.add)
                    elif g.dest == "kv":
                        e = add_heads(k, 0, bank, low, tiles=1)
                    else:
                        e = add_heads(q if g.dest == "q" else k, g.to, bank, low)
                    e.then_inc(sem["group_free"], 1)

            def attend(ph):
                job = job_of(ph)
                width = T + 1 if job.sink is not None else T
                loaded = (sem["bias_even"], sem["bias_odd"])
                b_loaded = (base(ph, "bias_even"), base(ph, "bias_odd"))
                B = {n: base(ph, n) for n in ("scores_ready", "biased", "probs_ready", "recip_ready", "rs_ready",
                                              "pv_ready", "o_done")}
                branch = {"nsa_slc": 1, "nsa_win": 2}.get(ph.job)

                def iteration(t, parity, pair, stages):
                    if 0 in stages:
                        if 2 in stages:
                            dve.wait_ge(sem["probs_ready"], t + (B["probs_ready"] - 1))
                        if job.sink is not None:
                            sink = spread(prm[:, bass.ds(t + job.sink, 1)], 1, TT)
                            nc.vector.tensor_copy(s[:, parity, :, SINK:SINK + 1], sink)
                        dve.wait_ge(sem["scores_ready"], t + (B["scores_ready"] + 1))
                        dve.wait_ge(loaded[parity], 16 * pair + (b_loaded[parity] + 16))
                        nc.vector.scalar_tensor_tensor(
                            out=s[:, parity, :, 0:T], in0=ps[:, parity, :].rearrange("p (a b) -> p a b", a=TT),
                            scalar=job.scale, in1=bias[:, parity, :, :], op0=ALU.mult,
                            op1=ALU.add).then_inc(sem["biased"], 1)
                        dve.wait_ge(sem["biased"], t + (B["biased"] + 1))
                        nc.vector.tensor_reduce(nmax[:, 2 * parity:2 * parity + 2], s[:, parity, :, 0:width], AX.X,
                                                ALU.max, negate=True).then_inc(sem["max_ready"], 1)
                    if 1 in stages:
                        r = rs[:, 2 - 2 * parity:4 - 2 * parity]
                        dve.wait_ge(sem["probs_ready"], t + B["probs_ready"])
                        if not isinstance(t, int) or t >= 3:
                            dve.wait_ge(sem["o_done"], t + (B["o_done"] - 2))
                        nc.vector.reciprocal(r, sums[:, 2 - 2 * parity:4 - 2 * parity]).then_inc(sem["recip_ready"], 1)
                        if ph.job == "diff" and parity == 0:
                            dve.wait_ge(sem["recip_ready"], t + B["recip_ready"])
                            nc.vector.tensor_scalar(r, r, lam[:, ph.layer:ph.layer + 1], None,
                                                    ALU.mult).then_inc(sem["rs_ready"], 1)
                        if branch is not None:
                            dve.wait_ge(sem["recip_ready"], t + B["recip_ready"])
                            g = gates[:, :, bass.ds((t - 1) * 3 + branch, 1)]
                            nc.vector.tensor_tensor(r.rearrange("p (a b) -> p a b", b=1),
                                                    r.rearrange("p (a b) -> p a b", b=1), g,
                                                    ALU.mult).then_inc(sem["rs_ready"], 1)
                    if 2 in stages:
                        dve.wait_ge(sem["recip_ready"], t + (B["recip_ready"] - 1))
                        if ph.job == "diff" and parity == 1:
                            dve.wait_ge(sem["rs_ready"], pair + B["rs_ready"])
                        if branch is not None:
                            dve.wait_ge(sem["rs_ready"], t + (B["rs_ready"] - 1))
                        dve.wait_ge(sem["pv_ready"], t + (B["pv_ready"] - 1))
                        add = branch is not None or (ph.job == "diff" and parity == 1)
                        if ph.job == "diff" and parity == 1:
                            dve.wait_ge(sem["o_done"], t + (B["o_done"] - 2))
                        for qt in range(TT):
                            dst = o[:, qt, bass.ds(job.ocol(t - 2), job.dv)]
                            src = ps[:, 4 + parity, qt * P:qt * P + job.dv]
                            r = rs[:, 2 * parity + qt:2 * parity + qt + 1]
                            if add:
                                e = nc.vector.scalar_tensor_tensor(out=dst, in0=src, scalar=r, in1=dst, op0=ALU.mult,
                                                                   op1=ALU.add)
                            else:
                                e = nc.vector.tensor_scalar(dst, src, r, None, ALU.mult)
                        e.then_inc(sem["o_done"], 1)

                pipelined(dve, ph.n, iteration)

            def turn(ph):
                gain = lambda k: None
                if ph.subln is not None:
                    b = base(ph, "head_norm")
                    heads = o[:, :, 0:A_HEADS * P].rearrange("p t (h c) -> p t h c", c=P)
                    sq = v[:, :, 0:A_HEADS * P].rearrange("p t (h c) -> p t h c", c=P)
                    nc.vector.tensor_tensor(sq, heads, heads, ALU.mult).then_inc(sem["head_norm"], 1)
                    dve.wait_ge(sem["head_norm"], b + 1)
                    nc.vector.tensor_reduce(stat.rearrange("p (t h) -> p t h", t=TT), sq, AX.X,
                                            ALU.add).then_inc(sem["head_norm"], 1)
                    dve.wait_ge(sem["head_norm"], b + 3)
                    nc.vector.reciprocal(rstd, stat).then_inc(sem["head_norm"], 1)
                    dve.wait_ge(sem["head_norm"], b + 4)
                    for tt in range(TT):
                        r = spread(rstd[:, tt * A_HEADS:(tt + 1) * A_HEADS], 2, P)
                        nc.vector.scalar_tensor_tensor(out=heads[:, tt], in0=heads[:, tt],
                                                       scalar=1.0 - LAM0[ph.subln], in1=r, op0=ALU.mult,
                                                       op1=ALU.mult).then_inc(sem["head_norm"], 1)
                    gain = lambda k: prm[:, PRM["subln"] + ph.subln:PRM["subln"] + ph.subln + 1]
                low_parts(ph, ph.n, mixed(ph)[:, ph.k0:ph.k0 + ph.n, :], gain)

            def rotate(lo, hi, c, sn, n, tmp, after):
                t1, t2, t3, t4 = tmp
                nc.vector.tensor_tensor(t1, lo, c, ALU.mult)
                nc.vector.tensor_tensor(t2, hi, sn, ALU.mult)
                nc.vector.tensor_tensor(t3, lo, sn, ALU.mult)
                nc.vector.tensor_tensor(t4, hi, c, ALU.mult).then_inc(after[0], 1)
                dve.wait_ge(after[0], after[1] + 1)
                nc.vector.tensor_tensor(lo, t1, t2, ALU.subtract)
                nc.vector.tensor_tensor(hi, t3, t4, ALU.add).then_inc(after[0], 1)

            cos = cst[:, CST["cos"]:CST["cos"] + TT * 32].rearrange("p (t f) -> p t f", t=TT)
            sin = cst[:, CST["sin"]:CST["sin"] + TT * 32].rearrange("p (t f) -> p t f", t=TT)

            def mla_latent(ph):
                b = base(ph, "xn_ready")
                at = C_QR + C_KVR
                tmp = [pr[:, 0, :, 64 * i:64 * i + 32] for i in range(4)]
                rotate(latent[:, :, at:at + 32], latent[:, :, at + 32:at + 64], cos, sin, 1, tmp, (sem["xn_ready"], b))
                dve.wait_ge(sem["std_ready"], base(ph, "std_ready") + 2)
                nc.vector.reciprocal(rstd[:, 0:4], stat[:, 0:4]).then_inc(sem["rstd_ready"], 1)
                dve.wait_ge(sem["rstd_ready"], base(ph, "rstd_ready") + 1)
                for n in range(4):
                    c0, c1 = ((0, C_QR), (C_QR, at))[n // 2]
                    part = latent[:, n % 2, c0:c1]
                    nc.vector.tensor_scalar(part, part, rstd[:, n:n + 1], None, ALU.mult).then_inc(sem["xn_ready"], 1)

                def gain(k):
                    at = PRM["cqn"] + ph.layer * 3 + k if k < 3 else PRM["ckvn"] + ph.layer * 2 + k - 3
                    return prm[:, at:at + 1]

                low_parts(ph, 5, chl, gain)
                dve.wait_ge(sem["tposed"], base(ph, "tposed") + 6)
                nc.vector.tensor_copy(kpe[0:C_ROPE, :], ps[0:C_ROPE, 5, 0:T])

            def mla_up(ph):
                lc = base(ph, "low_copied")
                ahead(ph, 0)
                ahead(ph, 1)
                ahead(ph, 2)
                for i in range(2):
                    dve.wait_ge(sem["low_copied"], lc + i + 1)
                    nc.vector.tensor_tensor(k1[:, 2 * i:2 * i + 2, :], ps[:, 4 + 2 * i:6 + 2 * i, T:2 * T],
                                            tl[:, i, :, :], ALU.add).then_inc(sem["k_stored"], 1)
                dve.wait_ge(sem["qv_stored"], base(ph, "qv_stored") + 2)
                heads = qtok.rearrange("p t (h c) -> p t h c", h=C_HEADS)
                b = base(ph, "rope_done")
                for tt in range(TT):
                    c, sn = spread(cos[:, tt, :], 1, C_HEADS), spread(sin[:, tt, :], 1, C_HEADS)
                    tmp = [pr[:, i // 2, i % 2, 0:128].rearrange("p (h f) -> p h f", f=32) if tt == 0 else
                           s[:, i // 2, i % 2, 0:128].rearrange("p (h f) -> p h f", f=32) for i in range(4)]
                    rotate(heads[:, tt, :, C_NOPE:C_NOPE + 32], heads[:, tt, :, C_NOPE + 32:C_NOPE + 64], c, sn,
                           C_HEADS, tmp, (sem["rope_done"], b + 2 * tt))
                for n in range(8):
                    dve.wait_ge(sem["tposed"], base(ph, "tposed") + n + 1)
                    if n < 4:
                        nc.vector.tensor_copy(q1[:, n, :], ps[:, n, 0:T])
                    else:
                        nc.vector.tensor_copy(qpe[0:C_ROPE, n - 4, :], ps[0:C_ROPE, n, 0:T])

            def gates_(ph):
                with dve.Fori(0, 4) as grp:
                    for n in range(3):
                        for part in range(2):
                            m = 2 * n + part
                            split(ph.step + m + 2, grp, 6)
                            dve.wait_ge(sem["low_copied"], 6 * grp + (base(ph, "low_copied") + m + 1))
                            dst, low = (a_sum, ta) if part == 0 else (g_sum, tg)
                            nc.vector.tensor_tensor(dst[:, :, :], ps[:, 2 * part:2 * part + 2, T:2 * T],
                                                    low[:, :, :], ALU.add).then_inc(sem["group_free"], 1)
                        dve.wait_ge(sem["gate_ready"], 3 * grp + (base(ph, "gate_ready") + n + 1))
                        dve.wait_ge(sem["group_free"], 6 * grp + (base(ph, "group_free") + 2 * n + 2))
                        if n == 0:
                            nc.vector.tensor_tensor(h[:, :, :], g_sum[:, :, :], silu[:, :, :], ALU.mult)\
                                .then_inc(sem["y_ready"], 1)
                        else:
                            nc.vector.tensor_tensor(g_sum[:, :, :], g_sum[:, :, :], silu[:, :, :], ALU.mult)\
                                .then_inc(sem["prod_ready"], 1)
                            dve.wait_ge(sem["prod_ready"], 2 * grp + (base(ph, "prod_ready") + n))
                            dve.wait_ge(sem["y_ready"], 3 * grp + (base(ph, "y_ready") + n))
                            nc.vector.tensor_tensor(h[:, :, :], h[:, :, :], g_sum[:, :, :], ALU.add)\
                                .then_inc(sem["y_ready"], 1)
                    dve.wait_ge(sem["hh_ready"], grp + (base(ph, "hh_ready") + 1))
                    nc.vector.tensor_tensor(yhl[:, bass.ds(2 * grp, 2), T:2 * T], h[:, :, :],
                                            yhl[:, bass.ds(2 * grp, 2), 0:T].bitcast(F32), ALU.subtract)

            def wout(ph):
                for i in range(4):
                    ahead(ph, i)

            def compress(ph):
                for w in range(2):
                    pos = prm[:, PRM["pos"] + w * LP:PRM["pos"] + (w + 1) * LP]
                    wait(dve, sem["blk_made"], base(ph, "blk_made") + w)
                    for g in range(KVG):
                        src = cmp_src[:, w, g, :]
                        blocks = bass.AP(src.tensor, src.offset, [list(src.ap[0]), [2, LP], [CMP_STRIDE, NCMP]])
                        e = nc.vector.tensor_tensor(cblk[:, :, g, :], blocks, spread(pos, 2, NCMP), ALU.add)
                    e.then_inc(sem["blk_added"], 1)
                    dve.wait_ge(sem["blk_added"], base(ph, "blk_added") + w + 1)
                    flat = cblk[:, :, :, :].rearrange("p l g n -> p l (g n)")
                    nc.vector.tensor_copy(blk[:, w, :, 0:NBLK], flat).then_inc(sem["blk_hi"], 1)
                    dve.wait_ge(sem["blk_hi"], base(ph, "blk_hi") + w + 1)
                    nc.vector.tensor_tensor(blk[:, w, :, NBLK:2 * NBLK], flat, blk[:, w, :, 0:NBLK].bitcast(F32),
                                            ALU.subtract).then_inc(sem["blk_made"], 1)
                nc.vector.memset(vblk[:, :, :], 0.0)
                for w in range(2):
                    ahead(ph, 2 * w)
                    ahead(ph, 2 * w + 1)
                    dve.wait_ge(sem["low_copied"], base(ph, "low_copied") + w + 1)
                    nc.vector.tensor_tensor(cpre[:, w, :, :], ps[:, 2 * w:2 * w + 2, NBLK:2 * NBLK],
                                            tl[:, w, :, 0:NBLK], ALU.add).then_inc(sem["group_free"], 1)
                dve.wait_ge(sem["cmp_ready"], base(ph, "cmp_ready") + 1)
                nc.vector.tensor_copy(kcb[0:DH, :], ps[0:DH, 4, 0:NBLK])
                for n in range(4):
                    nc.vector.tensor_copy(vblk[32 * n:32 * n + NCMP, :, n * DH:(n + 1) * DH],
                                          ps[0:NCMP, 5, 0:KVG * DH].rearrange("p (g d) -> p g d", g=KVG))

            def cmp_attend(ph):
                b = base(ph, "cmp_step")
                n = [0]

                def then(e):
                    n[0] += 1
                    e.then_inc(sem["cmp_step"], 1)
                    dve.wait_ge(sem["cmp_step"], b + n[0])

                neg = cst[:, CST["cmpneg"]:CST["cmpneg"] + TT * NCMP].rearrange("p (t n) -> p t n", t=TT)
                ok = cst[:, CST["cmpok"]:CST["cmpok"] + TT * NCMP].rearrange("p (t n) -> p t n", t=TT)
                rows = scmp[:, :, :, :].rearrange("p t h n -> p (t h) n")
                cmax, csum = small[:, 64:96], small[:, 96:128]
                then(nc.vector.memset(pcmp[:, :, :, :], 0.0))
                dve.wait_ge(sem["scores_ready"], base(ph, "scores_ready") + 1)
                then(nc.vector.tensor_scalar(scmp[:, :, :, :].rearrange("p t h n -> p (t h n)"),
                                             ps[:, 0, 0:TT * HEADS * NCMP], DH ** -0.5, None, ALU.mult))
                then(nc.vector.tensor_tensor(scmp[:, :, :, :], scmp[:, :, :, :], spread(neg, 2, HEADS), ALU.add))
                then(nc.vector.tensor_reduce(cmax, rows, AX.X, ALU.max))
                nc.vector.tensor_tensor(rows, rows, spread(cmax, 2, NCMP), ALU.subtract).then_inc(sem["max_ready"], 1)
                dve.wait_ge(sem["probs_ready"], base(ph, "probs_ready") + 1)
                then(nc.vector.tensor_tensor(scmp[:, :, :, :], scmp[:, :, :, :], spread(ok, 2, HEADS), ALU.mult))
                then(nc.vector.tensor_reduce(csum, rows, AX.X, ALU.add))
                then(nc.vector.tensor_scalar(csum, csum, TINY, None, ALU.max))
                then(nc.vector.reciprocal(csum, csum))
                g = gates[:, :, :].rearrange("p t (h b) -> p t h b", b=3)[:, :, :, 0]
                sums3 = csum.rearrange("p (t h) -> p t h", t=TT)
                then(nc.vector.tensor_tensor(sums3, sums3, g, ALU.mult))
                then(nc.vector.tensor_tensor(pcmp[:, :, :, 0:NCMP].rearrange("p t h n -> p (t h) n"), rows,
                                             spread(csum, 2, NCMP), ALU.mult))
                dve.wait_ge(sem["pv_ready"], base(ph, "pv_ready") + 1)
                for tt in range(TT):
                    nc.vector.tensor_copy(o[:, tt, :].rearrange("p (a b) -> p a b", a=2),
                                          ps[:, 4 + 2 * tt:6 + 2 * tt, :])

            run(dve, "dve", dict(setup=setup, between=between, ffn=ffn, project=project, attend=attend, turn=turn, mla_latent=mla_latent, mla_up=mla_up,
                                 gates=gates_, wout=wout, compress=compress, cmp_attend=cmp_attend))

        @block.tensor
        def _(pe):
            def step_parts(c, kk, cols):
                w = [part[:, c % RING, 0:kk * cols].rearrange("p (k n) -> p k n", k=kk) for part in (whi, wlo)]
                return w

            def use(c, i=None, stride=0):
                pe.wait_ge(sem["lo_ready"], at_step(c + 1, i, stride))

            def feature_tile(bank, w, col0, src, k0=0, first=True, last=True):
                hi, lo = w
                n = hi.shape[1]
                half = src.shape[2] // 2
                for k in range(n):
                    wide = lambda: pe.matmul(ps[:, bank, 0:2 * half], hi[:, k, col0:col0 + P], src[:, k0 + k, :],
                                             start=first and k == 0, stop=last and k == n - 1)
                    if k == 0:
                        wide()
                    e = pe.matmul(ps[:, bank, 0:half], lo[:, k, col0:col0 + P], src[:, k0 + k, 0:half],
                                  start=False, stop=False)
                    if k > 0:
                        e = wide()
                return e

            def token_tile(bank, w, cols, src, tt, k0=0, first=True, last=True):
                n = w[0].shape[1]
                for k in range(n):
                    hi, lo = cols(w[0], k), cols(w[1], k)
                    xh = src[:, k0 + k, tt * P:(tt + 1) * P]
                    xl = src[:, k0 + k, T + tt * P:T + (tt + 1) * P]
                    width = hi.free_size()
                    dst = ps[:, bank, 0:width]
                    if len(hi.shape) == 3:
                        dst = dst.rearrange("p (a b) -> p a b", a=hi.shape[1])
                    pe.matmul(dst, xh, hi, start=first and k == 0, stop=False)
                    pe.matmul(dst, xh, lo, start=False, stop=False)
                    e = pe.matmul(dst, xl, hi, start=False, stop=last and k == n - 1)
                return e

            def setup(ph):
                pe.wait_ge(sem["loaded"], N_LOADED)
                table = prm[0:BUCKETS + 1, PRM["table"]:PRM["table"] + HEADS]
                for w in range(2):
                    hot = cst[0:BUCKETS + 1, CST["onehot"] + w * VEC:CST["onehot"] + (w + 1) * VEC]
                    pe.matmul(ps[0:HEADS, w, :], table, hot, start=True, stop=True).then_inc(sem["vec_made"], 1)

            def between(ph):
                for n in range(4):
                    tt, k0 = n // 2, 4 * (n % 2)
                    if k0 == 0:
                        pe.wait_ge(sem["xn_ready"], base(ph, "xn_ready") + tt + 1)
                    for k in range(4):
                        e = pe.transpose(ps[:, n, k * P:(k + 1) * P], o[:, tt, (k0 + k) * P:(k0 + k + 1) * P], ident)
                    e.then_inc(sem["tposed"], 1)

            def ffn(ph):
                def up(c, bank, j=None):
                    use(c, j, 3)
                    w = step_parts(c, KD, 2 * P)
                    feature_tile(bank, w, 0, xhl)
                    feature_tile(bank + 1, w, P, xhl).then_inc(sem["step_used"], 1)

                def down(c, pair, j=None, first=False, last=False):
                    pe.wait_ge(sem["ht_ready"], pair + (base(ph, "ht_ready") + 1))
                    use(c, j, 3)
                    w = step_parts(c, 2, D)
                    order = [(kk, tt) for tt in range(TT) for kk in range(2)] if last else \
                        [(kk, tt) for kk in range(2) for tt in range(TT)]
                    for kk, tt in order:
                        hh, hl = (ht[:, 1 if last else 0, kk, part, tt * P:(tt + 1) * P] for part in (0, 1))
                        for half in range(2):
                            cols = slice(512 * half, 512 * half + 512)
                            dst = acc[:, 2 * tt + half, :]
                            pe.matmul(dst, hh, w[0][:, kk, cols], start=first and kk == 0, stop=False)
                            pe.matmul(dst, hh, w[1][:, kk, cols], start=False, stop=False)
                            e = pe.matmul(dst, hl, w[0][:, kk, cols], start=False, stop=last and kk == 1)
                        if last and (kk, tt) == (1, 0):
                            e.then_inc(sem["acc_half"], 1)
                    e.then_inc(sem["step_used"], 1)

                def body(j, c, i=None, first=False):
                    pe.wait_ge(sem["a_summed"], j + base(ph, "a_summed"))
                    up(c, 0, i)
                    down(c + 1, j - 1, i, first=first)
                    pe.wait_ge(sem["g_summed"], j + base(ph, "g_summed"))
                    up(c + 2, 2, i)

                up(ph.step, 0)
                up(ph.step + 1, 2)
                body(1, ph.step + 2, first=True)
                with pe.Fori(2, PAIRS - 1) as j:
                    body(j, ph.step - 1, j)
                last, end = PAIRS - 1, ph.step + 3 * PAIRS
                pe.wait_ge(sem["a_summed"], last + base(ph, "a_summed"))
                up(end - 4, 0)
                pe.wait_ge(sem["g_summed"], last + base(ph, "g_summed"))
                up(end - 3, 2)
                down(end - 2, last - 1)
                down(end - 1, last, last=True)

            def project(ph):
                emptied = []
                for g, step, bank, n in numbered(ph):
                    if len(emptied) >= 2:
                        name, count = emptied[-2]
                        pe.wait_ge(sem[name], base(ph, name) + count)
                    if g.number is not None:
                        emptied.append(("group_free", n + 1))
                        use(step)
                        w = step_parts(step, KD, 2 * P)
                        e = feature_tile(bank, w, 0, xhl)
                        if g.dest == "kv":
                            for tt in range(TT):
                                e = token_tile(4 + tt, w, lambda u, k: u[:, k, :], xhl, tt)
                        else:
                            e = feature_tile(bank + 1, w, P, xhl)
                        e.then_inc(sem["step_used"], 1)
                        continue
                    emptied.append(("stored_tokens", n + 1))
                    for i in range(g.steps):
                        use(step + i)
                        w = step_parts(step + i, g.kk, g.cols)
                        for tt in range(TT):
                            e = token_tile(bank + tt, w, lambda u, k: u[:, k, :], xhl, tt, k0=i * g.kk,
                                           first=i == 0, last=i == g.steps - 1)
                        e.then_inc(sem["step_used"], 1)

            def attend(ph):
                job = job_of(ph)
                B = {n: base(ph, n) for n in ("q_staged", "biased", "probs_ready", "pt_ready", "o_done")}
                r = job.rows

                def iteration(t, parity, pair, stages):
                    if 0 in stages:
                        pe.wait_ge(sem["q_staged"], t + (B["q_staged"] + 1))
                        if 2 in stages:
                            pe.wait_ge(sem["biased"], t + (B["biased"] - 1))
                        for qt in range(TT):
                            dst = ps[:, parity, qt * T:(qt + 1) * T]
                            e = pe.matmul(dst, qs[0:r, parity, qt * P:(qt + 1) * P], job.k[0:r, job.key(t), :],
                                          start=True, stop=not job.rotary)
                            if job.rotary:
                                e = pe.matmul(dst, qps[0:C_ROPE, parity, qt * P:(qt + 1) * P], kpe[0:C_ROPE, :],
                                              start=False, stop=True)
                        e.then_inc(sem["scores_ready"], 1)
                    if 1 in stages:
                        pe.wait_ge(sem["probs_ready"], t + B["probs_ready"])
                        if not isinstance(t, int) or t >= 3:
                            pe.wait_ge(sem["pt_ready"], t + (B["pt_ready"] - 2))
                        for kt in range(TT):
                            for qt in range(TT):
                                e = pe.transpose(ps[:, 3 - parity, kt * T + qt * P:kt * T + (qt + 1) * P],
                                                 pr[:, 1 - parity, qt, kt * P:(kt + 1) * P], ident)
                        e.then_inc(sem["transposed"], 1)
                    if 2 in stages:
                        pe.wait_ge(sem["pt_ready"], t + (B["pt_ready"] - 1))
                        if not isinstance(t, int) or t >= 4:
                            pe.wait_ge(sem["o_done"], t + (B["o_done"] - 3))
                        for qt in range(TT):
                            for kt in range(TT):
                                e = pe.matmul(ps[:, 4 + parity, qt * P:qt * P + job.dv],
                                              pt[:, parity, kt, qt * P:(qt + 1) * P],
                                              v[:, kt, bass.ds(job.vcol(t - 2), job.dv)], start=kt == 0,
                                              stop=kt == TT - 1)
                        e.then_inc(sem["pv_ready"], 1)

                pipelined(pe, ph.n, iteration)

            def turn(ph):
                if ph.subln is not None:
                    pe.wait_ge(sem["head_norm"], base(ph, "head_norm") + 6)
                for k in range(ph.n):
                    for tt in range(TT):
                        e = pe.transpose(ps[:, k, tt * P:(tt + 1) * P], o[:, tt, k * P:(k + 1) * P], ident)
                    e.then_inc(sem["tposed"], 1)

            def mla_latent(ph):
                b = base(ph, "xn_ready")
                for k in range(6):
                    pe.wait_ge(sem["xn_ready"], b + 6)
                    rows = P if k < 5 else C_ROPE
                    for tt in range(TT):
                        e = pe.transpose(ps[0:rows, k, tt * P:(tt + 1) * P], latent[:, tt, k * P:k * P + rows], ident)
                    e.then_inc(sem["tposed"], 1)

            def mla_up(ph):
                for i in range(2):
                    use(ph.step + i)
                    w = step_parts(ph.step + i, 3, C_QR)
                    for tt in range(TT):
                        e = token_tile(2 * i + tt, w, lambda u, k: u[:, k, :], chl, tt)
                    e.then_inc(sem["step_used"], 1)
                use(ph.step + 2)
                w = step_parts(ph.step + 2, 2, D)
                for h_ in range(C_HEADS):
                    e = feature_tile(4 + h_, w, 2 * P * h_, chl, k0=3)
                    if h_ % 2:
                        e.then_inc(sem["group_ready"], 1)
                pe.wait_ge(sem["qv_stored"], base(ph, "qv_stored") + 1)
                for tt in range(TT):
                    e = token_tile(tt, w, lambda u, k: u[:, k, :].rearrange("p (h c) -> p h c", h=C_HEADS)[:, :, P:2 * P],
                                   chl, tt, k0=3)
                e.then_inc(sem["step_used"], 1)
                pe.wait_ge(sem["qv_stored"], base(ph, "qv_stored") + 3)
                pe.wait_ge(sem["k_stored"], base(ph, "k_stored") + 2)
                pe.wait_ge(sem["rope_done"], base(ph, "rope_done") + 4)
                heads = qtok.rearrange("p t (h c) -> p t h c", h=C_HEADS)
                for n in range(8):
                    h_, rows, at = n % 4, (P if n < 4 else C_ROPE), (0 if n < 4 else C_NOPE)
                    for tt in range(TT):
                        e = pe.transpose(ps[0:rows, n, tt * P:(tt + 1) * P], heads[:, tt, h_, at:at + rows], ident)
                    e.then_inc(sem["tposed"], 1)

            def gates_(ph):
                gf = base(ph, "group_free")
                with pe.Fori(0, 4) as grp:
                    for m in range(6):
                        n, part = m // 2, m % 2
                        pe.wait_ge(sem["group_free"], 6 * grp + (gf + m - 1))
                        c = ph.step + m
                        use(c, grp, 6)
                        w = step_parts(c, KD if part == 0 else 4, 2 * P)
                        src, k0 = (xhl, 0) if part == 0 else (br1, 4 * n)
                        feature_tile(2 * part, w, 0, src, k0=k0)
                        feature_tile(2 * part + 1, w, P, src, k0=k0).then_inc(sem["step_used"], 1)

            def wout(ph):
                src = yhl if ph.src == "y" else br2
                for i in range(4):
                    use(ph.step + i)
                    w = step_parts(ph.step + i, 2, D)
                    for tt in range(TT):
                        for half in range(2):
                            e = token_tile(4 + 2 * tt + half, w,
                                           lambda u, k: u[:, k, 512 * half:512 * half + 512], src, tt, k0=2 * i,
                                           first=i == 0, last=i == 3)
                            if i == 3 and (tt, half) == (0, 1):
                                e.then_inc(sem["acc_half"], 1)
                    e.then_inc(sem["step_used"], 1)

            def compress(ph):
                for w_ in range(2):
                    pe.wait_ge(sem["blk_made"], base(ph, "blk_made") + w_ + 1)
                    for i in range(2):
                        c = ph.step + 2 * w_ + i
                        use(c)
                        w = step_parts(c, KD, CMP_HID)
                        for tile in range(2):
                            e = feature_tile(2 * w_ + tile, w, tile * P, blk[:, w_, :, :], k0=KD * i, first=i == 0,
                                             last=i == 1)
                        e.then_inc(sem["step_used"], 1)
                cw2 = prm[:, PRM["cw2"]:PRM["cw2"] + 4 * DH].rearrange("p (w k d) -> p w k d", w=2, k=2)
                pe.wait_ge(sem["gelu_done"], base(ph, "gelu_done") + 2)
                for k in range(2):
                    pe.matmul(ps[0:DH, 4, 0:NBLK], cw2[:, 0, k, :], chid[:, 0, k, :], start=k == 0, stop=k == 1)
                for g in range(KVG):
                    for k in range(2):
                        e = pe.matmul(ps[0:NCMP, 5, g * DH:(g + 1) * DH], chid[:, 1, k, g * NCMP:(g + 1) * NCMP],
                                      cw2[:, 1, k, :], start=k == 0, stop=k == 1)
                e.then_inc(sem["cmp_ready"], 1)

            def cmp_attend(ph):
                for qt in range(TT):
                    for h_ in range(HEADS):
                        g = h_ // (HEADS // KVG)
                        at = (qt * HEADS + h_) * NCMP
                        e = pe.matmul(ps[:, 0, at:at + NCMP], q2[0:DH, h_, qt * P:(qt + 1) * P],
                                      kcb[0:DH, g * NCMP:(g + 1) * NCMP], start=True, stop=True)
                e.then_inc(sem["scores_ready"], 1)
                pe.wait_ge(sem["cmp_step"], base(ph, "cmp_step") + 10)
                for qt in range(TT):
                    for g in range(KVG):
                        tile = pcmp[:, qt, 4 * g:4 * g + 4, :].rearrange("p h n -> p (h n)")
                        e = pe.transpose(ps[:, 2 + qt, g * P:(g + 1) * P], tile, ident)
                e.then_inc(sem["transposed"], 1)
                pe.wait_ge(sem["pt_ready"], base(ph, "pt_ready") + 1)
                for qt in range(TT):
                    for g in range(KVG):
                        e = pe.matmul(ps[:, 4 + 2 * qt + g // 2, (g % 2) * T:(g % 2) * T + T],
                                      ptc[:, qt, g * P:(g + 1) * P], vblk[:, g, :], start=True, stop=True)
                e.then_inc(sem["pv_ready"], 1)

            run(pe, "pe", dict(setup=setup, between=between, ffn=ffn, project=project, attend=attend,
                               turn=turn, mla_latent=mla_latent, mla_up=mla_up, gates=gates_, wout=wout,
                               compress=compress, cmp_attend=cmp_attend))


def stream_of(a, n_steps):
    w = np.zeros((n_steps, P, STEP), np.float32)
    at = [0]

    def put(block):
        k = block.shape[0] // P
        w[at[0], :, :k * block.shape[1]] = block.reshape(k, P, -1).transpose(1, 0, 2).reshape(P, -1)
        at[0] += 1

    def ffn(w13, w2):
        up = lambda j, g: w13[:, g * DFF + 2 * P * j:g * DFF + 2 * P * (j + 1)]
        down = lambda j: w2[2 * P * j:2 * P * (j + 1)]
        put(up(0, 0))
        put(up(0, 1))
        for j in range(1, PAIRS - 1):
            put(up(j, 0))
            put(down(j - 1))
            put(up(j, 1))
        put(up(PAIRS - 1, 0))
        put(up(PAIRS - 1, 1))
        put(down(PAIRS - 2))
        put(down(PAIRS - 1))

    def columns(m, c0, n, width=2 * P, kk=None):
        for c in range(n):
            part = m[:, c0 + c * width:c0 + (c + 1) * width]
            rows = m.shape[0] if kk is None else kk * P
            for r in range(0, m.shape[0], rows):
                put(part[r:r + rows])

    def rows(m):
        for r in range(0, D, 2 * P):
            put(m[r:r + 2 * P])

    for l in range(DEPTH1):
        ffn(a["ffn1_w13"][l], a["ffn1_w2"][l])
        m = a["w_in"][l]
        columns(m, 0, 4)
        columns(m, 1024, 1, 512, 4)
        columns(m, 1536, 3)
        columns(m, 2304, 2, C_COLS // 2, 4)
        columns(a["c_w_uq"][l].reshape(C_QR, -1), 0, 2, C_QR)
        put(a["c_w_ukv"][l].reshape(C_KVR, -1))
        for grp in range(4):
            for n in range(3):
                put(a["w_gate"][l][:, n * D + 2 * P * grp:n * D + 2 * P * (grp + 1)])
                put(a["w_branch"][l, n][:, 2 * P * grp:2 * P * (grp + 1)])
        rows(a["w_out"][l])
        ffn(a["ffn2_w13"][l], a["ffn2_w2"][l])
    for i in range(DEPTH2):
        ffn(a["ffn_w_in_2"][i, 0], a["ffn_w_out_2"][i, 0])
        j = i // 3
        if i % 3 == 0:
            columns(a["a_w_in_2"][j], 0, 5)
            rows(a["a_w_out_2"][j])
        elif i % 3 == 1:
            m = a["b_w_in_2"][j]
            columns(m, 0, 6)
            for t in range(2):
                for r in range(2):
                    put(a["b_cmp_w1_2"][j, t][r * D:(r + 1) * D])
            columns(m, 1536, 4)
            put(m[:, 2560:2608])
            rows(a["b_w_out_2"][j])
        else:
            m = a["c_w_in_2"][j]
            columns(m, 0, 8)
            columns(m, 2048, 2, 512, 4)
            rows(a["c_w_out_2"][j])
        ffn(a["ffn_w_in_2"][i, 1], a["ffn_w_out_2"][i, 1])
    return w, at[0]


def params_of(a):
    p = np.zeros((P, PRM_COLS), np.float32)

    def put(name, block):
        p[:block.shape[0], PRM[name]:PRM[name] + block.shape[1]] = block

    by_tile = lambda vector: vector.reshape(-1, P).T
    put("subln", a["a_subln"].T)
    put("cqn", by_tile(a["c_q_norm"].reshape(-1)))
    put("ckvn", by_tile(a["c_kv_norm"].reshape(-1)))
    put("bgate", by_tile(a["b_gate"].reshape(-1)))
    put("sink1", np.broadcast_to(a["b_sinks"].reshape(1, -1), (P, DEPTH1 * B_HEADS)))
    put("sink2", np.broadcast_to(a["a_sinks_2"].reshape(1, -1), (P, 2 * HEADS)))
    put("lam", np.broadcast_to(a["a_lambda"].reshape(1, -1), (P, DEPTH1 * 4 * DH)))
    put("pos", a["b_cmp_pos_2"][0].reshape(2, LP, P).transpose(2, 0, 1).reshape(P, -1))
    put("cw2", a["b_cmp_w2_2"][0].reshape(2, 2, P, DH).transpose(2, 0, 1, 3).reshape(P, -1))
    put("table", np.concatenate([a["rel_bias_2"], np.full((1, HEADS), NEG, np.float32)], 0))
    return p


def gains_of(a):
    def row(name):
        if name is None:
            return np.zeros(D, np.float32)
        if name[0] == "final":
            return a["final_norm"].reshape(D)
        return a["norm_g_2"][name[1], name[2]] if name[0] == "n2" else a[name[0] + "_norm"][name[1]]

    return np.stack([np.stack([row(post), row(pre)]) for post, pre in plan()[3]])


def constants():
    c = np.zeros((P, CST_COLS), np.float32)

    def put(name, block):
        c[:block.shape[0], CST[name]:CST[name] + block.shape[1]] = block

    put("ident", np.eye(P, dtype=np.float32))
    freq = (10000.0 ** (-np.arange(0, C_ROPE, 2, dtype=np.float32) / C_ROPE)).astype(np.float32)
    ang = np.arange(T, dtype=np.float32)[:, None] * freq[None, :]
    by_token = lambda m: m.reshape(TT, P, -1).transpose(1, 0, 2).reshape(P, -1)
    put("cos", by_token(np.cos(ang)))
    put("sin", by_token(np.sin(ang)))
    ok = (np.arange(NCMP)[None, :] * CMP_STRIDE + CMP_LEN - 1 <= np.arange(T)[:, None]).astype(np.float32)
    put("cmpok", by_token(ok))
    put("cmpneg", by_token((1 - ok) * np.float32(NEG)))
    d = T - 1 - np.arange(VEC)
    exact = BUCKETS // 2
    safe = np.maximum(d, 1).astype(np.float32)
    log_b = exact + (np.log(safe / exact) / np.float32(np.log(BUCKET_MAX / exact)) * (BUCKETS - exact)).astype(np.int32)
    bucket = np.where(d < exact, np.maximum(d, 0), np.minimum(log_b, BUCKETS - 1))
    hot = np.zeros((2, BUCKETS + 1, VEC), np.float32)
    for w, reach in enumerate((T, P)):
        row = np.where((d >= 0) & (d < reach), bucket, BUCKETS)
        hot[w, row, np.arange(VEC)] = 1.0
    put("onehot", hot.transpose(1, 0, 2).reshape(BUCKETS + 1, -1))
    q, k = np.arange(T)[:, None], np.arange(T)[None, :]
    dist = np.abs(q - k).astype(np.float32)
    slope = lambda n: 2.0 ** (-8.0 * np.arange(1, n + 1, dtype=np.float32) / n)
    fixed = np.zeros((NBIAS1, T, T), np.float32)
    fixed[:A_HEADS] = -slope(A_HEADS)[:, None, None] * dist
    fixed[A_HEADS:A_HEADS + B_HEADS] = np.where(dist <= 128, -slope(B_HEADS)[:, None, None] * dist, np.float32(NEG))
    return c, np.ascontiguousarray(fixed.reshape(NBIAS1, TT, P, T).transpose(0, 2, 1, 3))


def kernel(**inputs):
    import concourse.bacc as bacc
    from concourse.bass_utils import run_bass_kernel_spmd

    a = {name: np.asarray(value) for name, value in inputs.items()}
    steps = plan()[2] + 2
    steps += -steps % RING
    stream, used = stream_of(a, steps)
    cst, fixed = constants()
    arrays = {
        "stream": stream,
        "params": params_of(a),
        "constants": cst,
        "fixed_bias": fixed,
        "gains": gains_of(a),
        "x_tokens": np.ascontiguousarray(a["x"].reshape(TT, P, D).transpose(1, 0, 2)),
    }
    nc = bacc.Bacc("TRN2", target_bir_lowering=False, num_devices=1)
    args = [nc.dram_tensor(n, v.shape, F32, kind="ExternalInput").ap() for n, v in arrays.items()]
    out = nc.dram_tensor("y_tokens", (P, TT, D), F32, kind="ExternalOutput").ap()
    transformer_stacks(nc, *args, out)
    result = run_bass_kernel_spmd(nc, [arrays], core_ids=[0]).results[0]["y_tokens"]
    return np.asarray(result).transpose(1, 0, 2).reshape(1, T, D)
```

```python
from contextlib import ExitStack
from dataclasses import dataclass
from typing import Any

import numpy as np
import concourse.bass as bass
from concourse import mybir

F32 = mybir.dt.float32
F32R = mybir.dt.float32r
ALU = mybir.AluOpType
ACT = mybir.ActivationFunctionType
AX = mybir.AxisListType

P = 128
D = 1024
T = 256
TT = T // P
KD = D // P
DFF = 2816
PAIRS = DFF // (2 * P)
STEP = 2048
RING = 3
EPS = 1e-6
NEG = -1e30
TINY = 1e-30
DEPTH1, DEPTH2 = 2, 4
A_HEADS, B_HEADS, C_HEADS = 4, 8, 4
C_QR, C_KVR, C_NOPE, C_ROPE = 384, 256, 128, 64
C_COLS = C_QR + C_KVR + C_ROPE
HEADS = 16
DH = 64
KVG = 4
BUCKETS, BUCKET_MAX = 32, 1024
CMP_LEN, CMP_STRIDE, CMP_HID = 32, 16, 256
NCMP = (T - CMP_LEN) // CMP_STRIDE + 1
NBLK = KVG * NCMP
LP = CMP_LEN // 2
SINK = T
NBIAS1 = A_HEADS + B_HEADS + 1
VEC = 512
LAM0 = [0.8 - 0.6 * float(np.exp(-0.3 * l)) for l in range(DEPTH1)]

PRM = {}
_at = 0
for _name, _n in (("subln", DEPTH1), ("cqn", DEPTH1 * 3), ("ckvn", DEPTH1 * 2),
                  ("bgate", DEPTH1 * 24), ("sink1", DEPTH1 * B_HEADS), ("sink2", 2 * HEADS),
                  ("lam", DEPTH1 * 4 * DH), ("pos", 2 * LP), ("cw2", 2 * 2 * DH), ("table", HEADS)):
    PRM[_name] = _at
    _at += _n
PRM_COLS = _at
CST = {}
_at = 0
for _name, _n in (("ident", P), ("cos", TT * 32), ("sin", TT * 32), ("cmpneg", TT * NCMP), ("cmpok", TT * NCMP),
                  ("onehot", 2 * VEC)):
    CST[_name] = _at
    _at += _n
CST_COLS = _at


@dataclass(eq=False)
class Phase:
    kind: str
    engines: tuple
    before: dict
    base: dict
    step: int
    stack: int
    after: str = ""
    factor: float = 1.0
    final: bool = False
    pre: bool = False
    gains: int = 0
    dest: str = ""
    n: int = 0
    job: str = ""
    bias: str = ""
    bias0: int = 0
    layer: int = 0
    sink: Any = None
    groups: Any = None
    k0: int = 0
    subln: Any = None
    src: str = ""


@dataclass
class Group:
    dest: str
    number: Any
    steps: int
    kk: int
    cols: int
    to: int


@dataclass
class Job:
    q: Any
    staged: Any
    k: Any
    dv: int
    rotary: bool
    scale: float
    sink: Any
    bias_row: Any
    key: Any
    vcol: Any
    ocol: Any


def plan():
    phases, count, steps, gain_rows = [], {}, 0, []

    def add(kind, engines, steps_used=0, up=None, **args):
        nonlocal steps
        before = {e: count.get(e + "_phase", 0) for e in ("pe", "act", "dve", "pool")}
        phases.append(Phase(kind=kind, engines=engines, before=before, base=dict(count), step=steps,
                                      stack=2 if any(p.final for p in phases) else 1, **args))
        for name, n in (up or {}).items():
            count[name] = count.get(name, 0) + n
        for e in engines:
            count[e + "_phase"] = count.get(e + "_phase", 0) + 1
        steps += steps_used

    def between(pre=None, after="", factor=1.0, post=None, final=False):
        rounds = (after == "post") + final + (pre is not None)
        engines = ("pe", "act", "dve", "pool") if pre is not None else ("act", "dve", "pool")
        add("between", engines, after=after, factor=factor, final=final, pre=pre is not None,
            gains=len(gain_rows),
            up=dict(sq_ready=2 * rounds, ms_ready=2 * rounds, rstd_ready=2 * rounds,
                    y_ready=2 if after == "post" else 0, x_ready=(2 if after else 0) + (2 if final else 0),
                    xn_ready=2 if pre is not None else 0, tposed=4 if pre is not None else 0,
                    hi_made=4 if pre is not None else 0, gains_loaded=16))
        gain_rows.append((post, pre))

    def ffn():
        n = PAIRS
        add("ffn", ("pe", "act", "dve"), 3 * n,
            up=dict(low_a=n, low_g=n, a_summed=n, g_summed=n, silu_ready=n,
                    h_ready=n, hh_ready=n, ht_ready=n, acc_half=1))

    def f(dest, head0, n):
        return [Group(dest, n_, 1, KD, 2 * P, head0 + 4 * n_) for n_ in range(n)]

    def t(dest, col0, cols, kk, n, chunks):
        return [Group(dest, None, n, kk, cols, col0 + c * cols) for c in range(chunks)]

    def project(*parts):
        groups = [g for part in parts for g in part]
        n_f = sum(g.number is not None for g in groups)
        add("project", ("pe", "act", "dve"), sum(g.steps for g in groups), groups=groups,
            up=dict(low_copied=n_f, group_free=n_f, stored_tokens=len(groups) - n_f,
                    high_ready=sum(g.number is not None and g.dest != "cmp" for g in groups)))

    def attend(kind, n, bias, bias0, **a):
        extra = {"diff": dict(rs_ready=n // 2), "nsa_slc": dict(rs_ready=n), "nsa_win": dict(rs_ready=n)}.get(kind, {})
        add("attend", ("pe", "act", "dve", "pool"), job=kind, n=n, bias=bias, bias0=bias0, **a,
            up=dict(q_staged=n, scores_ready=n, biased=n, max_ready=n, probs_ready=n, transposed=n, pt_ready=n,
                    recip_ready=n, pv_ready=n, o_done=n, bias_even=n // 2 * 16, bias_odd=n // 2 * 16, **extra))

    def turn(k0, n, subln=None):
        add("turn", ("pe", "act", "dve"), k0=k0, n=n, subln=subln,
            up=dict(tposed=n, hi_made=n, head_norm=0 if subln is None else 6))

    def wout(src):
        add("wout", ("pe", "act", "dve"), 4, src=src, up=dict(acc_half=1))

    add("setup", ("pe", "act", "dve"), up=dict(vec_made=2, vec_copied=2, lam_sum=1, lam_exp=1, lam_sub=2,
                                                       lam_mul=1))
    for l in range(DEPTH1):
        if l == 0:
            between(pre=("ffn1", l))
        else:
            between(pre=("ffn1", l), after="plain", factor=0.5)
        ffn()
        between(pre=("mix", l), after="plain", factor=0.5)
        project(f("q", 0, 2), f("k", 0, 2), t("v", 0, 512, 4, 2, 1))
        attend("diff", 8, "fixed", 0, layer=l)
        turn(0, 4, subln=l)
        project(f("q", 0, 2), f("kv", 0, 1))
        attend("gqa1", 8, "fixed", A_HEADS, sink=PRM["sink1"] + l * B_HEADS)
        turn(4, 4)
        project(t("c", 0, C_COLS // 2, 4, 2, 2))
        add("mla_latent", ("pe", "act", "dve"), layer=l,
            up=dict(sumsq=4, std_ready=2, rstd_ready=1, xn_ready=6, tposed=6, hi_made=5))
        add("mla_up", ("pe", "act", "dve"), 3, layer=l,
            up=dict(group_ready=2, low_copied=2, qv_stored=3, k_stored=2, rope_done=4, tposed=8))
        attend("mla", 4, "fixed", NBIAS1 - 1)
        turn(8, 4)
        add("gates", ("pe", "act", "dve"), 18, layer=l,
            up=dict(low_copied=24, logits_summed=12, gate_ready=12, parts_summed=12, gated=12,
                    merged_ready=8, hh_ready=2))
        wout("y")
        between(pre=("ffn2", l), after="plain")
        ffn()
    for i in range(DEPTH2):
        if i == 0:
            between(pre=("n2", i, 0), after="plain", factor=0.5, final=True, post=("final",))
        else:
            between(pre=("n2", i, 0), after="post", factor=0.5, post=("n2", i - 1, 5))
        ffn()
        between(pre=("n2", i, 2), after="post", factor=0.5, post=("n2", i, 1))
        if i % 3 == 0:
            project(f("q", 0, 4), f("kv", 0, 1))
            attend("gqa2", HEADS, "window", 0, sink=PRM["sink2"] + (i // 3) * HEADS)
        elif i % 3 == 1:
            project(f("q", 0, 4), f("cmp", 0, 2))
            add("compress", ("pe", "act", "dve"), 4,
                up=dict(blk_added=2, blk_hi=2, blk_made=2, low_copied=2, group_free=2, gelu_done=2,
                        cmp_ready=1))
            project(f("k", 0, 1), t("v", 0, 256, 8, 1, 1), f("k", 4, 1), t("v", 256, 256, 8, 1, 1),
                    t("gate", 0, 48, 8, 1, 1))
            add("cmp_attend", ("pe", "act", "dve"),
                up=dict(scores_ready=1, cmp_step=10, max_ready=1, probs_ready=1, transposed=1, pt_ready=1,
                        pv_ready=1))
            attend("nsa_slc", HEADS, "causal", 0)
            attend("nsa_win", HEADS, "causal", 0)
        else:
            project(f("q", 0, 4), f("k", 0, 4), t("v", 0, 512, 4, 2, 2))
            attend("moba", HEADS, "causal", 0)
        turn(0, 8)
        wout("o")
        between(pre=("n2", i, 4), after="post", post=("n2", i, 3))
        ffn()
    between(after="post", factor=0.5, post=("n2", DEPTH2 - 1, 5))
    add("store", ("act",))
    return phases, count, steps, gain_rows


def transformer_stacks(nc, stream, prm_in, cst_in, fixed_bias, gains_in, x_in, out, limit=None):
    phases, totals, n_steps, gain_rows = plan()
    if limit is not None:
        limit_steps = phases[limit].step
        phases = phases[:limit] + [p for p in phases if p.kind == "store"]
        phases[-1].before = phases[-2].before | {
            e: phases[-2].before[e] + (e in phases[-2].engines) for e in phases[-2].before}
        n_steps = limit_steps
    n_gains = sum(p.kind == "between" for p in phases)
    n_steps += 2
    n_steps += -n_steps % RING
    vec = nc.dram_tensor("rel_vectors", [2 * HEADS, VEC], F32, kind="Internal").ap()
    rel_bias = nc.dram_tensor("rel_bias", [2 * HEADS, P, TT, T], F32, kind="Internal").ap()

    with ExitStack() as ctx:
        def sb(name, shape, dt=F32):
            return ctx.enter_context(nc.sbuf_tensor(name, shape, dt))

        def overlay(*regions):
            sizes = [sum(int(np.prod(shape[1:])) for _, shape, _ in region) for region in regions]
            assert sizes[-1] == max(sizes)
            made = []
            for n, region in enumerate(regions):
                if n == len(regions) - 1:
                    made += [sb(*t) for t in region]
                    continue
                with ExitStack() as part:
                    made += [part.enter_context(nc.sbuf_tensor(*t)) for t in region]
            return made

        raw = sb("raw", [P, RING, STEP])
        whi = sb("whi", [P, RING, STEP], F32R)
        wlo = sb("wlo", [P, RING, STEP], F32R)
        x = sb("x", [P, TT, D])
        xhl = sb("xhl", [P, KD, 2 * T], F32R)
        v = sb("v", [P, TT, D])
        o = sb("o", [P, TT, D])
        prm = sb("prm", [P, PRM_COLS])
        cst = sb("cst", [P, CST_COLS])
        gains = sb("gain", [P, 2, D])
        small = sb("small", [P, 128])
        (yhl, br2, qm, km, qpe, kpe, q2, k2, under_blk, blk, q1, k1, br1) = overlay(
            [("yhl", [P, KD, 2 * T], F32R)],
            [("br2", [P, KD, 2 * T], F32R)],
            [("qm", [P, C_HEADS, T], F32), ("km", [P, C_HEADS, T], F32), ("qpe", [P, C_HEADS, T], F32),
             ("kpe", [P, T], F32)],
            [("q2", [P, HEADS, T], F32R), ("k2", [P, HEADS, 2, T], F32R)],
            [("under_blk", [P, HEADS, T], F32), ("blk", [P, 2, LP, 2 * NBLK], F32R)],
            [("q1", [P, 8, T], F32R), ("k1", [P, 8, 2, T], F32R), ("br1", [P, 12, 2 * T], F32R)])
        (qsm, pcmp, vblk, kcb, gates, chl) = overlay(
            [("qsm", [P, 2, T], F32)],
            [("pcmp", [P, TT, HEADS, 32], F32), ("vblk", [P, KVG, T], F32), ("kcb", [P, NBLK], F32),
             ("gates", [P, TT, 48], F32)],
            [("chl", [P, 5, 2 * T], F32R)])
        (low_half, logits, gate, part_sum, merged, ta, a_sum, silu, tg, g_sum, h, ht, tl, whole, high, cblk, chid, cpre, scmp, s, pr, pt, qs, qps, bias) = overlay(
            [("low_half", [P, 2, 2, T], F32), ("logits", [P, 2, 2, T], F32), ("gate", [P, 2, 2, T], F32),
             ("part_sum", [P, 2, 2, T], F32), ("merged", [P, 2, 2, T], F32)],
            [("ta", [P, 2, T], F32), ("a_sum", [P, 2, T], F32), ("silu", [P, 2, T], F32), ("tg", [P, 2, T], F32),
             ("g_sum", [P, 2, T], F32), ("h", [P, 2, T], F32), ("ht", [P, 2, 2, 2, T], F32R)],
            [("tl", [P, 2, 2, T], F32), ("whole", [P, 2, 2, T], F32), ("high", [P, 2, 2, T], F32R), ("cblk", [P, LP, KVG, NCMP], F32), ("chid", [P, 2, 2, NBLK], F32),
             ("cpre", [P, 2, 2, NBLK], F32), ("scmp", [P, TT, HEADS, NCMP], F32)],
            [("s", [P, 2, TT, T + 4], F32), ("pr", [P, 2, TT, T + 4], F32), ("pt", [P, 2, TT, T], F32),
             ("qs", [P, 2, T], F32R), ("qps", [P, 2, T], F32), ("bias", [P, 2, TT, T], F32)])
        latent = o[:, :, 0:C_COLS]
        qtok = o[:, :, 0:C_HEADS * (C_NOPE + C_ROPE)]
        cmp_src = o[:, :, :].rearrange("p w (g t) -> p w g t", g=KVG)
        ps = ctx.enter_context(nc.psum_tensor("ps", [P, 8, 512], F32))
        acc = ps[:, 4:8, :]

        ident = cst[:, CST["ident"]:CST["ident"] + P]
        stat = small[:, 0:8]
        nmax = small[:, 8:12]
        sums = small[:, 12:16]
        rs = small[:, 16:20]
        lam = small[:, 20:22]
        lam_s = small[:, 22:26]
        eps = small[:, 26:27]
        minus_half = small[:, 27:28]
        unused = small[:, 28:29]
        rstd = small[:, 32:40]

        names = [n for n in totals if not n.endswith("_phase")]
        sem = {n: ctx.enter_context(nc.semaphore(n)) for n in names}
        for n in ("pe_phase", "act_phase", "dve_phase", "pool_phase", "hi_ready", "lo_ready", "step_used",
                  "loaded", "vec_stored", "stored", "bias_stored", "eps_set"):
            sem[n] = ctx.enter_context(nc.semaphore(n))
        raw_ready = [ctx.enter_context(nc.semaphore(f"raw_ready{i}")) for i in range(RING)]
        N_LOADED = 16 * 3
        BIAS_PART = 4
        N_PARTS = 2 * HEADS // BIAS_PART * TT
        N_STORED = 16 * N_PARTS
        FIRST_LOADS = 1 + N_PARTS

        ptf = pt[:, :, :, :].rearrange("p a b c -> p a (b c)")

        def wait(eng, semaphore, value):
            if isinstance(value, int) and value <= 0:
                return
            eng.wait_ge(semaphore, value)

        def enter(eng, me, ph):
            for e in ("pe", "act", "dve", "pool"):
                if e == "pe" and ph.kind == "between":
                    continue
                wait(eng, sem[e + "_phase"], ph.before[e])

        def leave(eng, me):
            eng.drain().then_inc(sem[me + "_phase"], 1)

        def run(eng, me, kinds):
            for ph in phases:
                if me in ph.engines:
                    enter(eng, me, ph)
                    kinds[ph.kind](ph)
                    leave(eng, me)

        def base(ph, name):
            return ph.base.get(name, 0)

        def at_step(c, i, stride):
            return c if i is None else stride * i + c

        def landings(c, i, stride):
            n = c // RING + 1
            return n if i is None else (stride // RING) * i + n

        def spread(ap, axis, n):
            dims = [list(d) for d in ap.ap]
            return bass.AP(ap.tensor, ap.offset, dims[:axis] + [[0, n]] + dims[axis:])

        def pipelined(eng, n, iteration):
            for t in range(4):
                iteration(t, t % 2, t // 2, [d for d in range(3) if t - d >= 0])
            if n > 4:
                with eng.Fori(2, n // 2 - 1) as i:
                    for parity in (0, 1):
                        iteration(2 * i + parity, parity, i, [0, 1, 2])
                for t in (n - 2, n - 1):
                    iteration(t, t % 2, t // 2, [0, 1, 2])
            for t in (n, n + 1):
                iteration(t, t % 2, t // 2, [d for d in (1, 2) if t - d < n])

        def job_of(ph):
            kind = ph.job
            first = kind in ("diff", "gqa1", "mla")
            wide = kind in ("diff", "mla")
            dv = P if wide else DH
            same = lambda t: t
            key, value = {
                "diff": (same, lambda t: t // 2),
                "gqa1": (lambda t: t // 4, lambda t: t // 4),
                "mla": (same, same),
                "gqa2": (lambda t: t // 8, lambda t: t // 8),
                "nsa_slc": (lambda t: t // 4, lambda t: t // 4),
                "nsa_win": (lambda t: t // 4 + KVG, lambda t: t // 4 + KVG),
                "moba": (same, same),
            }[kind]
            row = {"diff": lambda t: t // 2, "mla": lambda t: ph.bias0}.get(kind, lambda t: t + ph.bias0)
            q, k, staged = (qm, km, qsm) if kind == "mla" else (q1, k1, qs) if first else (q2, k2, qs)
            return Job(q=q, k=k, staged=staged, dv=dv,
                       rotary=kind == "mla", scale=(C_NOPE + C_ROPE if kind == "mla" else DH) ** -0.5, sink=ph.sink,
                       bias_row=row, key=key, vcol=lambda t: value(t) * dv,
                       ocol=lambda t: (t // 2 if kind == "diff" else t) * dv)

        def accumulated(eng, ph, tt):
            if tt == 0:
                eng.wait_ge(sem["acc_half"], base(ph, "acc_half"))
            else:
                eng.wait_ge(sem["step_used"], ph.step)

        def halves(ap):
            return ap.rearrange("p (a b) -> p a b", a=2)

        def blocks_of(ph):
            return [(kt, qt) for kt in range(TT) for qt in range(TT) if ph.bias == "fixed" or kt <= qt]

        def numbered(ph):
            step, before = ph.step, [0, 0]
            for n, g in enumerate(ph.groups):
                form = int(g.number is None)
                yield g, step, 2 * (n % 2), before[form]
                step += g.steps
                before[form] += 1

        def by_head(ph, g, nt, part):
            q, k = (q1, k1) if ph.stack == 1 else (q2, k2)
            for half in range(2):
                rows = slice(half * DH, half * DH + DH)
                heads = slice(g.to + half, g.to + 2 * nt, 2)
                if g.dest == "q":
                    yield rows, half, q[part * DH:part * DH + DH, heads, :]
                else:
                    for at in (0, DH):
                        yield rows, half, k[at:at + DH, heads, part, :]

        def mixed(ph):
            return br1 if ph.stack == 1 else br2

        block = ctx.enter_context(nc.Block())

        @block.sync
        def _(sp):
            sp.wait_ge(sem["loaded"], N_LOADED)
            sp.dma_start(raw[:, 0, :], stream[0]).then_inc(raw_ready[0], 16)
            sp.dma_start(raw[:, 1, :], stream[1]).then_inc(raw_ready[1], 16)
            sp.dma_start(raw[:, 2, :], stream[2]).then_inc(raw_ready[2], 16)
            for i in range(1, FIRST_LOADS):
                for slot in range(RING):
                    sp.wait_ge(sem["lo_ready"], RING * i + (slot - RING + 1))
                    sp.dma_start(raw[:, slot, :], stream[RING * i + slot]).then_inc(raw_ready[slot], 16)
                if i == 1:
                    sp.wait_ge(sem["vec_stored"], 16)
                qt, h0 = (i - 1) % TT, (i - 1) // TT * BIAS_PART
                src = bass.AP(vec.tensor, h0 * VEC + T - 1 - qt * P, [[VEC, BIAS_PART], [-1, P], [1, T]])
                sp.dma_start(rel_bias[h0:h0 + BIAS_PART, :, qt, :], src).then_inc(sem["bias_stored"], 16)
            with sp.Fori(FIRST_LOADS, n_steps // RING) as i:
                for slot in range(RING):
                    sp.wait_ge(sem["lo_ready"], RING * i + (slot - RING + 1))
                    sp.dma_start(raw[:, slot, :], stream[RING * i + slot]).then_inc(raw_ready[slot], 16)
            sp.wait_ge(sem["bias_stored"], N_STORED)
            for slot in range(RING):
                sp.wait_ge(raw_ready[slot], n_steps // RING * 16)

        @block.gpsimd
        def _(pool):

            def between(ph):
                rounds = ([ph.factor] if ph.after == "post" else []) + [1.0] * (ph.final + ph.pre)
                for r, factor in enumerate(rounds):
                    for tt in range(TT):
                        n = 2 * r + tt
                        ms = stat[:, n:n + 1]
                        pool.wait_ge(sem["sq_ready"], base(ph, "sq_ready") + n + 1)
                        pool.tensor_scalar(ms, ms, EPS, factor ** -2.0, ALU.add, ALU.mult)\
                            .then_inc(sem["ms_ready"], 1)
                        pool.wait_ge(sem["ms_ready"], base(ph, "ms_ready") + n + 1)
                        pool.tensor_tensor(rstd[:, n:n + 1], ms, minus_half, ALU.pow).then_inc(sem["rstd_ready"], 1)
            def attend(ph):
                job = job_of(ph)

                def stage(t, parity):
                    if not isinstance(t, int) or t >= 2:
                        pool.wait_ge(sem["scores_ready"], t + (base(ph, "scores_ready") - 1))
                    if job.rotary:
                        pool.tensor_copy(qps[0:C_ROPE, parity, :], qpe[0:C_ROPE, t, :])
                    pool.tensor_copy(job.staged[:, parity, :], job.q[:, t, :]).then_inc(sem["q_staged"], 1)

                stage(0, 0)
                stage(1, 1)
                with pool.Fori(1, ph.n // 2) as i:
                    for parity in (0, 1):
                        stage(2 * i + parity, parity)

            run(pool, "pool", dict(between=between, attend=attend))

        @block.scalar
        def _(act):
            def split(c, i=None, stride=0):
                slot = c % RING
                act.wait_ge(raw_ready[slot], 16 * landings(c, i, stride))
                wait(act, sem["step_used"], at_step(c - (RING - 1), i, stride))
                nc.scalar.copy(whi[:, slot, :], raw[:, slot, :]).then_inc(sem["hi_ready"], 1)

            def after_between(ph):
                if phases[phases.index(ph) - 1].kind == "between":
                    split(ph.step + 1)

            def ahead(ph, k):
                split(ph.step + k + 2)

            def multiplied(c, i=None, stride=0):
                act.wait_ge(sem["step_used"], at_step(c + 1, i, stride))

            def load_gains(n):
                row = gains_in[n].rearrange("a n -> (a n)")
                act.dma_start(gains[:, :, :].rearrange("p a n -> p (a n)"),
                              row.partition_broadcast(P)).then_inc(sem["gains_loaded"], 16)

            def setup(ph):
                act.dma_start(x[:, :, :], x_in).then_inc(sem["loaded"], 16)
                act.dma_start(prm[:, :], prm_in).then_inc(sem["loaded"], 16)
                act.dma_start(cst[:, :], cst_in).then_inc(sem["loaded"], 16)
                load_gains(0)
                act.wait_ge(sem["lam_sum"], 1)
                nc.scalar.activation(lam_s, lam_s, ACT.Exp).then_inc(sem["lam_exp"], 1)
                act.wait_ge(sem["vec_copied"], 2)
                act.dma_start(vec.rearrange("(w h) n -> h w n", w=2),
                              o[0:HEADS, :, 0:VEC]).then_inc(sem["vec_stored"], 16)

            def between(ph):
                def mean_square(n, tt, src):
                    junk = v[:, tt, :] if len(src.shape) == 2 else halves(v[:, tt, :])
                    nc.scalar.activation(junk, src, ACT.Square, scale=D ** -0.5,
                                         accum_out=stat[:, n:n + 1]).then_inc(sem["sq_ready"], 1)

                n = 0
                if ph.after == "post":
                    for tt in range(TT):
                        accumulated(act, ph, tt)
                        mean_square(n + tt, tt, acc[:, 2 * tt:2 * tt + 2, :])
                    n += 2
                done = base(ph, "x_ready") + (2 if ph.after else 0)
                for _ in range(ph.final + ph.pre):
                    for tt in range(TT):
                        wait(act, sem["x_ready"], done - 1 + tt)
                        mean_square(n + tt, tt, x[:, tt, :])
                    n += 2
                    done += 2
                if ph.gains == 0:
                    split(0)
                if ph.pre:
                    for n in range(4):
                        tt, k0 = n // 2, 4 * (n % 2)
                        act.wait_ge(sem["tposed"], base(ph, "tposed") + n + 1)
                        nc.scalar.copy(xhl[:, k0:k0 + 4, tt * P:(tt + 1) * P],
                                       ps[:, n, :].rearrange("p (k q) -> p k q", k=4)).then_inc(sem["hi_made"], 1)
                if ph.gains + 1 < n_gains:
                    load_gains(ph.gains + 1)

            def ffn(ph):
                def half_a(j):
                    nc.scalar.copy(ta[:, :, :], ps[:, 0:2, 0:T]).then_inc(sem["low_a"], 1)
                    act.wait_ge(sem["a_summed"], j + (base(ph, "a_summed") + 1))
                    nc.scalar.activation(silu[:, :, :], a_sum[:, :, :], ACT.Silu).then_inc(sem["silu_ready"], 1)

                def half_g(j, buffer=0):
                    nc.scalar.copy(tg[:, :, :], ps[:, 2:4, 0:T]).then_inc(sem["low_g"], 1)
                    act.wait_ge(sem["h_ready"], j + (base(ph, "h_ready") + 1))
                    nc.scalar.copy(ht[:, buffer, :, 0, :], h[:, :, :]).then_inc(sem["hh_ready"], 1)

                after_between(ph)
                end = ph.step + 3 * PAIRS
                split(ph.step + 2)
                multiplied(ph.step)
                half_a(0)
                split(ph.step + 3)
                multiplied(ph.step + 1)
                half_g(0)
                with act.Fori(1, PAIRS - 1) as j:
                    split(ph.step + 1, j, 3)
                    multiplied(ph.step - 1, j, 3)
                    half_a(j)
                    split(ph.step + 2, j, 3)
                    split(ph.step + 3, j, 3)
                    multiplied(ph.step + 1, j, 3)
                    half_g(j)
                split(end - 2)
                multiplied(end - 4)
                half_a(PAIRS - 1)
                split(end - 1)
                multiplied(end - 3)
                half_g(PAIRS - 1, 1)
                split(end)

            def load_bias(ph, t, parity):
                table = fixed_bias if ph.bias == "fixed" else rel_bias
                row0 = HEADS if ph.bias == "window" else 0
                act.dma_start(bias[:, parity, :, :], table[job_of(ph).bias_row(t) + row0])\
                    .then_inc((sem["bias_even"], sem["bias_odd"])[parity], 16)

            def first_biases(ph):
                if ph.bias != "fixed":
                    act.wait_ge(sem["bias_stored"], N_STORED)
                load_bias(ph, 0, 0)
                load_bias(ph, 1, 1)

            def follows_product(ph):
                return ph.kind == "attend" and phases[phases.index(ph) - 1].kind in ("project", "mla_up")

            def bias_ahead(ph):
                follower = phases[phases.index(ph) + 1]
                if follows_product(follower):
                    first_biases(follower)

            def project(ph):
                after_between(ph)
                bias_ahead(ph)
                token_major = {"v": v, "c": latent, "gate": gates}
                for g, step, bank, n in numbered(ph):
                    for i in range(g.steps):
                        split(step + i + 2)
                    multiplied(step + g.steps - 1)
                    if g.number is None:
                        func = ACT.Sigmoid if g.dest == "gate" else ACT.Copy
                        nc.scalar.activation(token_major[g.dest][:, :, g.to:g.to + g.cols],
                                             ps[:, bank:bank + 2, 0:g.cols], func).then_inc(sem["stored_tokens"], 1)
                        continue
                    if g.dest == "cmp":
                        wait(act, sem["group_free"], base(ph, "group_free") + n - 1)
                    nt = 1 if g.dest == "kv" else 2
                    nc.scalar.copy(tl[:, n % 2, 0:nt, :], ps[:, bank:bank + nt, 0:T]).then_inc(sem["low_copied"], 1)
                    if g.dest == "kv":
                        nc.scalar.copy(v[:, :, 0:P], ps[:, 4:6, P:T])
                    if g.dest != "cmp":
                        act.wait_ge(sem["group_free"], base(ph, "group_free") + n + 1)
                        nc.scalar.copy(high[:, n % 2, 0:nt, :], whole[:, n % 2, 0:nt, :]).then_inc(sem["high_ready"], 1)
                        for rows, half, dst in by_head(ph, g, nt, 0):
                            nc.scalar.copy(dst, whole[rows, n % 2, 0:nt, :])

            def attend(ph):
                job = job_of(ph)
                blocks = blocks_of(ph)
                B = {n: base(ph, n) for n in ("max_ready", "transposed", "recip_ready", "pv_ready")}
                if not follows_product(ph):
                    first_biases(ph)
                nc.scalar.activation(unused, eps, ACT.Exp)

                def iteration(t, parity, pair, stages, width=T + 1):
                    if 0 in stages:
                        act.wait_ge(sem["max_ready"], t + (B["max_ready"] + 1))
                        if not isinstance(t, int) or t + 2 < ph.n:
                            load_bias(ph, t + 2, parity)
                        if 2 in stages:
                            act.wait_ge(sem["transposed"], t + (B["transposed"] - 1))
                            act.wait_ge(sem["recip_ready"], t + (B["recip_ready"] - 1))
                        for qt in range(TT):
                            n = 2 * parity + qt
                            if job.sink is None:
                                width = sum(q == qt for _, q in blocks) * P
                            e = nc.scalar.activation(pr[:, parity, qt, 0:width], s[:, parity, qt, 0:width], ACT.Exp,
                                                     bias=nmax[:, n:n + 1], accum_out=sums[:, n:n + 1])
                        e.then_inc(sem["probs_ready"], 1)
                    if 1 in stages:
                        act.wait_ge(sem["transposed"], t + B["transposed"])
                        if not isinstance(t, int) or t >= 3:
                            act.wait_ge(sem["pv_ready"], t + (B["pv_ready"] - 2))
                        nc.scalar.copy(ptf[:, 1 - parity, 0:len(blocks) * P],
                                       ps[:, 3 - parity, 0:len(blocks) * P]).then_inc(sem["pt_ready"], 1)

                pipelined(act, ph.n, iteration)

            def turn(ph):
                for k in range(ph.n):
                    act.wait_ge(sem["tposed"], base(ph, "tposed") + k + 1)
                    dst = mixed(ph)[:, ph.k0 + k, 0:T]
                    if ph.subln is None:
                        nc.scalar.copy(dst, ps[:, k, 0:T]).then_inc(sem["hi_made"], 1)
                    else:
                        g = prm[:, PRM["subln"] + ph.subln:PRM["subln"] + ph.subln + 1]
                        nc.scalar.activation(dst, ps[:, k, 0:T], ACT.Identity, scale=g).then_inc(sem["hi_made"], 1)

            def turn_subln(ph):
                if ph.subln is not None:
                    act.wait_ge(sem["head_norm"], base(ph, "head_norm") + 2)
                    nc.scalar.activation(stat[:, 0:8], stat[:, 0:8], ACT.Sqrt, bias=eps,
                                         scale=1.0 / P).then_inc(sem["head_norm"], 1)
                turn(ph)

            def mla_latent(ph):
                parts = [latent[:, tt, 0:C_QR] for tt in range(TT)] + [latent[:, tt, C_QR:C_QR + C_KVR]
                                                                      for tt in range(TT)]
                for n, part in enumerate(parts):
                    nc.scalar.activation(v[:, n // 2, 512 * (n % 2):512 * (n % 2) + part.free_size()], part,
                                         ACT.Square, accum_out=stat[:, n:n + 1]).then_inc(sem["sumsq"], 1)
                act.wait_ge(sem["sumsq"], base(ph, "sumsq") + 4)
                nc.scalar.activation(stat[:, 0:2], stat[:, 0:2], ACT.Sqrt, bias=eps,
                                     scale=1.0 / C_QR).then_inc(sem["std_ready"], 1)
                nc.scalar.activation(stat[:, 2:4], stat[:, 2:4], ACT.Sqrt, bias=eps,
                                     scale=1.0 / C_KVR).then_inc(sem["std_ready"], 1)
                for k in range(5):
                    at = PRM["cqn"] + ph.layer * 3 + k if k < 3 else PRM["ckvn"] + ph.layer * 2 + k - 3
                    act.wait_ge(sem["tposed"], base(ph, "tposed") + k + 1)
                    nc.scalar.activation(chl[:, k, 0:T], ps[:, k, 0:T], ACT.Identity,
                                         scale=prm[:, at:at + 1]).then_inc(sem["hi_made"], 1)

            def mla_up(ph):
                bias_ahead(ph)
                gr = base(ph, "group_ready")
                for i in range(2):
                    ahead(ph, i)
                    multiplied(ph.step + i)
                    nc.scalar.copy(qtok[:, :, i * C_QR:(i + 1) * C_QR],
                                   ps[:, 2 * i:2 * i + 2, 0:C_QR]).then_inc(sem["qv_stored"], 1)
                ahead(ph, 2)
                for i in range(2):
                    act.wait_ge(sem["group_ready"], gr + 1 + i)
                    nc.scalar.copy(tl[:, i, :, :], ps[:, 4 + 2 * i:6 + 2 * i, 0:T]).then_inc(sem["low_copied"], 1)
                multiplied(ph.step + 2)
                nc.scalar.copy(v[:, :, 0:512], ps[:, 0:2, :]).then_inc(sem["qv_stored"], 1)

            def gates_(ph):
                def low(half, bank):
                    nc.scalar.copy(low_half[:, half, :, :], ps[:, bank:bank + 2, 0:T]).then_inc(sem["low_copied"], 1)

                with act.Fori(0, 2) as grp:
                    for n in range(3):
                        c = ph.step + 3 * n
                        twice = 6 * grp + 2 * n
                        split(c + 2, grp, 9)
                        for half in range(2):
                            multiplied(c + half, grp, 9)
                            act.wait_ge(sem["parts_summed"], twice + base(ph, "parts_summed"))
                            low(half, 2 * half)
                            split(c + 3 + half, grp, 9)
                            act.wait_ge(sem["gated"], twice + base(ph, "gated"))
                            act.wait_ge(sem["logits_summed"], twice + (base(ph, "logits_summed") + half + 1))
                            for i in range(2):
                                col = PRM["bgate"] + ph.layer * 24 + n * 8 + 2 * half + i
                                e = nc.scalar.activation(gate[:, half, i, :], logits[:, half, i, :], ACT.Sigmoid,
                                                         bias=prm[:, bass.ds(4 * grp + col, 1)])
                            e.then_inc(sem["gate_ready"], 1)
                        multiplied(c + 2, grp, 9)
                        for half in range(2):
                            low(half, 4 + 2 * half)
                    act.wait_ge(sem["merged_ready"], 4 * grp + (base(ph, "merged_ready") + 4))
                    nc.scalar.copy(yhl[:, bass.ds(4 * grp, 4), 0:T], merged[:, :, :, :].rearrange("p a b t -> p (a b) t"))\
                        .then_inc(sem["hh_ready"], 1)

            def wout(ph):
                for i in range(3):
                    ahead(ph, i)

            def compress(ph):
                for w in range(2):
                    ahead(ph, 2 * w)
                    ahead(ph, 2 * w + 1)
                    multiplied(ph.step + 2 * w + 1)
                    nc.scalar.copy(tl[:, w, :, 0:NBLK], ps[:, 2 * w:2 * w + 2, 0:NBLK]).then_inc(sem["low_copied"], 1)
                    act.wait_ge(sem["group_free"], base(ph, "group_free") + w + 1)
                    nc.scalar.activation(chid[:, w, :, :], cpre[:, w, :, :], ACT.Gelu_apprx_tanh)\
                        .then_inc(sem["gelu_done"], 1)

            def cmp_attend(ph):
                act.wait_ge(sem["max_ready"], base(ph, "max_ready") + 1)
                nc.scalar.activation(scmp[:, :, :, :], scmp[:, :, :, :], ACT.Exp).then_inc(sem["probs_ready"], 1)
                act.wait_ge(sem["transposed"], base(ph, "transposed") + 1)
                nc.scalar.copy(ptf, ps[:, 2:4, :]).then_inc(sem["pt_ready"], 1)

            def store(ph):
                act.dma_start(out, x[:, :, :]).then_inc(sem["stored"], 16)
                act.wait_ge(sem["stored"], 16)

            run(act, "act", dict(setup=setup, between=between, ffn=ffn, project=project, attend=attend, turn=turn_subln, mla_latent=mla_latent,
                                 mla_up=mla_up, gates=gates_, wout=wout, compress=compress, cmp_attend=cmp_attend,
                                 store=store))

        @block.vector
        def _(dve):
            def split(c, i=None, stride=0):
                slot = c % RING
                dve.wait_ge(sem["hi_ready"], at_step(c + 1, i, stride))
                wait(dve, sem["step_used"], at_step(c - (RING - 1), i, stride))
                nc.vector.tensor_tensor(wlo[:, slot, :], raw[:, slot, :], whi[:, slot, :].bitcast(F32),
                                        ALU.subtract).then_inc(sem["lo_ready"], 1)

            def after_between(ph):
                if phases[phases.index(ph) - 1].kind == "between":
                    split(ph.step + 1)

            def ahead(ph, k):
                split(ph.step + k + 2)

            def setup(ph):
                nc.vector.memset(eps, EPS)
                nc.vector.memset(minus_half, -0.5)
                dve.wait_ge(sem["loaded"], N_LOADED)
                lp = prm[:, PRM["lam"]:PRM["lam"] + DEPTH1 * 4 * DH].rearrange("p (la b d) -> p la b d", b=2, d=DH)
                prod = v[:, 0, 0:4 * DH].rearrange("p (a d) -> p a d", a=4)
                nc.vector.tensor_tensor(prod, lp[:, :, 0, :], lp[:, :, 1, :], ALU.mult).then_inc(sem["lam_mul"], 1)
                dve.wait_ge(sem["lam_mul"], 1)
                nc.vector.tensor_reduce(lam_s, prod, AX.X, ALU.add).then_inc(sem["lam_sum"], 1)
                for w in range(2):
                    dve.wait_ge(sem["vec_made"], w + 1)
                    nc.vector.tensor_copy(o[0:HEADS, w, 0:VEC], ps[0:HEADS, w, :]).then_inc(sem["vec_copied"], 1)
                dve.wait_ge(sem["lam_exp"], 1)
                for l in range(DEPTH1):
                    nc.vector.scalar_tensor_tensor(out=lam[:, l:l + 1], in0=lam_s[:, 2 * l + 1:2 * l + 2],
                                                   scalar=-LAM0[l], in1=lam_s[:, 2 * l:2 * l + 1], op0=ALU.add,
                                                   op1=ALU.subtract).then_inc(sem["lam_sub"], 1)

            def low_parts(ph, n, dst, gain):
                for k in range(n):
                    dve.wait_ge(sem["hi_made"], base(ph, "hi_made") + k + 1)
                    hi = dst[:, k, 0:T].bitcast(F32)
                    g = gain(k)
                    nc.vector.scalar_tensor_tensor(out=dst[:, k, T:2 * T], in0=ps[:, k, 0:T],
                                                   scalar=1.0 if g is None else g, in1=hi, op0=ALU.mult,
                                                   op1=ALU.subtract)

            def between(ph):
                post, pre = gains[:, 0, :], gains[:, 1, :]
                b = {n: base(ph, n) for n in ("sq_ready", "rstd_ready", "y_ready", "gains_loaded")}
                n = 0
                if ph.after == "plain":
                    for tt in range(TT):
                        accumulated(dve, ph, tt)
                        xt = halves(x[:, tt, :])
                        nc.vector.scalar_tensor_tensor(out=xt, in0=acc[:, 2 * tt:2 * tt + 2, :], scalar=ph.factor,
                                                       in1=xt, op0=ALU.mult, op1=ALU.add).then_inc(sem["x_ready"], 1)
                dve.wait_ge(sem["gains_loaded"], b["gains_loaded"] + 16)
                if ph.after == "post":
                    for tt in range(TT):
                        dve.wait_ge(sem["sq_ready"], b["sq_ready"] + tt + 1)
                        nc.vector.tensor_tensor(halves(o[:, tt, :]), acc[:, 2 * tt:2 * tt + 2, :], halves(post),
                                                ALU.mult).then_inc(sem["y_ready"], 1)
                        dve.wait_ge(sem["rstd_ready"], b["rstd_ready"] + tt + 1)
                        dve.wait_ge(sem["y_ready"], b["y_ready"] + tt + 1)
                        nc.vector.scalar_tensor_tensor(out=x[:, tt, :], in0=o[:, tt, :], scalar=rstd[:, tt:tt + 1],
                                                       in1=x[:, tt, :], op0=ALU.mult, op1=ALU.add)\
                            .then_inc(sem["x_ready"], 1)
                    n = 2
                if ph.final:
                    for tt in range(TT):
                        dve.wait_ge(sem["rstd_ready"], b["rstd_ready"] + n + tt + 1)
                        nc.vector.scalar_tensor_tensor(out=x[:, tt, :], in0=x[:, tt, :],
                                                       scalar=rstd[:, n + tt:n + tt + 1], in1=post, op0=ALU.mult,
                                                       op1=ALU.mult).then_inc(sem["x_ready"], 1)
                    n += 2
                if ph.gains == 0:
                    dve.wait_ge(sem["vec_stored"], 16)
                if ph.pre:
                    for tt in range(TT):
                        dve.wait_ge(sem["rstd_ready"], b["rstd_ready"] + n + tt + 1)
                        nc.vector.scalar_tensor_tensor(out=o[:, tt, :], in0=x[:, tt, :],
                                                       scalar=rstd[:, n + tt:n + tt + 1], in1=pre, op0=ALU.mult,
                                                       op1=ALU.mult).then_inc(sem["xn_ready"], 1)
                    for n in range(4):
                        tt, k0 = n // 2, 4 * (n % 2)
                        dve.wait_ge(sem["hi_made"], base(ph, "hi_made") + n + 1)
                        nc.vector.tensor_tensor(xhl[:, k0:k0 + 4, T + tt * P:T + (tt + 1) * P],
                                                ps[:, n, :].rearrange("p (k q) -> p k q", k=4),
                                                xhl[:, k0:k0 + 4, tt * P:(tt + 1) * P].bitcast(F32), ALU.subtract)
                if ph.gains == 0:
                    split(0)

            def ffn(ph):
                def half_a(j):
                    dve.wait_ge(sem["low_a"], j + (base(ph, "low_a") + 1))
                    if not isinstance(j, int) or j > 0:
                        dve.wait_ge(sem["silu_ready"], j + base(ph, "silu_ready"))
                    nc.vector.tensor_tensor(a_sum[:, :, :], ps[:, 0:2, T:2 * T], ta[:, :, :], ALU.add)\
                        .then_inc(sem["a_summed"], 1)

                def half_g(j, buffer=0):
                    dve.wait_ge(sem["low_g"], j + (base(ph, "low_g") + 1))
                    nc.vector.tensor_tensor(g_sum[:, :, :], ps[:, 2:4, T:2 * T], tg[:, :, :], ALU.add)\
                        .then_inc(sem["g_summed"], 1)
                    dve.wait_ge(sem["g_summed"], j + (base(ph, "g_summed") + 1))
                    dve.wait_ge(sem["silu_ready"], j + (base(ph, "silu_ready") + 1))
                    if not isinstance(j, int) or j > 0:
                        dve.wait_ge(sem["ht_ready"], j + base(ph, "ht_ready"))
                    nc.vector.tensor_tensor(h[:, :, :], g_sum[:, :, :], silu[:, :, :], ALU.mult)\
                        .then_inc(sem["h_ready"], 1)
                    dve.wait_ge(sem["hh_ready"], j + (base(ph, "hh_ready") + 1))
                    nc.vector.tensor_tensor(ht[:, buffer, :, 1, :], h[:, :, :], ht[:, buffer, :, 0, :].bitcast(F32),
                                            ALU.subtract).then_inc(sem["ht_ready"], 1)

                after_between(ph)
                end = ph.step + 3 * PAIRS
                split(ph.step + 2)
                half_a(0)
                split(ph.step + 3)
                half_g(0)
                with dve.Fori(1, PAIRS - 1) as j:
                    split(ph.step + 1, j, 3)
                    half_a(j)
                    split(ph.step + 2, j, 3)
                    split(ph.step + 3, j, 3)
                    half_g(j)
                split(end - 2)
                half_a(PAIRS - 1)
                split(end - 1)
                half_g(PAIRS - 1, 1)
                split(end)

            def project(ph):
                after_between(ph)
                for g, step, bank, n in numbered(ph):
                    for i in range(g.steps):
                        split(step + i + 2)
                    if g.number is None:
                        continue
                    dve.wait_ge(sem["low_copied"], base(ph, "low_copied") + n + 1)
                    low = tl[:, n % 2, :, :]
                    if g.dest == "cmp":
                        for tile in range(2):
                            for half in range(2):
                                r = slice(half * DH, half * DH + DH)
                                to = cmp_src[:, g.number, 2 * tile + half, :]
                                nc.vector.tensor_tensor(to[0:DH, :], ps[r, bank + tile, T:2 * T],
                                                        low[r, tile, :], ALU.add)
                                e = nc.vector.tensor_tensor(to[DH:P, 0:T - 1], ps[r, bank + tile, T + 1:2 * T],
                                                            low[r, tile, 1:T], ALU.add)
                        e.then_inc(sem["group_free"], 1)
                        continue
                    nt = 1 if g.dest == "kv" else 2
                    nc.vector.tensor_tensor(whole[:, n % 2, 0:nt, :], ps[:, bank:bank + nt, T:2 * T], low[:, 0:nt, :],
                                            ALU.add).then_inc(sem["group_free"], 1)
                    dve.wait_ge(sem["high_ready"], base(ph, "high_ready") + n + 1)
                    for rows, half, dst in by_head(ph, g, nt, 1):
                        nc.vector.tensor_tensor(dst, whole[rows, n % 2, 0:nt, :],
                                                high[rows, n % 2, 0:nt, :].bitcast(F32), ALU.subtract)

            def attend(ph):
                job = job_of(ph)
                width = T + 1 if job.sink is not None else T
                loaded = (sem["bias_even"], sem["bias_odd"])
                b_loaded = (base(ph, "bias_even"), base(ph, "bias_odd"))
                B = {n: base(ph, n) for n in ("scores_ready", "biased", "probs_ready", "recip_ready", "rs_ready",
                                              "pv_ready", "o_done")}
                branch = {"nsa_slc": 1, "nsa_win": 2}.get(ph.job)

                def iteration(t, parity, pair, stages):
                    if 0 in stages:
                        if 2 in stages:
                            dve.wait_ge(sem["probs_ready"], t + (B["probs_ready"] - 1))
                        if job.sink is not None:
                            sink = spread(prm[:, bass.ds(t + job.sink, 1)], 1, TT)
                            nc.vector.tensor_copy(s[:, parity, :, SINK:SINK + 1], sink)
                        dve.wait_ge(sem["scores_ready"], t + (B["scores_ready"] + 1))
                        dve.wait_ge(loaded[parity], 16 * pair + (b_loaded[parity] + 16))
                        nc.vector.scalar_tensor_tensor(
                            out=s[:, parity, :, 0:T], in0=ps[:, parity, :].rearrange("p (a b) -> p a b", a=TT),
                            scalar=job.scale, in1=bias[:, parity, :, :], op0=ALU.mult,
                            op1=ALU.add).then_inc(sem["biased"], 1)
                        dve.wait_ge(sem["biased"], t + (B["biased"] + 1))
                        nc.vector.tensor_reduce(nmax[:, 2 * parity:2 * parity + 2], s[:, parity, :, 0:width], AX.X,
                                                ALU.max, negate=True).then_inc(sem["max_ready"], 1)
                    if 1 in stages:
                        r = rs[:, 2 - 2 * parity:4 - 2 * parity]
                        dve.wait_ge(sem["probs_ready"], t + B["probs_ready"])
                        if not isinstance(t, int) or t >= 3:
                            dve.wait_ge(sem["o_done"], t + (B["o_done"] - 2))
                        nc.vector.reciprocal(r, sums[:, 2 - 2 * parity:4 - 2 * parity]).then_inc(sem["recip_ready"], 1)
                        if ph.job == "diff" and parity == 0:
                            dve.wait_ge(sem["recip_ready"], t + B["recip_ready"])
                            nc.vector.tensor_scalar(r, r, lam[:, ph.layer:ph.layer + 1], None,
                                                    ALU.mult).then_inc(sem["rs_ready"], 1)
                        if branch is not None:
                            dve.wait_ge(sem["recip_ready"], t + B["recip_ready"])
                            g = gates[:, :, bass.ds((t - 1) * 3 + branch, 1)]
                            nc.vector.tensor_tensor(r.rearrange("p (a b) -> p a b", b=1),
                                                    r.rearrange("p (a b) -> p a b", b=1), g,
                                                    ALU.mult).then_inc(sem["rs_ready"], 1)
                    if 2 in stages:
                        dve.wait_ge(sem["recip_ready"], t + (B["recip_ready"] - 1))
                        if ph.job == "diff" and parity == 1:
                            dve.wait_ge(sem["rs_ready"], pair + B["rs_ready"])
                        if branch is not None:
                            dve.wait_ge(sem["rs_ready"], t + (B["rs_ready"] - 1))
                        dve.wait_ge(sem["pv_ready"], t + (B["pv_ready"] - 1))
                        add = branch is not None or (ph.job == "diff" and parity == 1)
                        if ph.job == "diff" and parity == 1:
                            dve.wait_ge(sem["o_done"], t + (B["o_done"] - 2))
                        for qt in range(TT):
                            dst = o[:, qt, bass.ds(job.ocol(t - 2), job.dv)]
                            src = ps[:, 4 + parity, qt * P:qt * P + job.dv]
                            r = rs[:, 2 * parity + qt:2 * parity + qt + 1]
                            if add:
                                e = nc.vector.scalar_tensor_tensor(out=dst, in0=src, scalar=r, in1=dst, op0=ALU.mult,
                                                                   op1=ALU.add)
                            else:
                                e = nc.vector.tensor_scalar(dst, src, r, None, ALU.mult)
                        e.then_inc(sem["o_done"], 1)

                pipelined(dve, ph.n, iteration)

            def turn(ph):
                gain = lambda k: None
                if ph.subln is not None:
                    b = base(ph, "head_norm")
                    heads = o[:, :, 0:A_HEADS * P].rearrange("p t (h c) -> p t h c", c=P)
                    sq = v[:, :, 0:A_HEADS * P].rearrange("p t (h c) -> p t h c", c=P)
                    nc.vector.tensor_tensor(sq, heads, heads, ALU.mult).then_inc(sem["head_norm"], 1)
                    dve.wait_ge(sem["head_norm"], b + 1)
                    nc.vector.tensor_reduce(stat.rearrange("p (t h) -> p t h", t=TT), sq, AX.X,
                                            ALU.add).then_inc(sem["head_norm"], 1)
                    dve.wait_ge(sem["head_norm"], b + 3)
                    nc.vector.reciprocal(rstd, stat).then_inc(sem["head_norm"], 1)
                    dve.wait_ge(sem["head_norm"], b + 4)
                    for tt in range(TT):
                        r = spread(rstd[:, tt * A_HEADS:(tt + 1) * A_HEADS], 2, P)
                        nc.vector.scalar_tensor_tensor(out=heads[:, tt], in0=heads[:, tt],
                                                       scalar=1.0 - LAM0[ph.subln], in1=r, op0=ALU.mult,
                                                       op1=ALU.mult).then_inc(sem["head_norm"], 1)
                    gain = lambda k: prm[:, PRM["subln"] + ph.subln:PRM["subln"] + ph.subln + 1]
                low_parts(ph, ph.n, mixed(ph)[:, ph.k0:ph.k0 + ph.n, :], gain)

            def rotate(lo, hi, c, sn, n, tmp, after):
                t1, t2, t3, t4 = tmp
                nc.vector.tensor_tensor(t1, lo, c, ALU.mult)
                nc.vector.tensor_tensor(t2, hi, sn, ALU.mult)
                nc.vector.tensor_tensor(t3, lo, sn, ALU.mult)
                nc.vector.tensor_tensor(t4, hi, c, ALU.mult).then_inc(after[0], 1)
                dve.wait_ge(after[0], after[1] + 1)
                nc.vector.tensor_tensor(lo, t1, t2, ALU.subtract)
                nc.vector.tensor_tensor(hi, t3, t4, ALU.add).then_inc(after[0], 1)

            cos = cst[:, CST["cos"]:CST["cos"] + TT * 32].rearrange("p (t f) -> p t f", t=TT)
            sin = cst[:, CST["sin"]:CST["sin"] + TT * 32].rearrange("p (t f) -> p t f", t=TT)

            def mla_latent(ph):
                b = base(ph, "xn_ready")
                at = C_QR + C_KVR
                tmp = [pr[:, 0, :, 64 * i:64 * i + 32] for i in range(4)]
                rotate(latent[:, :, at:at + 32], latent[:, :, at + 32:at + 64], cos, sin, 1, tmp, (sem["xn_ready"], b))
                dve.wait_ge(sem["std_ready"], base(ph, "std_ready") + 2)
                nc.vector.reciprocal(rstd[:, 0:4], stat[:, 0:4]).then_inc(sem["rstd_ready"], 1)
                dve.wait_ge(sem["rstd_ready"], base(ph, "rstd_ready") + 1)
                for n in range(4):
                    c0, c1 = ((0, C_QR), (C_QR, at))[n // 2]
                    part = latent[:, n % 2, c0:c1]
                    nc.vector.tensor_scalar(part, part, rstd[:, n:n + 1], None, ALU.mult).then_inc(sem["xn_ready"], 1)

                def gain(k):
                    at = PRM["cqn"] + ph.layer * 3 + k if k < 3 else PRM["ckvn"] + ph.layer * 2 + k - 3
                    return prm[:, at:at + 1]

                low_parts(ph, 5, chl, gain)
                dve.wait_ge(sem["tposed"], base(ph, "tposed") + 6)
                nc.vector.tensor_copy(kpe[0:C_ROPE, :], ps[0:C_ROPE, 5, 0:T])

            def mla_up(ph):
                lc = base(ph, "low_copied")
                ahead(ph, 0)
                ahead(ph, 1)
                ahead(ph, 2)
                for i in range(2):
                    dve.wait_ge(sem["low_copied"], lc + i + 1)
                    nc.vector.tensor_tensor(km[:, 2 * i:2 * i + 2, :], ps[:, 4 + 2 * i:6 + 2 * i, T:2 * T],
                                            tl[:, i, :, :], ALU.add).then_inc(sem["k_stored"], 1)
                dve.wait_ge(sem["qv_stored"], base(ph, "qv_stored") + 2)
                heads = qtok.rearrange("p t (h c) -> p t h c", h=C_HEADS)
                b = base(ph, "rope_done")
                for tt in range(TT):
                    c, sn = spread(cos[:, tt, :], 1, C_HEADS), spread(sin[:, tt, :], 1, C_HEADS)
                    tmp = [pr[:, i // 2, i % 2, 0:128].rearrange("p (h f) -> p h f", f=32) if tt == 0 else
                           s[:, i // 2, i % 2, 0:128].rearrange("p (h f) -> p h f", f=32) for i in range(4)]
                    rotate(heads[:, tt, :, C_NOPE:C_NOPE + 32], heads[:, tt, :, C_NOPE + 32:C_NOPE + 64], c, sn,
                           C_HEADS, tmp, (sem["rope_done"], b + 2 * tt))
                for n in range(8):
                    dve.wait_ge(sem["tposed"], base(ph, "tposed") + n + 1)
                    if n < 4:
                        nc.vector.tensor_copy(qm[:, n, :], ps[:, n, 0:T])
                    else:
                        nc.vector.tensor_copy(qpe[0:C_ROPE, n - 4, :], ps[0:C_ROPE, n, 0:T])

            def gates_(ph):
                with dve.Fori(0, 2) as grp:
                    for n in range(3):
                        c = ph.step + 3 * n
                        twice = 6 * grp + 2 * n
                        low = 12 * grp + (base(ph, "low_copied") + 4 * n)
                        dve.wait_ge(sem["gate_ready"], twice + base(ph, "gate_ready"))
                        for half in range(2):
                            split(c + 2 + half, grp, 9)
                            dve.wait_ge(sem["low_copied"], low + (half + 1))
                            nc.vector.tensor_tensor(logits[:, half, :, :], ps[:, 2 * half:2 * half + 2, T:2 * T],
                                                    low_half[:, half, :, :], ALU.add).then_inc(sem["logits_summed"], 1)
                        split(c + 4, grp, 9)
                        for half in range(2):
                            dve.wait_ge(sem["low_copied"], low + (half + 3))
                            nc.vector.tensor_tensor(part_sum[:, half, :, :], ps[:, 4 + 2 * half:6 + 2 * half, T:2 * T],
                                                    low_half[:, half, :, :], ALU.add).then_inc(sem["parts_summed"], 1)
                        for half in range(2):
                            dve.wait_ge(sem["gate_ready"], twice + (base(ph, "gate_ready") + half + 1))
                            dve.wait_ge(sem["parts_summed"], twice + (base(ph, "parts_summed") + half + 1))
                            dst = merged if n == 0 else part_sum
                            nc.vector.tensor_tensor(dst[:, half, :, :], part_sum[:, half, :, :], gate[:, half, :, :],
                                                    ALU.mult).then_inc(sem["gated"], 1)
                        for half in range(2):
                            if n == 0:
                                continue
                            dve.wait_ge(sem["gated"], twice + (base(ph, "gated") + half + 1))
                            if n == 2:
                                dve.wait_ge(sem["merged_ready"], 4 * grp + (base(ph, "merged_ready") + half + 1))
                            nc.vector.tensor_tensor(merged[:, half, :, :], merged[:, half, :, :],
                                                    part_sum[:, half, :, :], ALU.add).then_inc(sem["merged_ready"], 1)
                    dve.wait_ge(sem["hh_ready"], grp + (base(ph, "hh_ready") + 1))
                    nc.vector.tensor_tensor(yhl[:, bass.ds(4 * grp, 4), T:2 * T],
                                            merged[:, :, :, :].rearrange("p a b t -> p (a b) t"),
                                            yhl[:, bass.ds(4 * grp, 4), 0:T].bitcast(F32), ALU.subtract)

            def wout(ph):
                for i in range(3):
                    ahead(ph, i)

            def compress(ph):
                for w in range(2):
                    pos = prm[:, PRM["pos"] + w * LP:PRM["pos"] + (w + 1) * LP]
                    wait(dve, sem["blk_made"], base(ph, "blk_made") + w)
                    for g in range(KVG):
                        src = cmp_src[:, w, g, :]
                        blocks = bass.AP(src.tensor, src.offset, [list(src.ap[0]), [2, LP], [CMP_STRIDE, NCMP]])
                        e = nc.vector.tensor_tensor(cblk[:, :, g, :], blocks, spread(pos, 2, NCMP), ALU.add)
                    e.then_inc(sem["blk_added"], 1)
                    dve.wait_ge(sem["blk_added"], base(ph, "blk_added") + w + 1)
                    flat = cblk[:, :, :, :].rearrange("p l g n -> p l (g n)")
                    nc.vector.tensor_copy(blk[:, w, :, 0:NBLK], flat).then_inc(sem["blk_hi"], 1)
                    dve.wait_ge(sem["blk_hi"], base(ph, "blk_hi") + w + 1)
                    nc.vector.tensor_tensor(blk[:, w, :, NBLK:2 * NBLK], flat, blk[:, w, :, 0:NBLK].bitcast(F32),
                                            ALU.subtract).then_inc(sem["blk_made"], 1)
                nc.vector.memset(vblk[:, :, :], 0.0)
                for w in range(2):
                    ahead(ph, 2 * w)
                    ahead(ph, 2 * w + 1)
                    dve.wait_ge(sem["low_copied"], base(ph, "low_copied") + w + 1)
                    nc.vector.tensor_tensor(cpre[:, w, :, :], ps[:, 2 * w:2 * w + 2, NBLK:2 * NBLK],
                                            tl[:, w, :, 0:NBLK], ALU.add).then_inc(sem["group_free"], 1)
                dve.wait_ge(sem["cmp_ready"], base(ph, "cmp_ready") + 1)
                for at in (0, DH):
                    nc.vector.tensor_copy(kcb[at:at + DH, :], ps[0:DH, 4, 0:NBLK])
                for n in range(4):
                    nc.vector.tensor_copy(vblk[32 * n:32 * n + NCMP, :, n * DH:(n + 1) * DH],
                                          ps[0:NCMP, 5, 0:KVG * DH].rearrange("p (g d) -> p g d", g=KVG))

            def cmp_attend(ph):
                b = base(ph, "cmp_step")
                n = [0]

                def then(e):
                    n[0] += 1
                    e.then_inc(sem["cmp_step"], 1)
                    dve.wait_ge(sem["cmp_step"], b + n[0])

                neg = cst[:, CST["cmpneg"]:CST["cmpneg"] + TT * NCMP].rearrange("p (t n) -> p t n", t=TT)
                ok = cst[:, CST["cmpok"]:CST["cmpok"] + TT * NCMP].rearrange("p (t n) -> p t n", t=TT)
                rows = scmp[:, :, :, :].rearrange("p t h n -> p (t h) n")
                cmax, csum = small[:, 64:96], small[:, 96:128]
                then(nc.vector.memset(pcmp[:, :, :, :], 0.0))
                dve.wait_ge(sem["scores_ready"], base(ph, "scores_ready") + 1)
                then(nc.vector.tensor_scalar(scmp[:, :, :, :].rearrange("p t h n -> p (t h n)"),
                                             ps[:, 0, 0:TT * HEADS * NCMP], DH ** -0.5, None, ALU.mult))
                then(nc.vector.tensor_tensor(scmp[:, :, :, :], scmp[:, :, :, :], spread(neg, 2, HEADS), ALU.add))
                then(nc.vector.tensor_reduce(cmax, rows, AX.X, ALU.max))
                nc.vector.tensor_tensor(rows, rows, spread(cmax, 2, NCMP), ALU.subtract).then_inc(sem["max_ready"], 1)
                dve.wait_ge(sem["probs_ready"], base(ph, "probs_ready") + 1)
                then(nc.vector.tensor_tensor(scmp[:, :, :, :], scmp[:, :, :, :], spread(ok, 2, HEADS), ALU.mult))
                then(nc.vector.tensor_reduce(csum, rows, AX.X, ALU.add))
                then(nc.vector.tensor_scalar(csum, csum, TINY, None, ALU.max))
                then(nc.vector.reciprocal(csum, csum))
                g = gates[:, :, :].rearrange("p t (h b) -> p t h b", b=3)[:, :, :, 0]
                sums3 = csum.rearrange("p (t h) -> p t h", t=TT)
                then(nc.vector.tensor_tensor(sums3, sums3, g, ALU.mult))
                then(nc.vector.tensor_tensor(pcmp[:, :, :, 0:NCMP].rearrange("p t h n -> p (t h) n"), rows,
                                             spread(csum, 2, NCMP), ALU.mult))
                dve.wait_ge(sem["pv_ready"], base(ph, "pv_ready") + 1)
                for tt in range(TT):
                    nc.vector.tensor_copy(o[:, tt, :].rearrange("p (a b) -> p a b", a=2),
                                          ps[:, 4 + 2 * tt:6 + 2 * tt, :])

            run(dve, "dve", dict(setup=setup, between=between, ffn=ffn, project=project, attend=attend, turn=turn, mla_latent=mla_latent, mla_up=mla_up,
                                 gates=gates_, wout=wout, compress=compress, cmp_attend=cmp_attend))

        @block.tensor
        def _(pe):
            def step_parts(c, kk, cols):
                w = [part[:, c % RING, 0:kk * cols].rearrange("p (k n) -> p k n", k=kk) for part in (whi, wlo)]
                return w

            def use(c, i=None, stride=0):
                pe.wait_ge(sem["lo_ready"], at_step(c + 1, i, stride))

            def feature_tile(bank, w, col0, src, k0=0, first=True, last=True):
                hi, lo = w
                n = hi.shape[1]
                half = src.shape[2] // 2
                for k in range(n):
                    wide = lambda: pe.matmul(ps[:, bank, 0:2 * half], hi[:, k, col0:col0 + P], src[:, k0 + k, :],
                                             start=first and k == 0, stop=last and k == n - 1)
                    if k == 0:
                        wide()
                    e = pe.matmul(ps[:, bank, 0:half], lo[:, k, col0:col0 + P], src[:, k0 + k, 0:half],
                                  start=False, stop=False)
                    if k > 0:
                        e = wide()
                return e

            def token_tile(bank, w, cols, src, tt, k0=0, first=True, last=True):
                n = w[0].shape[1]
                for k in range(n):
                    hi, lo = cols(w[0], k), cols(w[1], k)
                    xh = src[:, k0 + k, tt * P:(tt + 1) * P]
                    xl = src[:, k0 + k, T + tt * P:T + (tt + 1) * P]
                    width = hi.free_size()
                    dst = ps[:, bank, 0:width]
                    if len(hi.shape) == 3:
                        dst = dst.rearrange("p (a b) -> p a b", a=hi.shape[1])
                    pe.matmul(dst, xh, hi, start=first and k == 0, stop=False)
                    pe.matmul(dst, xh, lo, start=False, stop=False)
                    e = pe.matmul(dst, xl, hi, start=False, stop=last and k == n - 1)
                return e

            def setup(ph):
                pe.wait_ge(sem["loaded"], N_LOADED)
                table = prm[0:BUCKETS + 1, PRM["table"]:PRM["table"] + HEADS]
                for w in range(2):
                    hot = cst[0:BUCKETS + 1, CST["onehot"] + w * VEC:CST["onehot"] + (w + 1) * VEC]
                    pe.matmul(ps[0:HEADS, w, :], table, hot, start=True, stop=True).then_inc(sem["vec_made"], 1)

            def between(ph):
                for n in range(4):
                    tt, k0 = n // 2, 4 * (n % 2)
                    if k0 == 0:
                        pe.wait_ge(sem["xn_ready"], base(ph, "xn_ready") + tt + 1)
                    for k in range(4):
                        e = pe.transpose(ps[:, n, k * P:(k + 1) * P], o[:, tt, (k0 + k) * P:(k0 + k + 1) * P], ident)
                    e.then_inc(sem["tposed"], 1)

            def ffn(ph):
                def up(c, bank, j=None):
                    use(c, j, 3)
                    w = step_parts(c, KD, 2 * P)
                    feature_tile(bank, w, 0, xhl)
                    feature_tile(bank + 1, w, P, xhl).then_inc(sem["step_used"], 1)

                def down(c, pair, j=None, first=False, last=False):
                    pe.wait_ge(sem["ht_ready"], pair + (base(ph, "ht_ready") + 1))
                    use(c, j, 3)
                    w = step_parts(c, 2, D)
                    order = [(kk, tt) for tt in range(TT) for kk in range(2)] if last else \
                        [(kk, tt) for kk in range(2) for tt in range(TT)]
                    for kk, tt in order:
                        hh, hl = (ht[:, 1 if last else 0, kk, part, tt * P:(tt + 1) * P] for part in (0, 1))
                        for half in range(2):
                            cols = slice(512 * half, 512 * half + 512)
                            dst = acc[:, 2 * tt + half, :]
                            pe.matmul(dst, hh, w[0][:, kk, cols], start=first and kk == 0, stop=False)
                            pe.matmul(dst, hh, w[1][:, kk, cols], start=False, stop=False)
                            e = pe.matmul(dst, hl, w[0][:, kk, cols], start=False, stop=last and kk == 1)
                        if last and (kk, tt) == (1, 0):
                            e.then_inc(sem["acc_half"], 1)
                    e.then_inc(sem["step_used"], 1)

                def body(j, c, i=None, first=False):
                    pe.wait_ge(sem["a_summed"], j + base(ph, "a_summed"))
                    up(c, 0, i)
                    down(c + 1, j - 1, i, first=first)
                    pe.wait_ge(sem["g_summed"], j + base(ph, "g_summed"))
                    up(c + 2, 2, i)

                up(ph.step, 0)
                up(ph.step + 1, 2)
                body(1, ph.step + 2, first=True)
                with pe.Fori(2, PAIRS - 1) as j:
                    body(j, ph.step - 1, j)
                last, end = PAIRS - 1, ph.step + 3 * PAIRS
                pe.wait_ge(sem["a_summed"], last + base(ph, "a_summed"))
                up(end - 4, 0)
                pe.wait_ge(sem["g_summed"], last + base(ph, "g_summed"))
                up(end - 3, 2)
                down(end - 2, last - 1)
                down(end - 1, last, last=True)

            def project(ph):
                emptied = []
                for g, step, bank, n in numbered(ph):
                    if len(emptied) >= 2:
                        name, count = emptied[-2]
                        pe.wait_ge(sem[name], base(ph, name) + count)
                    if g.number is not None:
                        emptied.append(("group_free", n + 1))
                        use(step)
                        w = step_parts(step, KD, 2 * P)
                        e = feature_tile(bank, w, 0, xhl)
                        if g.dest == "kv":
                            for tt in range(TT):
                                e = token_tile(4 + tt, w, lambda u, k: u[:, k, :], xhl, tt)
                        else:
                            e = feature_tile(bank + 1, w, P, xhl)
                        e.then_inc(sem["step_used"], 1)
                        continue
                    emptied.append(("stored_tokens", n + 1))
                    for i in range(g.steps):
                        use(step + i)
                        w = step_parts(step + i, g.kk, g.cols)
                        for tt in range(TT):
                            e = token_tile(bank + tt, w, lambda u, k: u[:, k, :], xhl, tt, k0=i * g.kk,
                                           first=i == 0, last=i == g.steps - 1)
                        e.then_inc(sem["step_used"], 1)

            def attend(ph):
                job, blocks = job_of(ph), blocks_of(ph)
                B = {n: base(ph, n) for n in ("q_staged", "biased", "probs_ready", "pt_ready", "o_done")}

                def scores(t, parity):
                    pe.wait_ge(sem["q_staged"], t + (B["q_staged"] + 1))
                    if not isinstance(t, int) or t >= 2:
                        pe.wait_ge(sem["biased"], t + (B["biased"] - 1))
                    for qt in range(TT):
                        dst = ps[:, parity, qt * T:(qt + 1) * T]
                        q = job.staged[:, parity, qt * P:(qt + 1) * P]
                        if not job.rotary:
                            pe.matmul(dst, q, job.k[:, job.key(t), 0, :], start=True, stop=False)
                            e = pe.matmul(dst, q, job.k[:, job.key(t), 1, :], start=False, stop=True)
                        else:
                            pe.matmul(dst, q, job.k[:, job.key(t), :], start=True, stop=False)
                            e = pe.matmul(dst, qps[0:C_ROPE, parity, qt * P:(qt + 1) * P], kpe[0:C_ROPE, :],
                                          start=False, stop=True)
                    e.then_inc(sem["scores_ready"], 1)

                def iteration(t, parity, pair, stages):
                    if 0 in stages and (not isinstance(t, int) or t + 1 < ph.n):
                        scores(t + 1, 1 - parity)
                    if 1 in stages:
                        pe.wait_ge(sem["probs_ready"], t + B["probs_ready"])
                        if not isinstance(t, int) or t >= 3:
                            pe.wait_ge(sem["pt_ready"], t + (B["pt_ready"] - 2))
                        for n, (kt, qt) in enumerate(blocks):
                            e = pe.transpose(ps[:, 3 - parity, n * P:(n + 1) * P],
                                             pr[:, 1 - parity, qt, kt * P:(kt + 1) * P], ident)
                        e.then_inc(sem["transposed"], 1)
                    if 2 in stages:
                        pe.wait_ge(sem["pt_ready"], t + (B["pt_ready"] - 1))
                        if not isinstance(t, int) or t >= 4:
                            pe.wait_ge(sem["o_done"], t + (B["o_done"] - 3))
                        for qt in range(TT):
                            mine = [(n, kt) for n, (kt, q) in enumerate(blocks) if q == qt]
                            for n, kt in mine:
                                e = pe.matmul(ps[:, 4 + parity, qt * P:qt * P + job.dv],
                                              ptf[:, parity, n * P:(n + 1) * P],
                                              v[:, kt, bass.ds(job.vcol(t - 2), job.dv)], start=kt == 0,
                                              stop=kt == mine[-1][1])
                        e.then_inc(sem["pv_ready"], 1)

                scores(0, 0)
                pipelined(pe, ph.n, iteration)

            def turn(ph):
                if ph.subln is not None:
                    pe.wait_ge(sem["head_norm"], base(ph, "head_norm") + 6)
                for k in range(ph.n):
                    for tt in range(TT):
                        e = pe.transpose(ps[:, k, tt * P:(tt + 1) * P], o[:, tt, k * P:(k + 1) * P], ident)
                    e.then_inc(sem["tposed"], 1)

            def mla_latent(ph):
                b = base(ph, "xn_ready")
                for k in range(6):
                    pe.wait_ge(sem["xn_ready"], b + 6)
                    rows = P if k < 5 else C_ROPE
                    for tt in range(TT):
                        e = pe.transpose(ps[0:rows, k, tt * P:(tt + 1) * P], latent[:, tt, k * P:k * P + rows], ident)
                    e.then_inc(sem["tposed"], 1)

            def mla_up(ph):
                for i in range(2):
                    use(ph.step + i)
                    w = step_parts(ph.step + i, 3, C_QR)
                    for tt in range(TT):
                        e = token_tile(2 * i + tt, w, lambda u, k: u[:, k, :], chl, tt)
                    e.then_inc(sem["step_used"], 1)
                use(ph.step + 2)
                w = step_parts(ph.step + 2, 2, D)
                for h_ in range(C_HEADS):
                    e = feature_tile(4 + h_, w, 2 * P * h_, chl, k0=3)
                    if h_ % 2:
                        e.then_inc(sem["group_ready"], 1)
                pe.wait_ge(sem["qv_stored"], base(ph, "qv_stored") + 1)
                for tt in range(TT):
                    e = token_tile(tt, w, lambda u, k: u[:, k, :].rearrange("p (h c) -> p h c", h=C_HEADS)[:, :, P:2 * P],
                                   chl, tt, k0=3)
                e.then_inc(sem["step_used"], 1)
                pe.wait_ge(sem["qv_stored"], base(ph, "qv_stored") + 3)
                pe.wait_ge(sem["k_stored"], base(ph, "k_stored") + 2)
                pe.wait_ge(sem["rope_done"], base(ph, "rope_done") + 4)
                heads = qtok.rearrange("p t (h c) -> p t h c", h=C_HEADS)
                for n in range(8):
                    h_, rows, at = n % 4, (P if n < 4 else C_ROPE), (0 if n < 4 else C_NOPE)
                    for tt in range(TT):
                        e = pe.transpose(ps[0:rows, n, tt * P:(tt + 1) * P], heads[:, tt, h_, at:at + rows], ident)
                    e.then_inc(sem["tposed"], 1)

            def gates_(ph):
                with pe.Fori(0, 2) as grp:
                    for n in range(3):
                        c = ph.step + 3 * n
                        twice = 6 * grp + 2 * n
                        pe.wait_ge(sem["logits_summed"], twice + base(ph, "logits_summed"))
                        for half in range(2):
                            use(c + half, grp, 9)
                            w = step_parts(c + half, KD, 2 * P)
                            feature_tile(2 * half, w, 0, xhl)
                            feature_tile(2 * half + 1, w, P, xhl).then_inc(sem["step_used"], 1)
                        pe.wait_ge(sem["parts_summed"], twice + base(ph, "parts_summed"))
                        use(c + 2, grp, 9)
                        w = step_parts(c + 2, 4, 4 * P)
                        for i in range(4):
                            e = feature_tile(4 + i, w, i * P, br1, k0=4 * n)
                        e.then_inc(sem["step_used"], 1)

            def wout(ph):
                src = yhl if ph.src == "y" else br2
                for i in range(4):
                    use(ph.step + i)
                    w = step_parts(ph.step + i, 2, D)
                    for tt in range(TT):
                        for half in range(2):
                            e = token_tile(4 + 2 * tt + half, w,
                                           lambda u, k: u[:, k, 512 * half:512 * half + 512], src, tt, k0=2 * i,
                                           first=i == 0, last=i == 3)
                            if i == 3 and (tt, half) == (0, 1):
                                e.then_inc(sem["acc_half"], 1)
                    e.then_inc(sem["step_used"], 1)

            def compress(ph):
                for w_ in range(2):
                    pe.wait_ge(sem["blk_made"], base(ph, "blk_made") + w_ + 1)
                    for i in range(2):
                        c = ph.step + 2 * w_ + i
                        use(c)
                        w = step_parts(c, KD, CMP_HID)
                        for tile in range(2):
                            e = feature_tile(2 * w_ + tile, w, tile * P, blk[:, w_, :, :], k0=KD * i, first=i == 0,
                                             last=i == 1)
                        e.then_inc(sem["step_used"], 1)
                cw2 = prm[:, PRM["cw2"]:PRM["cw2"] + 4 * DH].rearrange("p (w k d) -> p w k d", w=2, k=2)
                pe.wait_ge(sem["gelu_done"], base(ph, "gelu_done") + 2)
                for k in range(2):
                    pe.matmul(ps[0:DH, 4, 0:NBLK], cw2[:, 0, k, :], chid[:, 0, k, :], start=k == 0, stop=k == 1)
                for g in range(KVG):
                    for k in range(2):
                        e = pe.matmul(ps[0:NCMP, 5, g * DH:(g + 1) * DH], chid[:, 1, k, g * NCMP:(g + 1) * NCMP],
                                      cw2[:, 1, k, :], start=k == 0, stop=k == 1)
                e.then_inc(sem["cmp_ready"], 1)

            def cmp_attend(ph):
                for qt in range(TT):
                    for h_ in range(HEADS):
                        g = h_ // (HEADS // KVG)
                        at = (qt * HEADS + h_) * NCMP
                        e = pe.matmul(ps[:, 0, at:at + NCMP], q2[:, h_, qt * P:(qt + 1) * P].bitcast(F32),
                                      kcb[:, g * NCMP:(g + 1) * NCMP], start=True, stop=True)
                e.then_inc(sem["scores_ready"], 1)
                pe.wait_ge(sem["cmp_step"], base(ph, "cmp_step") + 10)
                for qt in range(TT):
                    for g in range(KVG):
                        tile = pcmp[:, qt, 4 * g:4 * g + 4, :].rearrange("p h n -> p (h n)")
                        e = pe.transpose(ps[:, 2 + qt, g * P:(g + 1) * P], tile, ident)
                e.then_inc(sem["transposed"], 1)
                pe.wait_ge(sem["pt_ready"], base(ph, "pt_ready") + 1)
                for qt in range(TT):
                    for g in range(KVG):
                        e = pe.matmul(ps[:, 4 + 2 * qt + g // 2, (g % 2) * T:(g % 2) * T + T],
                                      ptf[:, qt, g * P:(g + 1) * P], vblk[:, g, :], start=True, stop=True)
                e.then_inc(sem["pv_ready"], 1)

            run(pe, "pe", dict(setup=setup, between=between, ffn=ffn, project=project, attend=attend,
                               turn=turn, mla_latent=mla_latent, mla_up=mla_up, gates=gates_, wout=wout,
                               compress=compress, cmp_attend=cmp_attend))


def stream_of(a, n_steps):
    w = np.zeros((n_steps, P, STEP), np.float32)
    at = [0]

    def put(block):
        k = block.shape[0] // P
        w[at[0], :, :k * block.shape[1]] = block.reshape(k, P, -1).transpose(1, 0, 2).reshape(P, -1)
        at[0] += 1

    def ffn(w13, w2):
        up = lambda j, g: w13[:, g * DFF + 2 * P * j:g * DFF + 2 * P * (j + 1)]
        down = lambda j: w2[2 * P * j:2 * P * (j + 1)]
        put(up(0, 0))
        put(up(0, 1))
        for j in range(1, PAIRS - 1):
            put(up(j, 0))
            put(down(j - 1))
            put(up(j, 1))
        put(up(PAIRS - 1, 0))
        put(up(PAIRS - 1, 1))
        put(down(PAIRS - 2))
        put(down(PAIRS - 1))

    def columns(m, c0, n, width=2 * P, kk=None):
        for c in range(n):
            part = m[:, c0 + c * width:c0 + (c + 1) * width]
            rows = m.shape[0] if kk is None else kk * P
            for r in range(0, m.shape[0], rows):
                put(part[r:r + rows])

    def rows(m):
        for r in range(0, D, 2 * P):
            put(m[r:r + 2 * P])

    for l in range(DEPTH1):
        ffn(a["ffn1_w13"][l], a["ffn1_w2"][l])
        m = a["w_in"][l]
        columns(m, 0, 4)
        columns(m, 1024, 1, 512, 4)
        columns(m, 1536, 3)
        columns(m, 2304, 2, C_COLS // 2, 4)
        columns(a["c_w_uq"][l].reshape(C_QR, -1), 0, 2, C_QR)
        put(a["c_w_ukv"][l].reshape(C_KVR, -1))
        for grp in range(2):
            for n in range(3):
                columns(a["w_gate"][l], n * D + 4 * P * grp, 2)
                put(a["w_branch"][l, n][:, 4 * P * grp:4 * P * (grp + 1)])
        rows(a["w_out"][l])
        ffn(a["ffn2_w13"][l], a["ffn2_w2"][l])
    for i in range(DEPTH2):
        ffn(a["ffn_w_in_2"][i, 0], a["ffn_w_out_2"][i, 0])
        j = i // 3
        if i % 3 == 0:
            columns(a["a_w_in_2"][j], 0, 5)
            rows(a["a_w_out_2"][j])
        elif i % 3 == 1:
            m = a["b_w_in_2"][j]
            columns(m, 0, 6)
            for t in range(2):
                for r in range(2):
                    put(a["b_cmp_w1_2"][j, t][r * D:(r + 1) * D])
            columns(m, 1536, 4)
            put(m[:, 2560:2608])
            rows(a["b_w_out_2"][j])
        else:
            m = a["c_w_in_2"][j]
            columns(m, 0, 8)
            columns(m, 2048, 2, 512, 4)
            rows(a["c_w_out_2"][j])
        ffn(a["ffn_w_in_2"][i, 1], a["ffn_w_out_2"][i, 1])
    return w, at[0]


def params_of(a):
    p = np.zeros((P, PRM_COLS), np.float32)

    def put(name, block):
        p[:block.shape[0], PRM[name]:PRM[name] + block.shape[1]] = block

    by_tile = lambda vector: vector.reshape(-1, P).T
    put("subln", a["a_subln"].T)
    put("cqn", by_tile(a["c_q_norm"].reshape(-1)))
    put("ckvn", by_tile(a["c_kv_norm"].reshape(-1)))
    put("bgate", by_tile(a["b_gate"].reshape(-1)))
    put("sink1", np.broadcast_to(a["b_sinks"].reshape(1, -1), (P, DEPTH1 * B_HEADS)))
    put("sink2", np.broadcast_to(a["a_sinks_2"].reshape(1, -1), (P, 2 * HEADS)))
    put("lam", np.broadcast_to(a["a_lambda"].reshape(1, -1), (P, DEPTH1 * 4 * DH)))
    put("pos", a["b_cmp_pos_2"][0].reshape(2, LP, P).transpose(2, 0, 1).reshape(P, -1))
    put("cw2", a["b_cmp_w2_2"][0].reshape(2, 2, P, DH).transpose(2, 0, 1, 3).reshape(P, -1))
    put("table", np.concatenate([a["rel_bias_2"], np.full((1, HEADS), NEG, np.float32)], 0))
    return p


def gains_of(a):
    def row(name):
        if name is None:
            return np.zeros(D, np.float32)
        if name[0] == "final":
            return a["final_norm"].reshape(D)
        return a["norm_g_2"][name[1], name[2]] if name[0] == "n2" else a[name[0] + "_norm"][name[1]]

    return np.stack([np.stack([row(post), row(pre)]) for post, pre in plan()[3]])


def constants():
    c = np.zeros((P, CST_COLS), np.float32)

    def put(name, block):
        c[:block.shape[0], CST[name]:CST[name] + block.shape[1]] = block

    put("ident", np.eye(P, dtype=np.float32))
    freq = (10000.0 ** (-np.arange(0, C_ROPE, 2, dtype=np.float32) / C_ROPE)).astype(np.float32)
    ang = np.arange(T, dtype=np.float32)[:, None] * freq[None, :]
    by_token = lambda m: m.reshape(TT, P, -1).transpose(1, 0, 2).reshape(P, -1)
    put("cos", by_token(np.cos(ang)))
    put("sin", by_token(np.sin(ang)))
    ok = (np.arange(NCMP)[None, :] * CMP_STRIDE + CMP_LEN - 1 <= np.arange(T)[:, None]).astype(np.float32)
    put("cmpok", by_token(ok))
    put("cmpneg", by_token((1 - ok) * np.float32(NEG)))
    d = T - 1 - np.arange(VEC)
    exact = BUCKETS // 2
    safe = np.maximum(d, 1).astype(np.float32)
    log_b = exact + (np.log(safe / exact) / np.float32(np.log(BUCKET_MAX / exact)) * (BUCKETS - exact)).astype(np.int32)
    bucket = np.where(d < exact, np.maximum(d, 0), np.minimum(log_b, BUCKETS - 1))
    hot = np.zeros((2, BUCKETS + 1, VEC), np.float32)
    for w, reach in enumerate((T, P)):
        row = np.where((d >= 0) & (d < reach), bucket, BUCKETS)
        hot[w, row, np.arange(VEC)] = 1.0
    put("onehot", hot.transpose(1, 0, 2).reshape(BUCKETS + 1, -1))
    q, k = np.arange(T)[:, None], np.arange(T)[None, :]
    dist = np.abs(q - k).astype(np.float32)
    slope = lambda n: 2.0 ** (-8.0 * np.arange(1, n + 1, dtype=np.float32) / n)
    fixed = np.zeros((NBIAS1, T, T), np.float32)
    fixed[:A_HEADS] = -slope(A_HEADS)[:, None, None] * dist
    fixed[A_HEADS:A_HEADS + B_HEADS] = np.where(dist <= 128, -slope(B_HEADS)[:, None, None] * dist, np.float32(NEG))
    return c, np.ascontiguousarray(fixed.reshape(NBIAS1, TT, P, T).transpose(0, 2, 1, 3))


def kernel(**inputs):
    import concourse.bacc as bacc
    from concourse.bass_utils import run_bass_kernel_spmd

    a = {name: np.asarray(value) for name, value in inputs.items()}
    steps = plan()[2] + 2
    steps += -steps % RING
    stream, used = stream_of(a, steps)
    cst, fixed = constants()
    arrays = {
        "stream": stream,
        "params": params_of(a),
        "constants": cst,
        "fixed_bias": fixed,
        "gains": gains_of(a),
        "x_tokens": np.ascontiguousarray(a["x"].reshape(TT, P, D).transpose(1, 0, 2)),
    }
    nc = bacc.Bacc("TRN2", target_bir_lowering=False, num_devices=1)
    args = [nc.dram_tensor(n, v.shape, F32, kind="ExternalInput").ap() for n, v in arrays.items()]
    out = nc.dram_tensor("y_tokens", (P, TT, D), F32, kind="ExternalOutput").ap()
    transformer_stacks(nc, *args, out)
    result = run_bass_kernel_spmd(nc, [arrays], core_ids=[0]).results[0]["y_tokens"]
    return np.asarray(result).transpose(1, 0, 2).reshape(1, T, D)
```
